# Optimizing a Trainium2 kernel written in Bass

```python
import math
import jax, jax.numpy as jnp
from jax import lax
import numpy as np

D_MODEL = 1024
BATCH = 1
SEQ = 256
DEPTH = 2

N_A_LAYERS = DEPTH // 2
N_B_LAYERS = DEPTH - N_A_LAYERS
LRU_WIDTH = 1280
LRU_BLOCK = 256
LRU_HEADS = LRU_WIDTH // LRU_BLOCK
CONV_WIDTH = 4
LRU_C = 8.0
N_HEADS = 8
N_KV_HEADS = 4
HEAD_DIM = 128
KV_GROUP = N_HEADS // N_KV_HEADS
MOBA_BLOCK = 256
MOBA_TOPK = 3
Q_CHUNK = 16
REL_BUCKETS = 32
REL_MAX_DIST = 128
D_FF = -(-8 * D_MODEL // (3 * 256)) * 256
RMS_EPS = 1e-6
NEG_INF = -1e30


def rmsnorm(x, g):
    xf = x.astype(jnp.float32)
    y = xf * lax.rsqrt(jnp.mean(xf * xf, axis=-1, keepdims=True) + RMS_EPS)
    return (y * g.astype(jnp.float32)).astype(x.dtype)

def modulate(h, shift, scale):
    return h * (1 + scale[:, None, :]) + shift[:, None, :]

def swiglu(h, w_gate, w_up, w_down):
    return (jax.nn.silu(h @ w_gate) * (h @ w_up)) @ w_down

def _lru_combine(left, right):
    a_l, b_l = left
    a_r, b_r = right
    return a_l * a_r, a_r * b_l + b_r

def rglru_mixer(h, w_in, conv_w, conv_b, w_gates, b_gates, lru_lambda, w_out):
    B, S, _ = h.shape
    u = h @ w_in
    y_br = jax.nn.gelu(u[..., :LRU_WIDTH])
    x_br = u[..., LRU_WIDTH:]
    xp = jnp.pad(x_br, ((0, 0), (CONV_WIDTH - 1, 0), (0, 0)))
    xc = sum(xp[:, k:k + S, :] * conv_w[k] for k in range(CONV_WIDTH)) + conv_b
    xb = xc.reshape(B, S, LRU_HEADS, LRU_BLOCK)
    g = jnp.einsum('bshi,hio->bsho', xb, w_gates)
    gr = g[..., :LRU_BLOCK].reshape(B, S, LRU_WIDTH) + b_gates[0]
    gi = g[..., LRU_BLOCK:].reshape(B, S, LRU_WIDTH) + b_gates[1]
    r = jax.nn.sigmoid(gr.astype(jnp.float32))
    i = jax.nn.sigmoid(gi.astype(jnp.float32))
    log_a = -LRU_C * r * jax.nn.softplus(-lru_lambda.astype(jnp.float32))
    a = jnp.exp(log_a)
    mult = jnp.sqrt(-jnp.expm1(2.0 * log_a))
    b = mult * (i * xc.astype(jnp.float32))
    _, hs = lax.associative_scan(_lru_combine, (a, b), axis=1)
    return (hs.astype(h.dtype) * y_br) @ w_out

def shared_kv(x, shift, scale, g, w_kv):
    B, S, _ = x.shape
    h = modulate(rmsnorm(x, g), shift, scale)
    kv = h @ w_kv
    nb = -(-S // MOBA_BLOCK)
    pad = nb * MOBA_BLOCK - S
    def blk(t):
        t = t.reshape(B, S, N_KV_HEADS, HEAD_DIM).transpose(0, 2, 1, 3)
        t = jnp.pad(t, ((0, 0), (0, 0), (0, pad), (0, 0)))
        return t.reshape(B, N_KV_HEADS, nb, MOBA_BLOCK, HEAD_DIM)
    k_blocks = blk(kv[..., :N_KV_HEADS * HEAD_DIM])
    v_blocks = blk(kv[..., N_KV_HEADS * HEAD_DIM:])
    k_mean = jnp.mean(k_blocks.astype(jnp.float32), axis=3)
    return k_blocks, v_blocks, k_mean

def t5_bucket(dist):
    dist = jnp.maximum(dist, 0)
    max_exact = REL_BUCKETS // 2
    d = jnp.maximum(dist, 1).astype(jnp.float32)
    large = max_exact + (jnp.log(d / max_exact) / math.log(REL_MAX_DIST / max_exact)
                         * (REL_BUCKETS - max_exact)).astype(jnp.int32)
    large = jnp.minimum(large, REL_BUCKETS - 1)
    return jnp.where(dist < max_exact, dist, large)

def moba_mixer(h, w_q, w_o, k_blocks, v_blocks, k_mean, rel_bias):
    B, S, _ = h.shape
    nb = k_blocks.shape[2]
    s_pad = nb * MOBA_BLOCK
    n_sel = min(MOBA_TOPK, nb)
    scale = HEAD_DIM ** -0.5
    q = (h @ w_q).reshape(B, S, N_HEADS, HEAD_DIM).transpose(0, 2, 1, 3)
    q = jnp.pad(q, ((0, 0), (0, 0), (0, s_pad - S), (0, 0)))
    kv_head = jnp.arange(N_HEADS) // KV_GROUP
    km = k_mean[:, kv_head]
    bi = jnp.arange(B)[:, None, None, None]
    kvh = kv_head[None, :, None, None]
    hi5 = jnp.arange(N_HEADS)[None, :, None, None, None]
    bias_tab = rel_bias.astype(jnp.float32)
    blk_pos = jnp.arange(MOBA_BLOCK)

    def chunk(ci):
        t0 = ci * Q_CHUNK
        qf = lax.dynamic_slice_in_dim(q, t0, Q_CHUNK, axis=2).astype(jnp.float32)
        pos = t0 + jnp.arange(Q_CHUNK)
        own = t0 // MOBA_BLOCK
        gate = jnp.einsum('bhcd,bhnd->bhcn', qf, km)
        gate = jnp.where(jnp.arange(nb) < own, gate, NEG_INF)
        _, idx = lax.top_k(gate, n_sel)
        sel_valid = jnp.arange(n_sel) < own
        ksel = k_blocks[bi, kvh, idx].astype(jnp.float32)
        vsel = v_blocks[bi, kvh, idx].astype(jnp.float32)
        s_sel = jnp.einsum('bhcd,bhcnkd->bhcnk', qf, ksel) * scale
        kpos_sel = idx[..., None] * MOBA_BLOCK + blk_pos
        dist_sel = pos[None, None, :, None, None] - kpos_sel
        s_sel = jnp.where(sel_valid[:, None], s_sel + bias_tab[hi5, t5_bucket(dist_sel)], NEG_INF)
        k_own = lax.dynamic_index_in_dim(k_blocks, own, axis=2, keepdims=False)[:, kv_head].astype(jnp.float32)
        v_own = lax.dynamic_index_in_dim(v_blocks, own, axis=2, keepdims=False)[:, kv_head].astype(jnp.float32)
        s_own = jnp.einsum('bhcd,bhkd->bhck', qf, k_own) * scale
        dist_own = pos[:, None] - (own * MOBA_BLOCK + blk_pos)[None, :]
        s_own = jnp.where(dist_own >= 0, s_own + bias_tab[:, t5_bucket(dist_own)], NEG_INF)
        logits = jnp.concatenate([s_sel.reshape(B, N_HEADS, Q_CHUNK, n_sel * MOBA_BLOCK), s_own], axis=-1)
        p = jax.nn.softmax(logits, axis=-1)
        p_sel = p[..., :n_sel * MOBA_BLOCK].reshape(B, N_HEADS, Q_CHUNK, n_sel, MOBA_BLOCK)
        p_own = p[..., n_sel * MOBA_BLOCK:]
        o = jnp.einsum('bhcnk,bhcnkd->bhcd', p_sel, vsel) + jnp.einsum('bhck,bhkd->bhcd', p_own, v_own)
        return o.astype(h.dtype)

    o = lax.map(chunk, jnp.arange(s_pad // Q_CHUNK))
    o = o.transpose(1, 0, 3, 2, 4).reshape(B, s_pad, N_HEADS * HEAD_DIM)[:, :S]
    return o @ w_o

def first_inputs(seed: int = 0) -> dict:
    key = jax.random.key(seed)
    ks = jax.random.split(key, 32)
    nrm = lambda k, shape, s: jax.random.normal(k, shape, jnp.float32) * s
    D = D_MODEL
    u = jax.random.uniform(ks[10], (N_A_LAYERS, LRU_WIDTH), jnp.float32, 0.9, 0.999)
    a_base = u ** (1.0 / LRU_C)
    lru_lambda = jnp.log(a_base) - jnp.log1p(-a_base)
    return {
        "x": nrm(ks[0], (BATCH, SEQ, D), 1.0),
        "c": nrm(ks[1], (BATCH, D), 1.0),
        "mod_w": nrm(ks[2], (DEPTH, D, 6 * D), 0.5 * D ** -0.5),
        "mod_b": nrm(ks[3], (DEPTH, 6 * D), 0.02),
        "norm_mix": 1.0 + nrm(ks[4], (DEPTH, D), 0.02),
        "norm_ffn": 1.0 + nrm(ks[5], (DEPTH, D), 0.02),
        "lru_w_in": nrm(ks[6], (N_A_LAYERS, D, 2 * LRU_WIDTH), D ** -0.5),
        "lru_conv_w": nrm(ks[7], (N_A_LAYERS, CONV_WIDTH, LRU_WIDTH), CONV_WIDTH ** -0.5),
        "lru_conv_b": nrm(ks[8], (N_A_LAYERS, LRU_WIDTH), 0.02),
        "lru_w_gates": nrm(ks[9], (N_A_LAYERS, LRU_HEADS, LRU_BLOCK, 2 * LRU_BLOCK), LRU_BLOCK ** -0.5),
        "lru_b_gates": nrm(ks[11], (N_A_LAYERS, 2, LRU_WIDTH), 0.02),
        "lru_lambda": lru_lambda,
        "lru_w_out": nrm(ks[12], (N_A_LAYERS, LRU_WIDTH, D), LRU_WIDTH ** -0.5),
        "kv_mod_w": nrm(ks[13], (D, 2 * D), 0.5 * D ** -0.5),
        "kv_mod_b": nrm(ks[14], (2 * D,), 0.02),
        "kv_norm": 1.0 + nrm(ks[15], (D,), 0.02),
        "w_kv": nrm(ks[16], (D, 2 * N_KV_HEADS * HEAD_DIM), D ** -0.5),
        "attn_w_q": nrm(ks[17], (N_B_LAYERS, D, N_HEADS * HEAD_DIM), D ** -0.5),
        "attn_w_o": nrm(ks[18], (N_B_LAYERS, N_HEADS * HEAD_DIM, D), (N_HEADS * HEAD_DIM) ** -0.5),
        "rel_bias": nrm(ks[19], (N_HEADS, REL_BUCKETS), 0.2),
        "ffn_w_gate": nrm(ks[20], (DEPTH, D, D_FF), D ** -0.5),
        "ffn_w_up": nrm(ks[21], (DEPTH, D, D_FF), D ** -0.5),
        "ffn_w_down": nrm(ks[22], (DEPTH, D_FF, D), D_FF ** -0.5),
        "final_norm": 1.0 + nrm(ks[23], (D,), 0.02),
    }

def first_block(x, c, mod_w, mod_b, norm_mix, norm_ffn, lru_w_in, lru_conv_w, lru_conv_b,
              lru_w_gates, lru_b_gates, lru_lambda, lru_w_out, kv_mod_w, kv_mod_b, kv_norm,
              w_kv, attn_w_q, attn_w_o, rel_bias, ffn_w_gate, ffn_w_up, ffn_w_down, final_norm):
    D = D_MODEL
    cs = jax.nn.silu(c)
    kv = None
    for l in range(DEPTH):
        if l == N_A_LAYERS:
            kv_mod = cs @ kv_mod_w + kv_mod_b
            kv = shared_kv(x, kv_mod[:, :D], kv_mod[:, D:], kv_norm, w_kv)
        mod = cs @ mod_w[l] + mod_b[l]
        sh_m, sc_m, g_m = mod[:, :D], mod[:, D:2 * D], mod[:, 2 * D:3 * D]
        sh_f, sc_f, g_f = mod[:, 3 * D:4 * D], mod[:, 4 * D:5 * D], mod[:, 5 * D:]
        h = modulate(rmsnorm(x, norm_mix[l]), sh_m, sc_m)
        if l < N_A_LAYERS:
            mix = rglru_mixer(h, lru_w_in[l], lru_conv_w[l], lru_conv_b[l], lru_w_gates[l],
                              lru_b_gates[l], lru_lambda[l], lru_w_out[l])
        else:
            j = l - N_A_LAYERS
            mix = moba_mixer(h, attn_w_q[j], attn_w_o[j], kv[0], kv[1], kv[2], rel_bias)
        x = x + g_m[:, None, :] * mix
        h = modulate(rmsnorm(x, norm_ffn[l]), sh_f, sc_f)
        x = x + g_f[:, None, :] * swiglu(h, ffn_w_gate[l], ffn_w_up[l], ffn_w_down[l])
    return rmsnorm(x, final_norm)


N_META = 16
CHUNK = 128
PAD = CHUNK - N_META
EPS = 1e-6

CONV_A_WIDTH = D_MODEL
CONV_A_K = 3
SSD_HEAD_DIM = 64
SSD_HEADS = D_MODEL // SSD_HEAD_DIM
SSD_INNER = SSD_HEADS * SSD_HEAD_DIM
SSD_GROUPS = 4
SSD_STATE = 128
SSD_CONV_K = 4
SSD_CONV_DIM = SSD_INNER + 2 * SSD_GROUPS * SSD_STATE
RET_HEADS = 4
RET_QK_DIM = 256
RET_V_DIM = D_MODEL // RET_HEADS
RET_WIDTH = RET_HEADS * RET_V_DIM
ROPE_BASE = 10000.0
SB_HEADS = 8
SB_HEAD_DIM = D_MODEL // SB_HEADS
SB_WIDTH = SB_HEADS * SB_HEAD_DIM
N_BRANCH = 4
BRANCH_WIDTH = D_MODEL
D_FF_2 = ((8 * D_MODEL // 3 + 255) // 256) * 256

IN_SIZES = (
    CONV_A_WIDTH, CONV_A_WIDTH, CONV_A_WIDTH,
    SSD_INNER, SSD_CONV_DIM, SSD_HEADS,
    RET_HEADS * RET_QK_DIM, RET_HEADS * RET_QK_DIM,
    RET_WIDTH, RET_WIDTH,
    SB_WIDTH, SB_WIDTH, SB_WIDTH,
    N_BRANCH * D_MODEL,
)
IN_WIDTH = sum(IN_SIZES)
IN_SPLITS = tuple(np.cumsum(IN_SIZES)[:-1].tolist())


def rmsnorm_2(x, w):
    xf = x.astype(jnp.float32)
    y = xf * lax.rsqrt(jnp.mean(xf * xf, axis=-1, keepdims=True) + EPS)
    return (y * w.astype(jnp.float32)).astype(x.dtype)

def causal_dwconv(u, w):
    k_taps = w.shape[0]
    length = u.shape[1]
    up = jnp.pad(u, ((0, 0), (k_taps - 1, 0), (0, 0)))
    out = up[:, 0:length] * w[0]
    for i in range(1, k_taps):
        out = out + up[:, i:i + length] * w[i]
    return out

def short_conv_mixer(b_gate, c_gate, xa, conv_w, valid):
    vm = valid[None, :, None].astype(xa.dtype)
    u = c_gate * xa * vm
    return (b_gate * causal_dwconv(u, conv_w)).astype(xa.dtype)

def ssd_mixer(z, xbc, dt_raw, conv_w, conv_b, dt_bias, a_log, d_skip, norm_w, valid):
    f32 = jnp.float32
    b, L, _ = z.shape
    nc = L // CHUNK
    hpg = SSD_HEADS // SSD_GROUPS
    vm = valid[None, :, None].astype(xbc.dtype)
    xbc = jax.nn.silu(causal_dwconv(xbc * vm, conv_w) + conv_b)
    xs, bm, cm = jnp.split(xbc, (SSD_INNER, SSD_INNER + SSD_GROUPS * SSD_STATE), axis=-1)
    xs = (xs * vm).astype(f32).reshape(b, nc, CHUNK, SSD_GROUPS, hpg, SSD_HEAD_DIM)
    bc = bm.astype(f32).reshape(b, nc, CHUNK, SSD_GROUPS, SSD_STATE)
    cc = cm.astype(f32).reshape(b, nc, CHUNK, SSD_GROUPS, SSD_STATE)
    dt = jax.nn.softplus(dt_raw.astype(f32) + dt_bias.astype(f32))
    a = (-jnp.exp(a_log.astype(f32)) * dt).reshape(b, nc, CHUNK, SSD_GROUPS, hpg)
    xdt = xs * dt.reshape(b, nc, CHUNK, SSD_GROUPS, hpg)[..., None]
    acs = jnp.moveaxis(jnp.cumsum(a, axis=2), 2, -1)
    causal = jnp.tril(jnp.ones((CHUNK, CHUNK), dtype=bool))
    seg = jnp.exp(jnp.where(causal, acs[..., :, None] - acs[..., None, :], -jnp.inf))
    cb = jnp.einsum('bclgn,bcsgn->bcgls', cc, bc)
    y_diag = jnp.einsum('bcgjls,bcsgjp->bclgjp', cb[:, :, :, None] * seg, xdt)
    decay_states = jnp.exp(acs[..., -1:] - acs)
    states = jnp.einsum('bclgn,bcgjl,bclgjp->bcgjpn', bc, decay_states, xdt)
    chunk_decay = jnp.exp(acs[..., -1])

    def step(hstate, inp):
        st, dec = inp
        return hstate * dec[..., None, None] + st, hstate

    h0 = jnp.zeros((b, SSD_GROUPS, hpg, SSD_HEAD_DIM, SSD_STATE), f32)
    _, prev = lax.scan(step, h0, (jnp.moveaxis(states, 1, 0), jnp.moveaxis(chunk_decay, 1, 0)))
    prev = jnp.moveaxis(prev, 0, 1)
    y_off = jnp.einsum('bclgn,bcgjpn,bcgjl->bclgjp', cc, prev, jnp.exp(acs))
    y = y_diag + y_off + xs * d_skip.astype(f32).reshape(SSD_GROUPS, hpg)[..., None]
    y = y.reshape(b, L, SSD_INNER) * jax.nn.silu(z.astype(f32))
    yg = y.reshape(b, L, SSD_GROUPS, SSD_INNER // SSD_GROUPS)
    yg = yg * lax.rsqrt(jnp.mean(yg * yg, axis=-1, keepdims=True) + EPS)
    return (yg.reshape(b, L, SSD_INNER) * norm_w.astype(f32)).astype(z.dtype)

def rotate(x, pos):
    half = x.shape[-1] // 2
    inv = ROPE_BASE ** (-jnp.arange(half, dtype=jnp.float32) / half)
    ang = pos.astype(jnp.float32)[:, None] * inv[None, :]
    cos = jnp.cos(ang)[None, :, None, :]
    sin = jnp.sin(ang)[None, :, None, :]
    x1, x2 = x[..., :half], x[..., half:]
    return jnp.concatenate([x1 * cos - x2 * sin, x1 * sin + x2 * cos], axis=-1)

def retention_mixer(q, k, v, g, valid):
    f32 = jnp.float32
    b, L, _ = q.shape
    nc = L // CHUNK
    pos = jnp.arange(L)
    qr = rotate(q.astype(f32).reshape(b, L, RET_HEADS, RET_QK_DIM), pos)
    kr = rotate(k.astype(f32).reshape(b, L, RET_HEADS, RET_QK_DIM), pos) * (RET_QK_DIM ** -0.5)
    vr = v.astype(f32).reshape(b, L, RET_HEADS, RET_V_DIM) * valid.astype(f32)[None, :, None, None]
    log_gamma = jnp.log(1.0 - jnp.power(2.0, -5.0 - jnp.arange(RET_HEADS, dtype=f32)))
    idx = jnp.arange(CHUNK, dtype=f32)
    rel = idx[:, None] - idx[None, :]
    dmask = jnp.where(rel >= 0, jnp.exp(log_gamma[:, None, None] * jnp.maximum(rel, 0.0)), 0.0)
    qc = qr.reshape(b, nc, CHUNK, RET_HEADS, RET_QK_DIM)
    kc = kr.reshape(b, nc, CHUNK, RET_HEADS, RET_QK_DIM)
    vc = vr.reshape(b, nc, CHUNK, RET_HEADS, RET_V_DIM)
    scores = jnp.einsum('bclhd,bcshd->bchls', qc, kc) * dmask
    y_in = jnp.einsum('bchls,bcshe->bclhe', scores, vc)
    k_decay = jnp.exp(log_gamma[:, None] * (CHUNK - 1 - idx)[None, :])
    kv = jnp.einsum('bcshd,hs,bcshe->bchde', kc, k_decay, vc)
    chunk_decay = jnp.exp(log_gamma * CHUNK)

    def step(r, kv_c):
        return r * chunk_decay[:, None, None] + kv_c, r

    r0 = jnp.zeros((b, RET_HEADS, RET_QK_DIM, RET_V_DIM), f32)
    _, prev = lax.scan(step, r0, jnp.moveaxis(kv, 1, 0))
    prev = jnp.moveaxis(prev, 0, 1)
    q_decay = jnp.exp(log_gamma[None, :] * (idx + 1.0)[:, None])
    y_cr = jnp.einsum('bclhd,bchde->bclhe', qc, prev) * q_decay[:, :, None]
    y = (y_in + y_cr).reshape(b, L, RET_HEADS, RET_V_DIM)
    mu = jnp.mean(y, axis=-1, keepdims=True)
    var = jnp.mean(jnp.square(y - mu), axis=-1, keepdims=True)
    y = ((y - mu) * lax.rsqrt(var + EPS)).reshape(b, L, RET_WIDTH)
    return (y * jax.nn.silu(g.astype(f32))).astype(q.dtype)

def stick_breaking_mixer(q, k, v, valid):
    f32 = jnp.float32
    b, L, _ = q.shape
    nb = L // CHUNK
    qh = q.reshape(b, L, SB_HEADS, SB_HEAD_DIM)
    kh = k.reshape(b, L, SB_HEADS, SB_HEAD_DIM)
    vh = v.reshape(b, L, SB_HEADS, SB_HEAD_DIM)
    qb = jnp.moveaxis(qh.reshape(b, nb, CHUNK, SB_HEADS, SB_HEAD_DIM), 1, 0)
    key_pos = jnp.arange(L)
    scale = SB_HEAD_DIM ** -0.5

    def block(args):
        q_blk, i = args
        t = i * CHUNK + jnp.arange(CHUNK)
        z = jnp.einsum('bthd,bshd->bhts', q_blk, kh).astype(f32) * scale
        m = (key_pos[None, :] < t[:, None]) & valid[None, :]
        l_neg = jnp.where(m, jax.nn.log_sigmoid(-z), 0.0)
        log_w = jax.nn.log_sigmoid(z) + lax.cumsum(l_neg, axis=3, reverse=True) - l_neg
        w = jnp.where(m, jnp.exp(log_w), 0.0)
        return jnp.einsum('bhts,bshe->bthe', w.astype(vh.dtype), vh)

    out = lax.map(block, (qb, jnp.arange(nb)))
    return jnp.moveaxis(out, 0, 1).reshape(b, L, SB_WIDTH).astype(q.dtype)

def hybrid_layer(h_res, valid, w_in, conv_a, ssd_conv_w, ssd_conv_b, ssd_dt_bias, ssd_a_log,
                 ssd_d, ssd_norm, w_branch, w_out, w_ffn_in, w_ffn_out,
                 n_mix_pre, n_mix_post, n_ffn_pre, n_ffn_post):
    b, L, _ = h_res.shape
    h = rmsnorm_2(h_res, n_mix_pre)
    proj = jnp.einsum('bld,de->ble', h, w_in)
    (a_b, a_c, a_x, s_z, s_xbc, s_dt, r_q, r_k, r_v, r_g,
     sb_q, sb_k, sb_v, gate_logits) = jnp.split(proj, IN_SPLITS, axis=-1)
    y_a = short_conv_mixer(a_b, a_c, a_x, conv_a, valid)
    y_b = ssd_mixer(s_z, s_xbc, s_dt, ssd_conv_w, ssd_conv_b, ssd_dt_bias, ssd_a_log, ssd_d, ssd_norm, valid)
    y_c = retention_mixer(r_q, r_k, r_v, r_g, valid)
    y_d = stick_breaking_mixer(sb_q, sb_k, sb_v, valid)
    branches = jnp.stack([y_a, y_b, y_c, y_d], axis=2).astype(h.dtype)
    up = jnp.einsum('blnw,nwd->blnd', branches, w_branch)
    gates = jax.nn.sigmoid(gate_logits.reshape(b, L, N_BRANCH, D_MODEL))
    merged = jnp.sum(gates * up, axis=2)
    mix = jnp.einsum('bld,de->ble', merged, w_out)
    h_res = h_res + rmsnorm_2(mix, n_mix_post)
    f = jnp.einsum('bld,df->blf', rmsnorm_2(h_res, n_ffn_pre), w_ffn_in)
    f_gate, f_up = jnp.split(f, 2, axis=-1)
    f = jnp.einsum('blf,fd->bld', jax.nn.silu(f_gate) * f_up, w_ffn_out)
    return h_res + rmsnorm_2(f, n_ffn_post)

def second_inputs(seed: int = 0) -> dict:
    key = jax.random.key(seed)
    ks = jax.random.split(key, 18)
    f32 = jnp.float32

    def nrm(k, shape, scale):
        return jax.random.normal(k, shape, f32) * scale

    dt0 = jnp.exp(jax.random.uniform(ks[6], (DEPTH, SSD_HEADS), f32, math.log(1e-3), math.log(1e-1)))
    return {
        'x': nrm(ks[0], (BATCH, SEQ, D_MODEL), 1.0),
        'meta': nrm(ks[1], (N_META, D_MODEL), 1.0),
        'w_in': nrm(ks[2], (DEPTH, D_MODEL, IN_WIDTH), D_MODEL ** -0.5),
        'conv_a': nrm(ks[3], (DEPTH, CONV_A_K, CONV_A_WIDTH), CONV_A_K ** -0.5),
        'ssd_conv_w': nrm(ks[4], (DEPTH, SSD_CONV_K, SSD_CONV_DIM), SSD_CONV_K ** -0.5),
        'ssd_conv_b': nrm(ks[5], (DEPTH, SSD_CONV_DIM), 0.02),
        'ssd_dt_bias': dt0 + jnp.log(-jnp.expm1(-dt0)),
        'ssd_a_log': jnp.log(jax.random.uniform(ks[7], (DEPTH, SSD_HEADS), f32, 1.0, 16.0)),
        'ssd_d': 1.0 + nrm(ks[8], (DEPTH, SSD_HEADS), 0.1),
        'ssd_norm': 1.0 + nrm(ks[9], (DEPTH, SSD_INNER), 0.02),
        'w_branch': nrm(ks[10], (DEPTH, N_BRANCH, BRANCH_WIDTH, D_MODEL), BRANCH_WIDTH ** -0.5),
        'w_out': nrm(ks[11], (DEPTH, D_MODEL, D_MODEL), D_MODEL ** -0.5),
        'w_ffn_in': nrm(ks[12], (DEPTH, D_MODEL, 2 * D_FF_2), D_MODEL ** -0.5),
        'w_ffn_out': nrm(ks[13], (DEPTH, D_FF_2, D_MODEL), D_FF_2 ** -0.5),
        'norm_mix_pre': 1.0 + nrm(ks[14], (DEPTH, D_MODEL), 0.02),
        'norm_mix_post': 1.0 + nrm(ks[15], (DEPTH, D_MODEL), 0.02),
        'norm_ffn_pre': 1.0 + nrm(ks[16], (DEPTH, D_MODEL), 0.02),
        'norm_ffn_post': 1.0 + nrm(ks[17], (DEPTH, D_MODEL), 0.02),
    }

def second_block(x, meta, w_in, conv_a, ssd_conv_w, ssd_conv_b, ssd_dt_bias, ssd_a_log, ssd_d,
              ssd_norm, w_branch, w_out, w_ffn_in, w_ffn_out,
              norm_mix_pre, norm_mix_post, norm_ffn_pre, norm_ffn_post):
    b = x.shape[0]
    dtype = x.dtype
    h = jnp.concatenate([
        jnp.zeros((b, PAD, D_MODEL), dtype),
        jnp.broadcast_to(meta.astype(dtype)[None], (b, N_META, D_MODEL)),
        x,
    ], axis=1)
    valid = jnp.arange(h.shape[1]) >= PAD
    for l in range(DEPTH):
        h = hybrid_layer(h, valid, w_in[l], conv_a[l], ssd_conv_w[l], ssd_conv_b[l],
                         ssd_dt_bias[l], ssd_a_log[l], ssd_d[l], ssd_norm[l], w_branch[l],
                         w_out[l], w_ffn_in[l], w_ffn_out[l], norm_mix_pre[l],
                         norm_mix_post[l], norm_ffn_pre[l], norm_ffn_post[l])
    return h[:, CHUNK:]


def setup_inputs(seed=0):
    out = dict(first_inputs(seed))
    for name, value in second_inputs(seed + 1).items():
        if name != "x":
            out[name + "_2"] = value
    return out


def reference(
    x, c, mod_w, mod_b, norm_mix, norm_ffn, lru_w_in, lru_conv_w, lru_conv_b, lru_w_gates,
    lru_b_gates, lru_lambda, lru_w_out, kv_mod_w, kv_mod_b, kv_norm, w_kv, attn_w_q, attn_w_o,
    rel_bias, ffn_w_gate, ffn_w_up, ffn_w_down, final_norm, meta_2, w_in_2, conv_a_2,
    ssd_conv_w_2, ssd_conv_b_2, ssd_dt_bias_2, ssd_a_log_2, ssd_d_2, ssd_norm_2, w_branch_2,
    w_out_2, w_ffn_in_2, w_ffn_out_2, norm_mix_pre_2, norm_mix_post_2, norm_ffn_pre_2,
    norm_ffn_post_2,
):
    x = first_block(
        x, c, mod_w, mod_b, norm_mix, norm_ffn, lru_w_in, lru_conv_w, lru_conv_b, lru_w_gates,
        lru_b_gates, lru_lambda, lru_w_out, kv_mod_w, kv_mod_b, kv_norm, w_kv, attn_w_q,
        attn_w_o, rel_bias, ffn_w_gate, ffn_w_up, ffn_w_down, final_norm,
    )
    return second_block(
        x, meta_2, w_in_2, conv_a_2, ssd_conv_w_2, ssd_conv_b_2, ssd_dt_bias_2, ssd_a_log_2,
        ssd_d_2, ssd_norm_2, w_branch_2, w_out_2, w_ffn_in_2, w_ffn_out_2, norm_mix_pre_2,
        norm_mix_post_2, norm_ffn_pre_2, norm_ffn_post_2,
    )


_drawn_inputs = setup_inputs


def setup_inputs(seed=0):
    import zlib

    import numpy as np

    out = dict(_drawn_inputs(seed))
    spreads = {}
    factors = {'norm_mix': 4.208,
     'norm_ffn': 3.295,
     'lru_b_gates': 8.0,
     'kv_mod_b': 3.901,
     'kv_norm': 8.0,
     'ssd_conv_b_2': 2.855,
     'ssd_norm_2': 3.995,
     'norm_ffn_post_2': 3.164}
    for name, (base, spread) in spreads.items():
        noise = np.random.default_rng([zlib.crc32(name.encode()), seed]).standard_normal(out[name].shape)
        drawn = base * np.exp(spread * noise) if base else spread * noise
        out[name] = __import__('jax').numpy.asarray(drawn.astype(out[name].dtype))
    for name, factor in factors.items():
        out[name] = (out[name] * factor).astype(out[name].dtype)
    return out
```

```python
from contextlib import ExitStack

import numpy as np
import concourse.bass as bass
from concourse import mybir

F32 = mybir.dt.float32
F32R = mybir.dt.float32r
ALU = mybir.AluOpType
ACT = mybir.ActivationFunctionType
AX = mybir.AxisListType

P = 128
D = 1024
SEQ = 256
META = 16
TOK = META + SEQ
DT8 = D // P
LRU = 1280
LT = LRU // P
FF = 2816
FT = FF // P
EPS = 1e-6
SLOTS = 4
KEYS = ((0, 128), (128, 128), (256, 16))
SEG = ((0, 0, 272), (272, 128, 144), (416, 256, 16))
PACK = 432

MU = 256
MOD_SECTIONS = 14
MOD_UNITS = MOD_SECTIONS * D // MU

PARAMS = [("c", 8), ("mod_b", 112), ("norm_mix", 16), ("norm_ffn", 16), ("kv_norm", 8), ("final_norm", 8),
          ("lru_conv_w", 40), ("lru_conv_b", 10), ("lru_b_gates", 20), ("lru_lambda", 10),
          ("norm_mix_pre", 16), ("norm_mix_post", 16), ("norm_ffn_pre", 16), ("norm_ffn_post", 16),
          ("conv_a", 48), ("ssd_conv_w", 128), ("ssd_conv_b", 32), ("ssd_norm", 16), ("ssd_d", 16)]
PCOL, _n = {}, 0
for _name, _w in PARAMS:
    PCOL[_name] = _n
    _n += _w
PCOLS = _n

CONSTS = [("ident", 128), ("suffix", 128), ("incl", PACK), ("strict", PACK), ("decay", 4 * PACK),
          ("cos", TOK), ("sin", TOK)]
CCOL, _n = {}, 0
for _name, _w in CONSTS:
    CCOL[_name] = _n
    _n += _w
CCOLS = _n
BIASW = 384


class Phase:

    def __init__(self, name, kind, n, rhs="H", kb=8, off=0, T=TOK, per=1, l=0, mods=None, t0=0, norm=0):
        self.name, self.kind, self.n, self.kb, self.rhs = name, kind, n, kb, rhs
        self.off, self.T, self.per, self.l, self.mods, self.t0 = off, T, per, l, mods, t0
        self.rounds = -(-n // SLOTS)
        pair = kind in ("glu", "cx", "merge", "merge_split", "rotate")
        self.units = n // 2 if pair else n // per
        self.count = {s: self.units for s in SIGNALS.get(kind, ())}

    def slots(self, r):
        return min(SLOTS, self.n - SLOTS * r)


SIGNALS = {"conv_split": ("mixed", "high", "low"), "conv_silu": ("mixed", "high"), "vtok": ("turned", "copied"),
           "glu": ("high", "low"), "conv_gate": ("high", "low"), "merge_split": ("mixed", "high", "low"),
           "rotate": ("mixed",)}
OWN_WAITS = {"conv_split": 3, "conv_silu": 3, "conv_gate": 3}


def plan():
    seq = dict(off=META, T=SEQ)
    ph = [Phase("lru_x", "conv_split", 10, mods=8, **seq), Phase("lru_y", "act", 10, mods=14, **seq),
          Phase("lru_gates", "gates", 10, "XC", kb=4, **seq), Phase("lru_out", "resid", 8, "XC", kb=10, **seq),
          Phase("ffn_up0", "glu", 44, mods=20, **seq),
          Phase("ffn_down0", "resid", 16, "F", kb=11, per=2, mods=42, **seq),
          Phase("kv_k", "act", 4, mods=50, **seq), Phase("kv_v", "vtok", 4, **seq), Phase("q", "act", 8, **seq),
          Phase("attn_out", "resid", 8, "Y", mods=52, **seq), Phase("ffn_up1", "glu", 44, **seq),
          Phase("ffn_down1", "resid", 16, "F", kb=11, per=2, **seq)]
    for l in range(2):
        tail = seq if l else {}
        ph += [Phase(f"a_cx{l}", "cx", 16, l=l), Phase(f"a_b{l}", "conv_gate", 8, l=l),
               Phase(f"up_a{l}", "merge", 16, "HY", l=l, **tail),
               Phase(f"dt{l}", "dt", 1, l=l), Phase(f"s_x{l}", "conv_silu", 8, l=l),
               Phase(f"s_bc{l}", "conv_silu", 8, l=l, t0=8), Phase(f"s_z{l}", "act", 8, l=l),
               Phase(f"up_b{l}", "merge", 16, "HY", l=l, **tail),
               Phase(f"r_v{l}", "vtok", 8, l=l), Phase(f"r_q{l}", "rotate", 8, l=l),
               Phase(f"r_k{l}", "rotate", 8, l=l), Phase(f"r_g{l}", "act", 8, l=l),
               Phase(f"up_c{l}", "merge", 16, "HY", l=l, **tail),
               Phase(f"b_v{l}", "vtok", 8, l=l), Phase(f"b_k{l}", "act", 8, l=l), Phase(f"b_q{l}", "act", 8, l=l),
               Phase(f"up_d{l}", "merge_split", 16, "HY", l=l, **tail),
               Phase(f"mix_out{l}", "act", 8, "M", l=l, **tail),
               Phase(f"ffn_up{2 + l}", "glu", 44, **tail),
               Phase(f"ffn_down{2 + l}", "act", 16, "F", kb=11, per=2, **tail)]
    count = {s: 0 for s in ("mixed", "high", "low", "turned", "copied")}
    slot, bank = [0] * SLOTS, [0] * SLOTS
    for p in ph:
        p.base = dict(count)
        for s, c in p.count.items():
            count[s] += c
        p.end = dict(count)
        p.slot, p.bank = list(slot), list(bank)
        for c in range(p.n):
            slot[c % SLOTS] += 1
            if p.per == 1 or c % 2:
                bank[c % SLOTS] += 1
        p.bank_end = list(bank)
    later = [[] for _ in range(SLOTS)]
    for p in reversed(ph):
        p.next_kb = {}
        for c in reversed(range(p.n)):
            s = c % SLOTS
            p.next_kb[c // SLOTS, s] = later[s][-1] if later[s] else None
            later[s].append(p.kb)
        p.looped = p.rounds
        if p.n % SLOTS:
            p.looped = 0
        elif any(p.next_kb[p.rounds - 1, s] != p.kb for s in range(SLOTS)):
            p.looped = p.rounds - 1
        if p.looped < 2:
            p.looped = 0
    return ph


class Own:

    def __init__(self, eng, sem):
        self.eng, self.sem, self.n, self.start, self.in_loop = eng, sem, 0, 0, None

    def wait(self, ins):
        self.n += 1
        ins.then_inc(self.sem, 1)
        at = self.n if self.in_loop is None else self.start + self.in_loop + self.n
        self.eng.wait_ge(self.sem, at)


def rounds(eng, p, step, own=None, per_round=0):
    if p.looped:
        if own is not None:
            own.start, own.n = own.n, 0
        with eng.Fori(0, p.looped) as r:
            if own is not None:
                own.in_loop = r * per_round
            step(r, True)
        if own is not None:
            assert own.n == per_round, (p.name, own.n, per_round)
            own.in_loop, own.n = None, own.start + p.looped * per_round
    for r in range(p.looped, p.rounds):
        step(r, False)


def flat(buf, t, off, n):
    if isinstance(t, int):
        return buf[:, t, off:off + n]
    return buf[:, bass.ds(t, 1), off:off + n].rearrange("p a n -> p (a n)")


def col(buf, c):
    return buf[:, c:c + 1] if isinstance(c, int) else buf[:, bass.ds(c, 1)]


def two_layer_pair(nc, a, out):
    ph = plan()
    by = {p.name: p for p in ph}
    ctx = ExitStack()
    with ctx:
        base = nc.sbuf_base + 31 & ~31
        top = [base]

        def place(name, shape, dt=F32, at=None):
            size = int(np.prod(shape[1:])) * 4
            if at is None:
                at = top[0]
                top[0] = at + (size + 31 & ~31)
            assert at + size <= nc.sbuf_usable_end, (name, at + size - nc.sbuf_usable_end)
            return nc.alloc_sbuf_tensor_at(name, shape, dt, offset=at)

        raw = place("raw", [P, SLOTS, 11 * P])
        w_hi = place("w_hi", [P, SLOTS, 11 * P], F32R)
        w_lo = place("w_lo", [P, SLOTS, 11 * P], F32R)
        X = place("x_res", [P, DT8, TOK])
        Hh = place("h_hi", [P, DT8, TOK], F32R)
        Hl = place("h_lo", [P, DT8, TOK], F32R)
        S8 = place("scratch8", [P, DT8, TOK])
        m_at = top[0]
        M = place("merged", [P, DT8, TOK])
        BT = place("bias_t", [P, 8, SEQ], at=m_at)
        M2 = place("lru_m2", [P, LT - 2, SEQ], at=m_at)
        OH = place("onehot", [32, BIASW], at=m_at)
        RB = place("rel_bias", [32, 8], at=m_at + 4 * BIASW)
        BR = place("bias_row", [8, BIASW], at=m_at + 8 * BIASW)
        CI = place("conv_in", [P, SLOTS, TOK + 4])
        CO = place("conv_out", [P, SLOTS, TOK])
        ACS = place("acs", [16, TOK])
        RSTD = place("rstd", [P, TOK])
        PV = place("params", [P, PCOLS])
        CS = place("consts", [P, CCOLS])
        ONES = place("ones", [P, P])
        MOD = place("mod", [P, MOD_SECTIONS * 8])
        SM = place("small", [P, 224])
        region = top[0]

        def tiles(name, shape, tile, dt=F32):
            return place(name, shape, dt, at=region + (int(tile * TOK) * 4 + 31 & ~31))

        Fh, Fl = tiles("f_hi", [P, FT, TOK], 0, F32R), tiles("f_lo", [P, FT, TOK], FT, F32R)
        MW = tiles("mod_raw", [P, 2, 8, MU], 52)
        ACC = tiles("mod_acc", [P, 2, MU], 50)
        XCh, XCl = tiles("xc_hi", [P, LT, TOK], 0, F32R), tiles("xc_lo", [P, LT, TOK], LT, F32R)
        YB, XC = tiles("y_branch", [P, LT, SEQ], 20), tiles("xc", [P, LT, SEQ], 30)
        LA = tiles("lru_a", [P, LT, SEQ], 40)
        Yh, Yl = tiles("y_hi", [P, DT8, TOK], 0, F32R), tiles("y_lo", [P, DT8, TOK], 8, F32R)
        AK, AQ = tiles("a_k", [P, 4, SEQ], 16), tiles("a_q", [P, 8, SEQ], 20)
        AV = tiles("a_v", [P, 2, 512], 28)
        AL, APT = tiles("a_logits", [P, 2, 384], 32), tiles("a_probs_t", [P, 2, 384], 35)
        U = tiles("u", [P, DT8, TOK + 2], 16)
        XS, BC, Z = tiles("s_xs", [P, 8, TOK], 16), tiles("s_bc", [P, 8, 384], 24), tiles("s_z", [P, 8, TOK], 36)
        XT = tiles("s_xdt", [P, 3, D], 44)
        SE, SX = tiles("s_decay", [P, 2, PACK], 55.5), tiles("s_mix", [P, 2, PACK], 59)
        SD = tiles("s_dt", [16, 7, TOK], 55.5)
        CB = tiles("s_cb", [P, 4, PACK], 0)
        YQ = tiles("y_squares", [P, 8, TOK], 24)
        YR = tiles("y_rstd_rows", [P, 4, TOK], 55.5)
        RQ, RK, RV = tiles("r_q", [P, 8, TOK], 16), tiles("r_k", [P, 8, 384], 24), tiles("r_v", [P, 3, D], 36)
        RG, RP = tiles("r_g", [P, 8, TOK], 47.4), tiles("r_p", [P, 2, PACK], 56)
        BK, BV, BQ = tiles("b_k", [P, 8, 384], 16), tiles("b_v", [P, 3, D], 28), tiles("b_q", [P, 8, TOK], 40)
        ZS, SA, SS, SW = (tiles(n, [P, 2, PACK], 48 + 4 * i) for i, n in enumerate(("b_z", "b_a", "b_s", "b_w")))
        Mh, Ml = tiles("m_hi", [P, DT8, TOK], 16, F32R), tiles("m_lo", [P, DT8, TOK], 24, F32R)

        bank = [ctx.enter_context(nc.psum_tensor(f"stream{i}", [P, 512], F32)) for i in range(SLOTS)]
        B = [ctx.enter_context(nc.psum_tensor(f"side{i}", [P, 512], F32)) for i in range(4)]

        def sem(name):
            return ctx.enter_context(nc.semaphore(name))

        raw_ready = [sem(f"raw_ready{i}") for i in range(SLOTS)]
        hi_ready = [sem(f"hi_ready{i}") for i in range(SLOTS)]
        lo_ready = [sem(f"lo_ready{i}") for i in range(SLOTS)]
        chunk_done = [sem(f"chunk_done{i}") for i in range(SLOTS)]
        bank_free = [sem(f"bank_free{i}") for i in range(SLOTS)]
        sig = {s: sem(s) for s in ("mixed", "high", "low", "turned", "copied")}
        vec_own, act_own = sem("vec_own"), sem("act_own")
        loaded = {n: sem(f"loaded_{n}") for n in ("params", "consts", "x", "meta", "heads", "onehot", "bias")}
        const_ready = sem("const_ready")
        mod_ready = [sem(f"mod_ready{i}") for i in range(2)]
        mod_acc = [sem(f"mod_acc{i}") for i in range(2)]
        mod_sum = sem("mod_sum")
        squares, sum_done, rstd_ready = sem("squares"), sem("sum_done"), sem("rstd_ready")
        scaled, h_hi, h_lo = sem("scaled"), sem("h_hi_ready"), sem("h_lo_ready")
        silu_c = sem("silu_c")
        sp_u, sp_w, sp_ln = sem("sp_u"), sem("sp_w"), sem("sp_ln")
        side = {n: sem(n) for n in (
            "gate_exp", "gate_sig", "gate_pow", "gate_m2", "gate_sqrt", "lru_y32", "lru_hi", "lru_lo",
            "bias_sum", "bias_row", "bias_out", "att_s", "att_max", "att_exp", "att_p", "att_t", "att_pt",
            "att_o", "side_hi", "side_lo",
            "dt_in", "dt_neg", "dt_acs", "dt_turned", "dt_cols", "x_turned", "x_scaled", "cb_done", "cb_masked",
            "acs_rows", "decay_log", "decay_exp", "decay_mix", "head_y", "y_taken", "y_sq", "y_sum", "y_rstd", "y32",
            "ret_s", "ret_p", "ret_y", "ret_copy", "ret_mean", "sb_s", "sb_z", "sb_soft", "sb_sp", "sb_r",
            "sb_logw", "sb_w", "sb_we", "sb_o")}
        stored, finished = sem("stored"), sem("finished")

        norms = [(n, split) for n, split in [("mix0", 1), ("ffn0", 1), ("kv", 1), ("mix1", 1), ("ffn1", 1), ("final", 0)]]
        for l in range(2):
            norms += [(f"pre{l}", 1), (f"post{l}", 0), (f"fpre{l}", 1), (f"fpost{l}", 0)]
        stat_no = {n: i for i, (n, _) in enumerate(norms)}
        split_no = {n: sum(s for _, s in norms[:i]) for i, (n, _) in enumerate(norms)}

        rhs_of = {"H": (Hh, Hl), "XC": (XCh, XCl), "F": (Fh, Fl), "Y": (Yh, Yl), "M": (Mh, Ml)}
        ident = CS[:, CCOL["ident"]:CCOL["ident"] + P]
        suffix = CS[:, CCOL["suffix"]:CCOL["suffix"] + P]
        incl = CS[:, CCOL["incl"]:CCOL["incl"] + PACK]
        strict = CS[:, CCOL["strict"]:CCOL["strict"] + PACK]
        cos, sin = (CS[:, CCOL[n]:CCOL[n] + TOK] for n in ("cos", "sin"))
        CSC, GS, NB, SPL, SPT, SPW, DTT, NAT, AMX, ASM, EAL, EPSC, EA = 0, 8, 16, 36, 46, 56, 96, 144, 192, 196, 200, 210, 212
        bias_rows = nc.dram_tensor("bias_rows", (8, P, BIASW), F32, kind="Internal").ap()

        def pcol(name, k=0):
            return PV[:, PCOL[name] + k:PCOL[name] + k + 1]

        def gen(p, r, s):
            return p.slot[s] + r

        block = ctx.enter_context(nc.Block())

        @block.sync
        def _(sp):
            sp.dma_start(PV[:, :], a["params"]).then_inc(loaded["params"], 16)
            sp.dma_start(OH[:, :], a["onehot"]).then_inc(loaded["onehot"], 16)
            sp.dma_start(RB[:, :], a["rel_bias"]).then_inc(loaded["onehot"], 16)
            sp.dma_start(X[:, :, META:], a["x"]).then_inc(loaded["x"], 16)
            sp.dma_start(CS[:, :], a["consts"]).then_inc(loaded["consts"], 16)
            sp.dma_start(X[:, :, 0:META], a["meta"]).then_inc(loaded["meta"], 16)
            sp.dma_start(SM[0:16, EAL:EAL + 4], a["heads"]).then_inc(loaded["heads"], 16)
            sp.wait_ge(side["bias_row"], 1)
            sp.dma_start(bias_rows, BR[:, :].unsqueeze(1).to_broadcast([8, P, BIASW])).then_inc(side["bias_out"], 16)
            sp.wait_ge(side["bias_out"], 16)

            def load(p, r, looped):
                for s in range(p.slots(r) if not looped else SLOTS):
                    if p.name != ph[0].name or r:
                        sp.wait_ge(lo_ready[s], gen(p, r, s))
                    w = a[p.name]
                    src = w[r * SLOTS + s] if isinstance(r, int) else \
                        w[bass.ds(r * SLOTS + s, 1)].rearrange("c p n -> (c p) n")
                    sp.dma_start(raw[:, s, 0:p.kb * P], src).then_inc(raw_ready[s], 16)

            for p in ph:
                rounds(sp, p, lambda r, looped: load(p, r, looped))
                if p.name == "lru_out":
                    sp.wait_ge(side["lru_lo"], LT)
                    sp.dma_start(BT[:, :, :], bass.AP(tensor=bias_rows.tensor, offset=P - 1,
                                                      ap=[[BIASW - 1, P], [P * BIASW, 8], [1, SEQ]])).then_inc(loaded["bias"], 16)
            sp.wait_ge(finished, 1)
            sp.dma_start(out, X[:, :, META:]).then_inc(stored, 16)
            sp.wait_ge(stored, 16)

        @block.gpsimd
        def _(pool):
            def load_mod(r, first=False):
                for i in range(2):
                    if not first:
                        pool.wait_ge(mod_acc[i], r)
                    src = a["mod_w"][2 * r + i] if isinstance(r, int) else \
                        a["mod_w"][bass.ds(2 * r + i, 1)].rearrange("u p k n -> (u p) k n")
                    pool.dma_start(MW[:, i, :, :], src).then_inc(mod_ready[i], 16)

            load_mod(0, True)
            with pool.Fori(1, 10) as r:
                load_mod(r)
            with pool.Fori(10, MOD_UNITS // 2) as r:
                load_mod(r)

        @block.tensor
        def _(pe):
            def three(ps, w, wcols, x, k, off, n, first, last):
                W = slice(wcols * P, (wcols + 1) * P)
                pe.matmul(ps, w_hi[:, w, W], x[0][:, k, off:off + n], start=first, stop=False)
                pe.matmul(ps, w_hi[:, w, W], x[1][:, k, off:off + n], start=False, stop=False)
                return pe.matmul(ps, w_lo[:, w, W], x[0][:, k, off:off + n], start=False, stop=last)

            def chunk(p, r, s):
                pe.wait_ge(lo_ready[s], gen(p, r, s) + 1)
                b = s if p.per == 1 else s | 1
                if p.per == 1 or s % 2 == 0:
                    pe.wait_ge(bank_free[b], p.bank[b] + r)
                if p.kind == "gates":
                    j = 4 * r + s
                    for g in range(2):
                        for k in range(2):
                            last = three(bank[s][:, g * SEQ:(g + 1) * SEQ], s, 2 * g + k, rhs_of["XC"],
                                         2 * (j // 2) + k, 0, SEQ, k == 0, k == 1)
                else:
                    x = rhs_of[p.rhs] if p.rhs != "HY" else rhs_of["HY"[s % 2]]
                    kx = 11 * (s % 2) if p.per == 2 else 0
                    off = 0 if p.rhs in ("XC",) else p.off
                    for k in range(p.kb):
                        last = three(bank[b][:, 0:p.T], s, k, x, kx + k, off, p.T,
                                     k == 0 and (p.per == 1 or s % 2 == 0), k == p.kb - 1 and (p.per == 1 or s % 2 == 1))
                last.then_inc(chunk_done[s], 1)

            def turn(p, r, s):
                t = SLOTS * r + s
                b = B[s % 2]
                pe.wait_ge(bank_free[s], p.bank[s] + r + 1)
                pe.wait_ge(sig["copied"], p.base["copied"] + t + 1)
                keys = KEYS if p.T == TOK else KEYS[:2]
                for i, (q, n) in enumerate(keys):
                    last = pe.transpose(b[0:n, i * P:(i + 1) * P], CO[:, s, q:q + n], ident)
                last.then_inc(sig["turned"], 1)

            def mod_sums(p, r):
                for i in range(2):
                    m = p.mods // 2 + r
                    mod_columns(m, i)

            def mod_columns(m, i):
                pe.wait_ge(mod_acc[i], m + 1)
                for j in range(2):
                    last = pe.matmul(B[2 + i][:, j:j + 1], ACC[:, i, j * P:(j + 1) * P], ONES[:, 0:1],
                                     start=True, stop=True)
                last.then_inc(mod_sum, 1)

            def step(p, r, looped):
                n = SLOTS if looped else p.slots(r)
                for s in range(n):
                    chunk(p, r, s)
                    if p.kind == "vtok" and s:
                        turn(p, r, s - 1)
                if p.kind == "vtok":
                    turn(p, r, n - 1)
                if p.mods is not None:
                    mod_sums(p, r)

            def sum_squares(name, off, n):
                i = stat_no[name]
                for k in range(DT8):
                    if k % 4 == 0:
                        pe.wait_ge(squares, 2 * i + k // 4 + 1)
                    last = pe.matmul(B[0][:, 0:n], ONES[:, :], S8[:, k, off:off + n], start=k == 0, stop=k == DT8 - 1)
                last.then_inc(sum_done, 1)

            def attention():
                def scores(h):
                    if h >= 2:
                        pe.wait_ge(side["att_p"], h - 1)
                    pe.matmul(B[h % 2][:, 0:P], AQ[:, h, 0:P], AK[:, h // 2, 0:P], start=True, stop=True)
                    pe.matmul(B[h % 2][:, P:384], AQ[:, h, P:SEQ], AK[:, h // 2, :], start=True, stop=True)\
                        .then_inc(side["att_s"], 1)

                def turn_probs(h):
                    pe.wait_ge(side["att_p"], h + 1)
                    if h:
                        pe.wait_ge(side["att_pt"], h)
                    for i in range(3):
                        last = pe.transpose(B[2][:, i * P:(i + 1) * P], AL[:, h % 2, i * P:(i + 1) * P], ident)
                    last.then_inc(side["att_t"], 1)

                def values(h):
                    pe.wait_ge(side["att_pt"], h + 1)
                    if h:
                        pe.wait_ge(side["side_lo"], h)
                    v = slice(h // 2 * P, (h // 2 + 1) * P)
                    pe.matmul(B[3][:, 0:SEQ], AV[:, 0, v], APT[:, h % 2, 0:SEQ], start=True, stop=False)
                    pe.matmul(B[3][:, P:SEQ], AV[:, 1, v], APT[:, h % 2, SEQ:], start=False, stop=True)\
                        .then_inc(side["att_o"], 1)

                for i in range(8 + 2):
                    if i < 8:
                        scores(i)
                    if i >= 2:
                        values(i - 2)
                    if 1 <= i <= 8:
                        turn_probs(i - 1)

            def packed_scores(b, key, ktiles, q, qt):
                for n, (c, q0, w) in enumerate(SEG):
                    for i, (kt, qq) in enumerate(zip(ktiles, qt)):
                        last = pe.matmul(b[:, c:c + w], key[:, kt, n * P:(n + 1) * P], q[:, qq, q0:q0 + w],
                                         start=i == 0, stop=i == len(qt) - 1)
                return last

            def weighted(b, rows, v, vcols, w):
                for n, (c, q0, m) in enumerate(SEG):
                    k = KEYS[n][1]
                    last = pe.matmul(b[rows, q0:q0 + m], v[0:k, n, vcols], w[0:k, c:c + m], start=n == 0, stop=n == 2)
                return last

            def state_space(l):
                pe.wait_ge(side["dt_acs"], l + 1)
                for i in range(2):
                    for n, (q, w) in enumerate(KEYS):
                        src = SD[0:16, 6, q:q + w] if i == 0 else ACS[0:16, q:q + w]
                        last = pe.transpose(B[0][0:w, 48 * i + 16 * n:48 * i + 16 * n + 16], src, CS[0:16, 0:16])
                last.then_inc(side["dt_turned"], 1)
                p = by[f"s_z{l}"]
                pe.wait_ge(side["dt_cols"], l + 1)
                pe.wait_ge(sig["high"], by[f"s_x{l}"].end["high"])
                for m in range(6):
                    if m >= 3:
                        pe.wait_ge(side["x_scaled"], 6 * l + m - 2)
                    n, half = m // 2, m % 2
                    q, w = KEYS[n]
                    for j in range(4):
                        last = pe.transpose(B[1 + m % 3][0:w, j * P:(j + 1) * P], XS[:, 4 * half + j, q:q + w], ident)
                    last.then_inc(side["x_turned"], 1)
                pe.wait_ge(side["x_scaled"], 6 * (l + 1))
                pe.wait_ge(sig["high"], by[f"s_bc{l}"].end["high"])
                for g in range(4):
                    packed_scores(B[g], BC, [g], BC, [4 + g]).then_inc(side["cb_done"], 1)

                def rows(h):
                    if h < 2:
                        pe.wait_ge(side["cb_masked"], 4 * l + 4)
                    else:
                        pe.wait_ge(side["decay_log"], 16 * l + h - 1)
                    sel = CS[0:16, h:h + 1].to_broadcast([16, P])
                    pe.matmul(B[h % 2][:, 0:TOK], sel, ACS[0:16, :], start=True, stop=True).then_inc(side["acs_rows"], 1)

                def outputs(h):
                    pe.wait_ge(side["decay_mix"], 16 * l + h + 1)
                    if h >= 4 and h % 2 == 0:
                        pe.wait_ge(side["y_taken"], 8 * l + h // 2 - 1)
                    lo = h % 2 * 64
                    weighted(B[2 + h // 2 % 2], slice(lo, lo + 64), XT, slice(h * 64, h * 64 + 64), SX[:, h % 2])\
                        .then_inc(side["head_y"], 1)

                for i in range(17):
                    if i < 16:
                        rows(i)
                    if i >= 1:
                        outputs(i - 1)
                for g in range(4):
                    pe.wait_ge(side["y_sq"], 8 * l + g + 1)
                    for k in range(2):
                        last = pe.matmul(B[g][:, 0:TOK], ONES[:, :], YQ[:, 2 * g + k, :], start=k == 0, stop=k == 1)
                    last.then_inc(side["y_sum"], 1)

            def retention(l):
                pe.wait_ge(sig["mixed"], by[f"r_k{l}"].end["mixed"])
                pe.wait_ge(sig["copied"], by[f"r_v{l}"].end["copied"] + 2)

                def scores(h):
                    if h >= 2:
                        pe.wait_ge(side["ret_p"], 4 * l + h - 1)
                    packed_scores(B[h % 2], RK, [2 * h, 2 * h + 1], RQ, [2 * h, 2 * h + 1]).then_inc(side["ret_s"], 1)

                def outputs(h):
                    pe.wait_ge(side["ret_p"], 4 * l + h + 1)
                    for e in range(2):
                        t = 2 * h + e
                        if t >= 2:
                            pe.wait_ge(side["ret_copy"], 8 * l + t - 1)
                        weighted(B[2 + e], slice(0, P), RV, slice(t * P, (t + 1) * P), RP[:, h % 2])\
                            .then_inc(side["ret_y"], 1)

                for i in range(5):
                    if i < 4:
                        scores(i)
                    if i >= 1:
                        outputs(i - 1)
                for h in range(4):
                    pe.wait_ge(side["ret_copy"], 8 * (l + 1))
                    for k in range(2):
                        last = pe.matmul(B[h][:, 0:TOK], ONES[:, :], S8[:, 2 * h + k, :], start=k == 0, stop=k == 1)
                    last.then_inc(side["ret_mean"], 1)
                for h in range(4):
                    pe.wait_ge(side["y_sq"], 8 * l + 4 + h + 1)
                    for k in range(2):
                        last = pe.matmul(B[h][:, 0:TOK], ONES[:, :], YQ[:, 2 * h + k, :], start=k == 0, stop=k == 1)
                    last.then_inc(side["y_sum"], 1)

            def stick_breaking(l):
                pe.wait_ge(sig["copied"], by[f"b_v{l}"].end["copied"] + 2)
                for s in range(SLOTS):
                    pe.wait_ge(bank_free[s], by[f"b_q{l}"].bank_end[s])

                def scores(h):
                    if h >= 2:
                        pe.wait_ge(side["sb_z"], 8 * l + h - 1)
                    packed_scores(B[h % 2], BK, [h], BQ, [h]).then_inc(side["sb_s"], 1)

                def suffix_sums(h):
                    pe.wait_ge(side["sb_sp"], 8 * l + h + 1)
                    if h:
                        pe.wait_ge(side["sb_logw"], 8 * l + h)
                    S = SS[:, h % 2]
                    b = B[2]
                    pe.matmul(b[:, 0:272], suffix, S[:, 0:272], start=True, stop=False)
                    pe.matmul(b[:, P:272], ONES[:, :], S[:, 272:416], start=False, stop=False)
                    pe.matmul(b[:, 256:272], ONES[0:16, :], S[0:16, 416:432], start=False, stop=True)
                    pe.matmul(b[:, 272:416], suffix, S[:, 272:416], start=True, stop=False)
                    pe.matmul(b[:, 400:416], ONES[0:16, :], S[0:16, 416:432], start=False, stop=True)
                    pe.matmul(b[:, 416:432], suffix[0:16, :], S[0:16, 416:432], start=True, stop=True)\
                        .then_inc(side["sb_r"], 1)

                def outputs(h):
                    pe.wait_ge(side["sb_w"], 8 * l + h + 1)
                    if h:
                        pe.wait_ge(side["side_lo"], 24 + 24 * l + h)
                    weighted(B[3], slice(0, P), BV, slice(h * P, (h + 1) * P), SW[:, h % 2]).then_inc(side["sb_o"], 1)

                for i in range(10):
                    if i < 8:
                        scores(i)
                    if 1 <= i <= 8:
                        suffix_sums(i - 1)
                    if i >= 2:
                        outputs(i - 2)

            def run(name):
                p = by[name]
                rounds(pe, p, lambda r, looped: step(p, r, looped))

            def normed(name):
                pe.wait_ge(h_lo, 8 * (split_no[name] + 1))

            pe.wait_ge(loaded["onehot"], 32)
            pe.matmul(B[1][0:8, 0:BIASW], RB[:, :], OH[:, :], start=True, stop=True).then_inc(side["bias_sum"], 1)
            pe.wait_ge(const_ready, 1)
            for m in range(4):
                for i in range(2):
                    mod_columns(m, i)
            pe.wait_ge(loaded["consts"], 16)
            sum_squares("mix0", META, SEQ)
            normed("mix0")
            run("lru_x")
            run("lru_y")
            pe.wait_ge(sig["low"], by["lru_x"].end["low"])
            run("lru_gates")
            pe.wait_ge(side["lru_lo"], LT)
            run("lru_out")
            sum_squares("ffn0", META, SEQ)
            normed("ffn0")
            run("ffn_up0")
            pe.wait_ge(sig["low"], by["ffn_up0"].end["low"])
            run("ffn_down0")
            sum_squares("kv", META, SEQ)
            normed("kv")
            run("kv_k")
            run("kv_v")
            sum_squares("mix1", META, SEQ)
            normed("mix1")
            run("q")
            for s in range(SLOTS):
                pe.wait_ge(bank_free[s], by["q"].bank_end[s])
            pe.wait_ge(sig["copied"], by["kv_v"].end["copied"] + 2)
            attention()
            pe.wait_ge(side["side_lo"], 8)
            run("attn_out")
            sum_squares("ffn1", META, SEQ)
            normed("ffn1")
            run("ffn_up1")
            pe.wait_ge(sig["low"], by["ffn_up1"].end["low"])
            run("ffn_down1")
            sum_squares("final", META, SEQ)
            for l in range(2):
                off, n = (META, SEQ) if l else (0, TOK)
                sum_squares(f"pre{l}", 0, TOK)
                normed(f"pre{l}")
                run(f"a_cx{l}")
                run(f"a_b{l}")
                pe.wait_ge(sig["low"], by[f"a_b{l}"].end["low"])
                run(f"up_a{l}")
                run(f"dt{l}")
                run(f"s_x{l}")
                run(f"s_bc{l}")
                run(f"s_z{l}")
                state_space(l)
                pe.wait_ge(side["side_lo"], 16 + 24 * l)
                run(f"up_b{l}")
                run(f"r_v{l}")
                run(f"r_q{l}")
                run(f"r_k{l}")
                run(f"r_g{l}")
                retention(l)
                pe.wait_ge(side["side_lo"], 24 + 24 * l)
                run(f"up_c{l}")
                run(f"b_v{l}")
                run(f"b_k{l}")
                run(f"b_q{l}")
                stick_breaking(l)
                pe.wait_ge(side["side_lo"], 32 + 24 * l)
                run(f"up_d{l}")
                pe.wait_ge(sig["low"], by[f"up_d{l}"].end["low"])
                run(f"mix_out{l}")
                sum_squares(f"post{l}", off, n)
                sum_squares(f"fpre{l}", off, n)
                normed(f"fpre{l}")
                run(f"ffn_up{2 + l}")
                pe.wait_ge(sig["low"], by[f"ffn_up{2 + l}"].end["low"])
                run(f"ffn_down{2 + l}")
                sum_squares(f"fpost{l}", off, n)

        @block.scalar
        def _(act):
            own = Own(act, act_own)

            def cut(p, r, s, looped):
                kb = p.kb if looped else p.next_kb[r, s]
                if kb is None:
                    return
                g = gen(p, r, s) + 1
                act.wait_ge(raw_ready[s], 16 * (g + 1))
                act.wait_ge(chunk_done[s], g)
                act.copy(w_hi[:, s, 0:kb * P], raw[:, s, 0:kb * P]).then_inc(hi_ready[s], 1)

            acts = {"lru_y": (YB, ACT.Gelu_apprx_tanh, 1.0), "kv_k": (AK, ACT.Copy, 1.0), "q": (AQ, ACT.Copy, 1.0)}
            for l in range(2):
                acts |= {f"s_z{l}": (Z, ACT.Silu, 1.0), f"r_g{l}": (RG, ACT.Silu, 1.0), f"b_k{l}": (BK, ACT.Copy, 1.0),
                         f"b_q{l}": (BQ, ACT.Copy, P ** -0.5), f"mix_out{l}": (M, ACT.Copy, 1.0),
                         f"ffn_down{2 + l}": (M, ACT.Copy, 1.0)}

            def step(p, r, looped):
                n = SLOTS if looped else p.slots(r)
                for s in range(n):
                    done = gen(p, r, s) + 1
                    free = p.bank[s] + r + 1
                    t = r * SLOTS + s
                    if p.kind in ("conv_split", "conv_silu"):
                        act.wait_ge(chunk_done[s], done)
                        act.copy(CI[:, s, 3:3 + p.T], bank[s][:, 0:p.T]).then_inc(bank_free[s], 1)
                        cut(p, r, s, looped)
                        act.wait_ge(sig["mixed"], p.base["mixed"] + t + 1)
                        if p.kind == "conv_split":
                            act.copy(flat(XCh, t, 0, p.T), flat(XC, t, 0, p.T)).then_inc(sig["high"], 1)
                        else:
                            dst = XS if p.t0 == 0 else BC
                            act.activation(flat(dst, t, 0, p.T), CO[:, s, 0:p.T], ACT.Silu).then_inc(sig["high"], 1)
                        continue
                    if p.kind == "vtok":
                        act.wait_ge(chunk_done[s], done)
                        act.wait_ge(sig["copied"], p.base["copied"] + t + 1)
                        act.copy(CO[:, s, 0:p.T], bank[s][:, 0:p.T]).then_inc(bank_free[s], 1)
                    if p.kind == "act":
                        b = s
                        if p.per == 2:
                            t = r * 2 + s // 2
                        if p.per == 1 or s % 2:
                            act.wait_ge(chunk_done[s], done)
                            dst, func, scale = acts[p.name]
                            off = p.off if dst is M else 0
                            act.activation(flat(dst, t, off, p.T), bank[b][:, 0:p.T], func, scale=scale)\
                                .then_inc(bank_free[b], 1)
                    if p.kind in ("glu", "cx", "merge", "merge_split") and s % 2 == 0:
                        func = {"glu": ACT.Silu, "cx": ACT.Copy}.get(p.kind, ACT.Sigmoid)
                        act.wait_ge(chunk_done[s], done)
                        act.activation(CI[:, s, 3:3 + p.T], bank[s][:, 0:p.T], func).then_inc(bank_free[s], 1)
                    if p.kind in ("glu", "cx", "merge", "merge_split") and s % 2:
                        q = r * 2 + s // 2
                        act.wait_ge(bank_free[s], free)
                        if p.kind == "glu":
                            act.copy(flat(Fh, q, p.off, p.T), CO[:, s - 1, 0:p.T]).then_inc(sig["high"], 1)
                        if p.kind == "merge_split":
                            act.wait_ge(sig["mixed"], p.base["mixed"] + q + 1)
                            act.copy(flat(Mh, q, p.off, p.T), CO[:, s - 1, 0:p.T]).then_inc(sig["high"], 1)
                    if p.kind == "conv_gate":
                        cut(p, r, s, looped)
                        act.wait_ge(bank_free[s], free)
                        act.copy(flat(Yh, t, 0, p.T), CI[:, s, 3:3 + p.T]).then_inc(sig["high"], 1)
                        continue
                    if p.kind == "dt":
                        act.wait_ge(chunk_done[s], done)
                        act.activation(SD[:, 0, :], bank[0][0:16, 0:TOK], ACT.Identity,
                                       bias=SM[0:16, EAL + 2 * p.l:EAL + 2 * p.l + 1]).then_inc(bank_free[0], 1)
                        cut(p, r, s, looped)
                        act.activation(SM[0:16, EA + p.l:EA + p.l + 1], SM[0:16, EAL + 2 * p.l + 1:EAL + 2 * p.l + 2], ACT.Exp)
                        act.wait_ge(bank_free[0], free)
                        softplus(SD[:, 0, :], SD[:, 1, :], SD[:, 2, :], SD[:, 3, :], 2 + p.l)
                        continue
                    if p.kind == "gates":
                        act.wait_ge(chunk_done[s], done)
                        if t >= 2:
                            act.wait_ge(side["gate_m2"], t - 1)
                        for g in range(2):
                            ins = act.activation(S8[:, 4 * (t % 2) + g, 0:SEQ], bank[s][:, g * SEQ:(g + 1) * SEQ],
                                                 ACT.Exp, bias=SM[:, NB + 10 * g + t:NB + 10 * g + t + 1], scale=-1.0)
                        ins.then_inc(bank_free[s], 1)
                        cut(p, r, s, looped)
                        act.wait_ge(side["gate_sig"], t + 1)
                        act.activation(LA[:, t, :], S8[:, 4 * (t % 2), 0:SEQ], ACT.Exp, scale=SM[:, SPL + t:SPL + t + 1])
                        act.activation(S8[:, 4 * (t % 2) + 2, 0:SEQ], S8[:, 4 * (t % 2), 0:SEQ], ACT.Tanh,
                                       scale=SM[:, SPT + t:SPT + t + 1]).then_inc(side["gate_pow"], 1)
                        continue
                    cut(p, r, s, looped)

            def run(name):
                p = by[name]
                rounds(act, p, lambda r, looped: step(p, r, looped))

            def inverse_root(src, dst, scale, ready, no, done):
                act.wait_ge(ready, no)
                own.wait(act.activation(dst, src, ACT.Ln, bias=SM[:, EPSC:EPSC + 1], scale=scale))
                act.activation(dst, dst, ACT.Exp, scale=-0.5).then_inc(done, 1)

            def norm(name, off, n, shift=None):
                i = stat_no[name]
                inverse_root(B[0][:, 0:n], RSTD[:, 0:n], 1.0 / D, sum_done, i + 1, rstd_ready)
                if not norms[i][1]:
                    return
                for k in range(DT8):
                    act.wait_ge(scaled, 8 * split_no[name] + k + 1)
                    if shift is None:
                        act.copy(Hh[:, k, off:off + n], S8[:, k, off:off + n]).then_inc(h_hi, 1)
                    else:
                        act.activation(Hh[:, k, off:off + n], S8[:, k, off:off + n], ACT.Identity,
                                       bias=MOD[:, shift + k:shift + k + 1]).then_inc(h_hi, 1)

            def softplus(z, u, ln, w, no):
                own.wait(act.activation(u, z, ACT.Abs))
                act.activation(u, u, ACT.Exp, scale=-1.0).then_inc(sp_u, 1)
                act.wait_ge(sp_w, no)
                act.activation(ln, w, ACT.Ln).then_inc(sp_ln, 1)

            def attention():
                def exps(h):
                    b = h % 2
                    act.wait_ge(side["att_max"], h + 1)
                    for i, (c, w) in enumerate(((0, P), (P, SEQ))):
                        ins = act.activation(AL[:, b, c:c + w], AL[:, b, c:c + w], ACT.Exp,
                                             bias=SM[:, AMX + 2 * b + i:AMX + 2 * b + i + 1],
                                             accum_out=SM[:, ASM + 2 * b + i:ASM + 2 * b + i + 1])
                    ins.then_inc(side["att_exp"], 1)

                def take_probs(h):
                    act.wait_ge(side["att_t"], h + 1)
                    if h >= 2:
                        act.wait_ge(side["att_o"], h - 1)
                    act.copy(APT[:, h % 2, :], B[2][:, 0:384]).then_inc(side["att_pt"], 1)

                for i in range(10):
                    if i < 8:
                        exps(i)
                    if 1 <= i <= 8:
                        take_probs(i - 1)
                    if i >= 2:
                        act.wait_ge(side["att_o"], i - 1)
                        act.copy(Yh[:, i - 2, META:], B[3][:, 0:SEQ]).then_inc(side["side_hi"], 1)

            def state_space(l):
                for h in range(16):
                    n16 = 16 * l + h
                    b = h % 2
                    act.wait_ge(side["decay_log"], n16 + 1)
                    act.activation(SE[:, b, 0:416], SE[:, b, 0:416], ACT.Exp)
                    act.activation(SE[0:16, b, 416:], SE[0:16, b, 416:], ACT.Exp).then_inc(side["decay_exp"], 1)
                for g in range(4):
                    inverse_root(B[g][:, 0:TOK], YR[:, g, :], 1.0 / 256, side["y_sum"], 8 * l + g + 1, side["y_rstd"])
                halves(16 * l)

            def halves(before):
                for k in range(8):
                    act.wait_ge(side["y32"], before + k + 1)
                    act.copy(Yh[:, k, :], S8[:, k, :]).then_inc(side["side_hi"], 1)

            def retention(l):
                for t in range(8):
                    act.wait_ge(side["ret_y"], 8 * l + t + 1)
                    act.copy(S8[:, t, :], B[2 + t % 2][:, 0:TOK]).then_inc(side["ret_copy"], 1)
                for h in range(4):
                    inverse_root(B[h][:, 0:TOK], YR[:, h, :], 1.0 / 256, side["y_sum"], 8 * l + 4 + h + 1, side["y_rstd"])
                halves(16 * l + 8)

            def stick_breaking(l):
                def soft(h):
                    b, n8 = h % 2, 8 * l + h
                    act.wait_ge(side["sb_s"], n8 + 1)
                    if h >= 2:
                        act.wait_ge(side["sb_logw"], n8 - 1)
                    act.copy(ZS[:, b, :], B[b][:, 0:PACK])
                    act.activation(SA[:, b, :], B[b][:, 0:PACK], ACT.Abs).then_inc(side["sb_z"], 1)
                    act.wait_ge(side["sb_z"], n8 + 1)
                    own.wait(act.activation(SA[:, b, :], SA[:, b, :], ACT.Exp, scale=-1.0))
                    act.activation(SA[:, b, :], SA[:, b, :], ACT.Ln, bias=ONES[:, 0:1]).then_inc(side["sb_soft"], 1)

                for i in range(10):
                    if i < 8:
                        soft(i)
                    if 1 <= i <= 8:
                        act.wait_ge(side["sb_logw"], 8 * l + i)
                        act.activation(SW[:, (i - 1) % 2, :], SW[:, (i - 1) % 2, :], ACT.Exp).then_inc(side["sb_we"], 1)
                    if i >= 2:
                        act.wait_ge(side["sb_o"], 8 * l + i - 1)
                        act.copy(Yh[:, i - 2, :], B[3][:, 0:TOK]).then_inc(side["side_hi"], 1)

            act.wait_ge(loaded["params"], 16)
            act.activation(SM[:, CSC:CSC + 8], PV[:, PCOL["c"]:PCOL["c"] + 8], ACT.Silu).then_inc(silu_c, 1)
            for s in range(SLOTS):
                act.wait_ge(raw_ready[s], 16)
                act.copy(w_hi[:, s, 0:DT8 * P], raw[:, s, 0:DT8 * P]).then_inc(hi_ready[s], 1)
            act.wait_ge(const_ready, 2)
            softplus(SM[:, SPT:SPT + LT], SM[:, SPW:SPW + 10], SM[:, SPW + 20:SPW + 30], SM[:, SPW + 10:SPW + 20], 1)
            norm("mix0", META, SEQ, shift=0)
            run("lru_x")
            run("lru_y")
            run("lru_gates")
            act.wait_ge(side["gate_m2"], LT)
            act.activation(M2[:, :, :], M2[:, :, :], ACT.Sqrt)
            act.activation(CO[:, 0:2, 0:SEQ], CO[:, 0:2, 0:SEQ], ACT.Sqrt).then_inc(side["gate_sqrt"], 1)
            for t in range(LT):
                act.wait_ge(side["lru_y32"], t + 1)
                act.copy(XCh[:, t, 0:SEQ], XC[:, t, :]).then_inc(side["lru_hi"], 1)
            run("lru_out")
            norm("ffn0", META, SEQ, shift=24)
            run("ffn_up0")
            run("ffn_down0")
            norm("kv", META, SEQ, shift=48)
            run("kv_k")
            run("kv_v")
            norm("mix1", META, SEQ, shift=64)
            run("q")
            attention()
            run("attn_out")
            norm("ffn1", META, SEQ, shift=88)
            run("ffn_up1")
            run("ffn_down1")
            norm("final", META, SEQ)
            for l in range(2):
                off, n = (META, SEQ) if l else (0, TOK)
                norm(f"pre{l}", 0, TOK)
                run(f"a_cx{l}")
                run(f"a_b{l}")
                run(f"up_a{l}")
                run(f"dt{l}")
                run(f"s_x{l}")
                run(f"s_bc{l}")
                run(f"s_z{l}")
                state_space(l)
                run(f"up_b{l}")
                run(f"r_v{l}")
                run(f"r_q{l}")
                run(f"r_k{l}")
                run(f"r_g{l}")
                retention(l)
                run(f"up_c{l}")
                run(f"b_v{l}")
                run(f"b_k{l}")
                run(f"b_q{l}")
                stick_breaking(l)
                run(f"up_d{l}")
                run(f"mix_out{l}")
                norm(f"post{l}", off, n)
                norm(f"fpre{l}", off, n)
                run(f"ffn_up{2 + l}")
                run(f"ffn_down{2 + l}")
                norm(f"fpost{l}", off, n)

        @block.vector
        def _(dve):
            own = Own(dve, vec_own)
            tt, ts, stt = dve.tensor_tensor, dve.tensor_scalar, dve.scalar_tensor_tensor

            def cut(p, r, s, looped):
                kb = p.kb if looped else p.next_kb[r, s]
                if kb is None:
                    return
                dve.wait_ge(hi_ready[s], gen(p, r, s) + 2)
                tt(w_lo[:, s, 0:kb * P], raw[:, s, 0:kb * P], w_hi[:, s, 0:kb * P].bitcast(F32), ALU.subtract)\
                    .then_inc(lo_ready[s], 1)

            def low(dst, src, high):
                return tt(dst, src, high.bitcast(F32), ALU.subtract)

            def mod_unit(m, i):
                dve.wait_ge(mod_ready[i], 16 * (m + 1))
                for k in range(8):
                    c = SM[:, CSC + k:CSC + k + 1]
                    if k == 0:
                        ins = ts(ACC[:, i, :], MW[:, i, 0, :], c, None, ALU.mult)
                    else:
                        ins = stt(ACC[:, i, :], MW[:, i, k, :], c, ACC[:, i, :], ALU.mult, ALU.add)
                    if k < 7:
                        own.wait(ins)
                ins.then_inc(mod_acc[i], 1)

            def mod_take(m, i):
                dve.wait_ge(mod_sum, 2 * m + i + 1)
                c = (2 * m + i) * 2
                if isinstance(c, int):
                    dst, b = MOD[:, c:c + 2], PV[:, PCOL["mod_b"] + c:PCOL["mod_b"] + c + 2]
                else:
                    dst, b = MOD[:, bass.ds(c, 2)], PV[:, bass.ds(PCOL["mod_b"] + c, 2)]
                return tt(dst, B[2 + i][:, 0:2], b, ALU.add)

            resid_gate = {"lru_out": 16, "ffn_down0": 40, "attn_out": 80, "ffn_down1": 104}

            def step(p, r, looped):
                n = SLOTS if looped else p.slots(r)
                if p.mods is not None:
                    for i in range(2):
                        mod_unit(p.mods // 2 + r, i)
                for s in range(n):
                    done = gen(p, r, s) + 1
                    t = r * SLOTS + s
                    T = p.T
                    if p.kind in ("conv_split", "conv_silu"):
                        tt_ = t + p.t0
                        names = ("lru_conv_w", "lru_conv_b", LT) if p.kind == "conv_split" else ("ssd_conv_w", "ssd_conv_b", 16)
                        w0, b0 = PCOL[names[0]] + 4 * names[2] * p.l, PCOL[names[1]] + names[2] * p.l
                        dve.wait_ge(bank_free[s], p.bank[s] + r + 1)
                        own.wait(ts(CO[:, s, 0:T], CI[:, s, 0:T], col(PV, w0 + tt_), col(PV, b0 + tt_), ALU.mult, ALU.add))
                        for j in range(1, 4):
                            dst = flat(XC, t, 0, T) if p.kind == "conv_split" and j == 3 else CO[:, s, 0:T]
                            ins = stt(dst, CI[:, s, j:j + T], col(PV, w0 + names[2] * j + tt_), CO[:, s, 0:T],
                                      ALU.mult, ALU.add)
                            if j < 3:
                                own.wait(ins)
                        ins.then_inc(sig["mixed"], 1)
                        cut(p, r, s, looped)
                        dve.wait_ge(sig["high"], p.base["high"] + t + 1)
                        if p.kind == "conv_split":
                            low(flat(XCl, t, 0, T), flat(XC, t, 0, T), flat(XCh, t, 0, T)).then_inc(sig["low"], 1)
                        continue
                    if p.kind == "vtok":
                        cut(p, r, s, looped)
                        if s:
                            take_values(p, t - 1, s - 1)
                        if s == n - 1:
                            take_values(p, t, s)
                        continue
                    if p.kind == "resid":
                        if p.per == 2:
                            t = r * 2 + s // 2
                        if p.per == 1 or s % 2:
                            dve.wait_ge(chunk_done[s], done)
                            x = flat(X, t, META, SEQ)
                            stt(x, bank[s][:, 0:SEQ], col(MOD, resid_gate[p.name] + t), x, ALU.mult, ALU.add)\
                                .then_inc(bank_free[s], 1)
                    q = r * 2 + s // 2
                    if p.kind in ("glu", "cx", "merge", "merge_split") and s % 2:
                        dve.wait_ge(chunk_done[s], done)
                        dve.wait_ge(bank_free[s - 1], p.bank[s - 1] + r + 1)
                        f = CI[:, s - 1, 3:3 + T]
                        if p.kind == "cx":
                            dst = U[:, q, 2:2 + T] if isinstance(q, int) else flat(U, q, 2, T)
                        elif p.name in ("up_a0", "up_a1"):
                            dst = flat(M, q, p.off, T)
                        else:
                            dst = CO[:, s - 1, 0:T]
                        tt(dst, f, bank[s][:, 0:T], ALU.mult).then_inc(bank_free[s], 1)
                        if p.kind in ("merge", "merge_split") and not p.name.startswith("up_a"):
                            dve.wait_ge(bank_free[s], p.bank[s] + r + 1)
                            m = flat(M, q, p.off, T)
                            if p.kind == "merge":
                                tt(m, m, dst, ALU.add)
                            else:
                                tt(dst, m, dst, ALU.add).then_inc(sig["mixed"], 1)
                    if p.kind == "conv_gate":
                        w0 = PCOL["conv_a"] + 24 * p.l
                        own.wait(ts(CO[:, s, 0:T], flat(U, t, 0, T), col(PV, w0 + t), None, ALU.mult))
                        for j in (1, 2):
                            own.wait(stt(CO[:, s, 0:T], flat(U, t, j, T), col(PV, w0 + 8 * j + t), CO[:, s, 0:T],
                                         ALU.mult, ALU.add))
                        dve.wait_ge(chunk_done[s], done)
                        tt(CI[:, s, 3:3 + T], CO[:, s, 0:T], bank[s][:, 0:T], ALU.mult).then_inc(bank_free[s], 1)
                        cut(p, r, s, looped)
                        dve.wait_ge(sig["high"], p.base["high"] + t + 1)
                        low(flat(Yl, t, 0, T), CI[:, s, 3:3 + T], flat(Yh, t, 0, T)).then_inc(sig["low"], 1)
                        continue
                    if p.kind == "rotate" and s % 2:
                        e = s - 1
                        dve.wait_ge(chunk_done[e], done)
                        dve.wait_ge(chunk_done[s], done)
                        p1, p2 = bank[e][:, 0:T], bank[s][:, 0:T]
                        t1, t2, t3, t4 = CO[:, e, 0:T], CO[:, s, 0:T], CI[:, e, 3:3 + T], CI[:, s, 3:3 + T]
                        tt(t1, p1, cos, ALU.mult)
                        tt(t3, p1, sin, ALU.mult).then_inc(bank_free[e], 1)
                        tt(t2, p2, sin, ALU.mult)
                        tt(t4, p2, cos, ALU.mult).then_inc(bank_free[s], 1)
                        dve.wait_ge(bank_free[s], p.bank[s] + r + 1)
                        dst = RQ if p.name.startswith("r_q") else RK
                        tt(flat(dst, 2 * q, 0, T), t1, t2, ALU.subtract)
                        tt(flat(dst, 2 * q + 1, 0, T), t3, t4, ALU.add).then_inc(sig["mixed"], 1)
                    if p.kind == "gates":
                        g = S8[:, 4 * (t % 2):4 * (t % 2) + 2, 0:SEQ]
                        pw, qq = S8[:, 4 * (t % 2) + 2, 0:SEQ], S8[:, 4 * (t % 2) + 3, 0:SEQ]
                        dve.wait_ge(bank_free[s], p.bank[s] + r + 1)
                        own.wait(ts(g, g, 1.0, None, ALU.add))
                        dve.reciprocal(g, g).then_inc(side["gate_sig"], 1)
                        cut(p, r, s, looped)
                        dve.wait_ge(side["gate_sig"], t + 1)
                        tt(XC[:, t, :], XC[:, t, :], S8[:, 4 * (t % 2) + 1, 0:SEQ], ALU.mult)
                        dve.wait_ge(side["gate_pow"], t + 1)
                        own.wait(ts(qq, pw, 1.0, None, ALU.add))
                        own.wait(dve.reciprocal(qq, qq))
                        dst = M2[:, t, :] if t < 8 else CO[:, t - 8, 0:SEQ]
                        stt(dst, pw, 2.0, qq, ALU.mult, ALU.mult).then_inc(side["gate_m2"], 1)
                        continue
                    if p.kind == "dt":
                        cut(p, r, s, looped)
                        continue
                    cut(p, r, s, looped)
                    if p.kind in ("glu", "merge_split") and s % 2:
                        dve.wait_ge(sig["high"], p.base["high"] + q + 1)
                        h, l_ = (Fh, Fl) if p.kind == "glu" else (Mh, Ml)
                        low(flat(l_, q, p.off, T), CO[:, s - 1, 0:T], flat(h, q, p.off, T)).then_inc(sig["low"], 1)
                if p.mods is not None:
                    for i in range(2):
                        mod_take(p.mods // 2 + r, i)

            def take_values(p, t, s):
                dve.wait_ge(sig["turned"], p.base["turned"] + t + 1)
                V = AV if p.name == "kv_v" else RV if p.name.startswith("r_v") else BV
                b = B[s % 2]
                if isinstance(t, int):
                    cols = slice(t * P, (t + 1) * P)
                else:
                    cols = bass.ds(t * P, P)
                if p.T == TOK:
                    dve.tensor_copy(V[0:16, 2, cols], b[0:16, 2 * P:3 * P])
                dve.tensor_copy(V[:, 0:2, cols], b[:, 0:2 * P].rearrange("p (a n) -> p a n", a=2)).then_inc(sig["copied"], 1)

            def run(name):
                p = by[name]
                per = OWN_WAITS.get(p.kind, 0) * SLOTS
                rounds(dve, p, lambda r, looped: step(p, r, looped), own, per + (14 if p.mods is not None else 0))

            def norm(name, off, n, src, g, shift=None, scale=None):
                i = stat_no[name]
                for hf in range(2):
                    x = src[:, 4 * hf:4 * hf + 4, off:off + n]
                    tt(S8[:, 4 * hf:4 * hf + 4, off:off + n], x, x, ALU.mult).then_inc(squares, 1)
                if scale is not None:
                    own.wait(stt(SM[:, GS:GS + 8], MOD[:, scale:scale + 8], 1.0, PV[:, g:g + 8], ALU.add, ALU.mult))
                dve.wait_ge(rstd_ready, i + 1)
                for k in range(DT8):
                    w = PV[:, g + k:g + k + 1] if scale is None else SM[:, GS + k:GS + k + 1]
                    dst = src if name == "final" else S8
                    ins = stt(dst[:, k, off:off + n], src[:, k, off:off + n], w, RSTD[:, 0:n], ALU.mult, ALU.mult)
                    if norms[i][1]:
                        ins.then_inc(scaled, 1)
                        if k:
                            low_h(name, k - 1, off, n, shift)
                if norms[i][1]:
                    low_h(name, DT8 - 1, off, n, shift)
                elif name == "final":
                    own.wait(ins)
                else:
                    own.wait(ins)
                    x = X[:, :, off:off + n]
                    last = tt(x, x, S8[:, :, off:off + n], ALU.add)
                    if name == "fpost1":
                        last.then_inc(finished, 1)
                    else:
                        own.wait(last)

            def low_h(name, k, off, n, shift):
                dve.wait_ge(h_hi, 8 * split_no[name] + k + 1)
                h = Hh[:, k, off:off + n].bitcast(F32)
                if shift is None:
                    ins = tt(Hl[:, k, off:off + n], S8[:, k, off:off + n], h, ALU.subtract)
                else:
                    ins = stt(Hl[:, k, off:off + n], S8[:, k, off:off + n], MOD[:, shift + k:shift + k + 1], h,
                              ALU.add, ALU.subtract)
                ins.then_inc(h_lo, 1)

            def taken(name):
                for s in range(SLOTS):
                    dve.wait_ge(bank_free[s], by[name].bank_end[s])

            def softplus(z, u, ln, w, d, tmp, dst, no):
                dve.wait_ge(sp_u, no)
                ts(w, u, 1.0, None, ALU.add).then_inc(sp_w, 1)
                dve.wait_ge(sp_w, no)
                own.wait(ts(d, w, -1.0, None, ALU.add))
                own.wait(ts(tmp, d, 1e-30, None, ALU.max))
                own.wait(dve.reciprocal(tmp, tmp))
                own.wait(tt(tmp, tmp, u, ALU.mult))
                dve.wait_ge(sp_ln, no)
                own.wait(tt(tmp, tmp, ln, ALU.mult))
                own.wait(stt(d, d, 0.0, u, ALU.is_equal, ALU.mult))
                own.wait(tt(tmp, tmp, d, ALU.add))
                own.wait(stt(dst, z, 0.0, tmp, ALU.max, ALU.add))

            def recurrence():
                dve.wait_ge(side["gate_sqrt"], 1)
                for s in range(SLOTS):
                    dve.wait_ge(bank_free[s], by["lru_y"].bank_end[s])
                for t in range(LT):
                    m = M2[:, t, :] if t < 8 else CO[:, t - 8, 0:SEQ]
                    own.wait(tt(XC[:, t, :], XC[:, t, :], m, ALU.mult))
                    own.wait(dve.tensor_tensor_scan(S8[:, t % 8, 0:SEQ], LA[:, t, :], XC[:, t, :], 0.0, ALU.mult, ALU.add))
                    tt(XC[:, t, :], S8[:, t % 8, 0:SEQ], YB[:, t, :], ALU.mult).then_inc(side["lru_y32"], 1)
                    if t:
                        low_y(t - 1)
                low_y(LT - 1)

            def low_y(t):
                dve.wait_ge(side["lru_hi"], t + 1)
                low(XCl[:, t, 0:SEQ], XC[:, t, :], XCh[:, t, 0:SEQ]).then_inc(side["lru_lo"], 1)

            def attention():
                dve.wait_ge(loaded["bias"], 16)

                def logits(h):
                    b = h % 2
                    dve.wait_ge(side["att_s"], h + 1)
                    if h >= 2:
                        dve.wait_ge(side["att_t"], h - 1)
                    stt(AL[:, b, 0:P], B[b][:, 0:P], P ** -0.5, BT[:, h, P:SEQ], ALU.mult, ALU.add)
                    own.wait(stt(AL[:, b, P:], B[b][:, P:384], P ** -0.5, BT[:, h, :], ALU.mult, ALU.add))
                    m = SM[:, AMX + 2 * b:AMX + 2 * b + 2]
                    dve.tensor_reduce(m[:, 0:1], AL[:, b, 0:P], AX.X, ALU.max)
                    own.wait(dve.tensor_reduce(m[:, 1:2], AL[:, b, P:], AX.X, ALU.max))
                    ts(m, m, -1.0, None, ALU.mult).then_inc(side["att_max"], 1)

                def probs(h):
                    b = h % 2
                    dve.wait_ge(side["att_exp"], h + 1)
                    sm = SM[:, ASM + 2 * b:ASM + 2 * b + 2]
                    own.wait(dve.reciprocal(sm, sm))
                    ts(AL[:, b, 0:P], AL[:, b, 0:P], sm[:, 0:1], None, ALU.mult)
                    ts(AL[:, b, P:], AL[:, b, P:], sm[:, 1:2], None, ALU.mult).then_inc(side["att_p"], 1)

                for i in range(10):
                    if i < 8:
                        logits(i)
                    if 1 <= i <= 8:
                        probs(i - 1)
                    if i >= 2:
                        h = i - 2
                        dve.wait_ge(side["side_hi"], h + 1)
                        low(Yl[:, h, META:], B[3][:, 0:SEQ], Yh[:, h, META:]).then_inc(side["side_lo"], 1)

            def step_sizes(l):
                softplus(SD[:, 0, :], SD[:, 1, :], SD[:, 2, :], SD[:, 3, :], SD[:, 4, :], SD[:, 5, :], SD[:, 6, :], 2 + l)
                own.wait(ts(SD[:, 5, :], SD[:, 6, :], SM[0:16, EA + l:EA + l + 1], -1.0, ALU.mult, ALU.mult))
                dve.tensor_tensor_scan(ACS[:, :], ONES[0:16, 0:1].to_broadcast([16, TOK]), SD[:, 5, :], 0.0,
                                       ALU.mult, ALU.add).then_inc(side["dt_acs"], 1)

            def state_space(l):
                dve.wait_ge(side["dt_turned"], l + 1)
                dve.tensor_copy(SM[:, DTT:DTT + 32], B[0][:, 0:32])
                dve.tensor_copy(SM[0:16, DTT + 32:DTT + 48], B[0][0:16, 32:48])
                ts(SM[:, NAT:NAT + 32], B[0][:, 48:80], -1.0, None, ALU.mult)
                ts(SM[0:16, NAT + 32:NAT + 48], B[0][0:16, 80:96], -1.0, None, ALU.mult).then_inc(side["dt_cols"], 1)
                dve.wait_ge(side["dt_cols"], l + 1)
                for m in range(6):
                    n, half = m // 2, m % 2
                    w = KEYS[n][1]
                    dve.wait_ge(side["x_turned"], 6 * l + m + 1)
                    step_size = SM[0:w, DTT + 16 * n + 8 * half:DTT + 16 * n + 8 * half + 8]
                    tt(XT[0:w, n, 512 * half:512 * half + 512].rearrange("p (h d) -> p h d", d=64),
                       B[1 + m % 3][0:w, :].rearrange("p (h d) -> p h d", d=64),
                       step_size.unsqueeze(2).to_broadcast([w, 8, 64]), ALU.mult).then_inc(side["x_scaled"], 1)
                for g in range(4):
                    dve.wait_ge(side["cb_done"], 4 * l + g + 1)
                    tt(CB[:, g, :], B[g][:, 0:PACK], incl, ALU.mult).then_inc(side["cb_masked"], 1)
                dve.wait_ge(side["cb_masked"], 4 * l + 4)

                def take(j):
                    dve.wait_ge(side["head_y"], 16 * l + 2 * j + 2)
                    c = PCOL["ssd_d"] + 8 * l + j
                    stt(S8[:, j, :], XS[:, j, :], PV[:, c:c + 1], B[2 + j % 2][:, 0:TOK], ALU.mult, ALU.add)\
                        .then_inc(side["y_taken"], 1)

                def log_decay(h):
                    b, n16 = h % 2, 16 * l + h
                    dve.wait_ge(side["acs_rows"], n16 + 1)
                    for n, (c, q0, w) in enumerate(SEG):
                        k, c0 = KEYS[n][1], NAT + 16 * n + h
                        ins = ts(SE[0:k, b, c:c + w], B[b][0:k, q0:q0 + w], SM[0:k, c0:c0 + 1], 0.0, ALU.add, ALU.min)
                    ins.then_inc(side["decay_log"], 1)

                def mix(h):
                    b, n16 = h % 2, 16 * l + h
                    dve.wait_ge(side["decay_exp"], n16 + 1)
                    if h >= 2:
                        dve.wait_ge(side["head_y"], n16 - 1)
                    tt(SX[:, b, 0:416], SE[:, b, 0:416], CB[:, h // 4, 0:416], ALU.mult)
                    tt(SX[0:16, b, 416:], SE[0:16, b, 416:], CB[0:16, h // 4, 416:], ALU.mult).then_inc(side["decay_mix"], 1)

                for i in range(17):
                    if i < 16:
                        log_decay(i)
                    if i:
                        mix(i - 1)
                    if i >= 3 and i % 2:
                        take((i - 3) // 2)
                take(7)
                taken(f"s_z{l}")
                dve.wait_ge(side["y_taken"], 8 * l + 8)
                for g in range(4):
                    y = S8[:, 2 * g:2 * g + 2, :]
                    own.wait(tt(y, y, Z[:, 2 * g:2 * g + 2, :], ALU.mult))
                    tt(YQ[:, 2 * g:2 * g + 2, :], y, y, ALU.mult).then_inc(side["y_sq"], 1)
                for g in range(4):
                    dve.wait_ge(side["y_rstd"], 8 * l + g + 1)
                    for t in (2 * g, 2 * g + 1):
                        c = PCOL["ssd_norm"] + 8 * l + t
                        stt(S8[:, t, :], S8[:, t, :], PV[:, c:c + 1], YR[:, g, :], ALU.mult, ALU.mult)\
                            .then_inc(side["y32"], 1)
                        if t:
                            low_side(8 + 24 * l, t - 1)
                low_side(8 + 24 * l, 7)

            def low_side(before, t):
                dve.wait_ge(side["side_hi"], before + t + 1)
                low(Yl[:, t, :], S8[:, t, :], Yh[:, t, :]).then_inc(side["side_lo"], 1)

            def retention(l):
                for h in range(4):
                    dve.wait_ge(side["ret_s"], 4 * l + h + 1)
                    if h >= 2:
                        dve.wait_ge(side["ret_y"], 8 * l + 2 * (h - 1))
                    c = CCOL["decay"] + h * PACK
                    tt(RP[:, h % 2, :], B[h % 2][:, 0:PACK], CS[:, c:c + PACK], ALU.mult).then_inc(side["ret_p"], 1)
                for h in range(4):
                    dve.wait_ge(side["ret_mean"], 4 * l + h + 1)
                    for t in (2 * h, 2 * h + 1):
                        ins = stt(S8[:, t, :], B[h][:, 0:TOK], -1.0 / 256, S8[:, t, :], ALU.mult, ALU.add)
                    own.wait(ins)
                    y = S8[:, 2 * h:2 * h + 2, :]
                    tt(YQ[:, 2 * h:2 * h + 2, :], y, y, ALU.mult).then_inc(side["y_sq"], 1)
                taken(f"r_g{l}")
                dve.wait_ge(side["y_sq"], 8 * l + 8)
                own.wait(tt(S8[:, :, :], S8[:, :, :], RG[:, :, :], ALU.mult))
                for h in range(4):
                    dve.wait_ge(side["y_rstd"], 8 * l + 4 + h + 1)
                    for t in (2 * h, 2 * h + 1):
                        tt(S8[:, t, :], S8[:, t, :], YR[:, h, :], ALU.mult).then_inc(side["y32"], 1)
                        if t:
                            low_side(16 + 24 * l, t - 1)
                low_side(16 + 24 * l, 7)

            def stick_breaking(l):
                for i in range(10):
                    n8 = 8 * l + i
                    if i < 8:
                        b = i % 2
                        dve.wait_ge(side["sb_soft"], n8 + 1)
                        if i >= 2:
                            dve.wait_ge(side["sb_r"], n8 - 1)
                        own.wait(stt(SS[:, b, :], ZS[:, b, :], 0.0, SA[:, b, :], ALU.max, ALU.add))
                        tt(SS[:, b, :], SS[:, b, :], strict, ALU.mult).then_inc(side["sb_sp"], 1)
                    if 1 <= i <= 8:
                        b = (i - 1) % 2
                        dve.wait_ge(side["sb_r"], n8)
                        if i >= 3:
                            dve.wait_ge(side["sb_o"], n8 - 2)
                        own.wait(tt(SW[:, b, :], ZS[:, b, :], B[2][:, 0:PACK], ALU.subtract))
                        ts(SW[:, b, :], SW[:, b, :], 0.0, None, ALU.min).then_inc(side["sb_logw"], 1)
                        dve.wait_ge(side["sb_we"], n8)
                        tt(SW[:, b, :], SW[:, b, :], strict, ALU.mult).then_inc(side["sb_w"], 1)
                    if i >= 2:
                        h = i - 2
                        dve.wait_ge(side["side_hi"], 24 + 24 * l + h + 1)
                        low(Yl[:, h, :], B[3][:, 0:TOK], Yh[:, h, :]).then_inc(side["side_lo"], 1)

            dve.memset(ONES[:, :], 1.0)
            dve.memset(CI[:, :, 0:3], 0.0)
            dve.memset(SM[:, EPSC:EPSC + 1], EPS).then_inc(sig["copied"], 2)
            dve.wait_ge(sig["copied"], 2)
            dve.memset(SM[:, EPSC + 1:EPSC + 2], 0.0).then_inc(const_ready, 1)
            dve.wait_ge(loaded["params"], 16)
            c = PCOL["lru_b_gates"]
            ts(SM[:, NB:NB + 20], PV[:, c:c + 20], -1.0, None, ALU.mult)
            c = PCOL["lru_lambda"]
            ts(SM[:, SPT:SPT + LT], PV[:, c:c + LT], -1.0, None, ALU.mult).then_inc(const_ready, 1)
            dve.wait_ge(side["bias_sum"], 1)
            own.wait(dve.tensor_copy(BR[:, :], B[1][0:8, 0:BIASW]))
            dve.memset(BR[:, SEQ:], -1e30).then_inc(side["bias_row"], 1)
            dve.wait_ge(silu_c, 1)
            for m in range(4):
                for i in range(2):
                    mod_unit(m, i)
                for i in range(2):
                    last = mod_take(m, i)
            own.wait(last)
            for s in range(SLOTS):
                dve.wait_ge(hi_ready[s], 1)
                low(w_lo[:, s, 0:DT8 * P], raw[:, s, 0:DT8 * P], w_hi[:, s, 0:DT8 * P]).then_inc(lo_ready[s], 1)
            sp = SM[:, SPW + 30:SPW + 40]
            softplus(SM[:, SPT:SPT + LT], SM[:, SPW:SPW + 10], SM[:, SPW + 20:SPW + 30], SM[:, SPW + 10:SPW + 20],
                     sp, SM[:, DTT:DTT + LT], SM[:, DTT + 16:DTT + 16 + LT], 1)
            ts(SM[:, SPL:SPL + LT], SM[:, DTT + 16:DTT + 16 + LT], -8.0, None, ALU.mult)
            own.wait(ts(SM[:, SPT:SPT + LT], SM[:, DTT + 16:DTT + 16 + LT], 8.0, None, ALU.mult))
            dve.wait_ge(loaded["x"], 16)
            norm("mix0", META, SEQ, X, PCOL["norm_mix"], 0, 8)
            run("lru_x")
            run("lru_y")
            run("lru_gates")
            recurrence()
            run("lru_out")
            taken("lru_out")
            norm("ffn0", META, SEQ, X, PCOL["norm_ffn"], 24, 32)
            run("ffn_up0")
            run("ffn_down0")
            taken("ffn_down0")
            norm("kv", META, SEQ, X, PCOL["kv_norm"], 48, 56)
            run("kv_k")
            run("kv_v")
            norm("mix1", META, SEQ, X, PCOL["norm_mix"] + 8, 64, 72)
            run("q")
            attention()
            run("attn_out")
            taken("attn_out")
            norm("ffn1", META, SEQ, X, PCOL["norm_ffn"] + 8, 88, 96)
            run("ffn_up1")
            run("ffn_down1")
            taken("ffn_down1")
            norm("final", META, SEQ, X, PCOL["final_norm"])
            dve.wait_ge(loaded["meta"], 16)
            dve.wait_ge(loaded["heads"], 16)
            for l in range(2):
                off, n = (META, SEQ) if l else (0, TOK)
                norm(f"pre{l}", 0, TOK, X, PCOL["norm_mix_pre"] + 8 * l)
                dve.memset(U[:, :, 0:2], 0.0)
                run(f"a_cx{l}")
                for s in range(SLOTS):
                    dve.wait_ge(bank_free[s], by[f"a_cx{l}"].bank_end[s])
                run(f"a_b{l}")
                run(f"up_a{l}")
                run(f"dt{l}")
                step_sizes(l)
                dve.memset(BC[:, 0:4, TOK:], 0.0)
                run(f"s_x{l}")
                run(f"s_bc{l}")
                run(f"s_z{l}")
                state_space(l)
                run(f"up_b{l}")
                dve.memset(RK[:, :, TOK:], 0.0)
                run(f"r_v{l}")
                run(f"r_q{l}")
                run(f"r_k{l}")
                run(f"r_g{l}")
                retention(l)
                run(f"up_c{l}")
                dve.memset(BK[:, :, TOK:], 0.0)
                run(f"b_v{l}")
                run(f"b_k{l}")
                run(f"b_q{l}")
                stick_breaking(l)
                run(f"up_d{l}")
                run(f"mix_out{l}")
                taken(f"mix_out{l}")
                norm(f"post{l}", off, n, M, PCOL["norm_mix_post"] + 8 * l)
                norm(f"fpre{l}", off, n, X, PCOL["norm_ffn_pre"] + 8 * l)
                run(f"ffn_up{2 + l}")
                run(f"ffn_down{2 + l}")
                taken(f"ffn_down{2 + l}")
                norm(f"fpost{l}", off, n, M, PCOL["norm_ffn_post"] + 8 * l)


def chunks(w, kb=8):
    k, m = w.shape
    w = w.reshape(k // (kb * P), kb, P, m // P, P)
    return w.transpose(3, 0, 2, 1, 4).reshape(-1, P, kb * P)


def pairs(u, v):
    return np.stack([u, v], axis=1).reshape(-1, *u.shape[1:])


def constants():
    cs = np.zeros((P, CCOLS), np.float32)
    cs[:, CCOL["ident"]:CCOL["ident"] + P] = np.eye(P)
    cs[:, CCOL["suffix"]:CCOL["suffix"] + P] = np.tril(np.ones((P, P)))
    gamma = np.log(1.0 - 2.0 ** (-5.0 - np.arange(4, dtype=np.float64)))
    for (c, q0, w), (k0, kn) in zip(SEG, KEYS):
        key, query = k0 + np.arange(kn)[:, None], q0 + np.arange(w)[None, :]
        cs[:kn, CCOL["incl"] + c:CCOL["incl"] + c + w] = key <= query
        cs[:kn, CCOL["strict"] + c:CCOL["strict"] + c + w] = key < query
        for h in range(4):
            at = CCOL["decay"] + h * PACK + c
            cs[:kn, at:at + w] = np.where(key <= query, np.exp(gamma[h] * np.maximum(query - key, 0)), 0) / 16
    pos = np.arange(P - META, P + SEQ).astype(np.float32)
    inv = np.float32(10000.0) ** (-np.arange(P, dtype=np.float32) / np.float32(P))
    ang = (pos[None, :] * inv[:, None]).astype(np.float32)
    cs[:, CCOL["cos"]:CCOL["cos"] + TOK] = np.cos(ang)
    cs[:, CCOL["sin"]:CCOL["sin"] + TOK] = np.sin(ang)
    dist = SEQ - 1 - np.arange(BIASW)
    d = np.maximum(dist, 1).astype(np.float32)
    large = 16 + (np.log(d / np.float32(16)) / np.float32(np.log(128 / 16)) * np.float32(16)).astype(np.int32)
    bucket = np.where(dist < 16, dist, np.minimum(large, 31))
    onehot = (np.arange(32)[:, None] == bucket[None, :]) & (dist >= 0)[None, :]
    return cs, onehot.astype(np.float32)


def columns(v):
    return v.reshape(-1, P).T


def layout(i):
    f = {n: np.asarray(v) for n, v in i.items()}
    a = {}
    a["x"] = f["x"][0].reshape(SEQ, DT8, P).transpose(2, 1, 0)
    a["meta"] = f["meta_2"].reshape(META, DT8, P).transpose(2, 1, 0)
    a["consts"], a["onehot"] = constants()
    a["rel_bias"] = f["rel_bias"].T
    a["heads"] = np.stack([f["ssd_dt_bias_2"][0], f["ssd_a_log_2"][0], f["ssd_dt_bias_2"][1], f["ssd_a_log_2"][1]], axis=1)
    mod = np.concatenate([f["mod_w"][0], f["kv_mod_w"], f["mod_w"][1]], axis=1)
    a["mod_w"] = mod.reshape(8, P, MOD_UNITS, MU).transpose(2, 1, 0, 3)
    src = {"c": f["c"], "mod_b": np.concatenate([f["mod_b"][0], f["kv_mod_b"], f["mod_b"][1]]),
           "ssd_d": np.repeat(f["ssd_d_2"], 64, axis=1), "lru_conv_w": f["lru_conv_w"][0], "lru_conv_b": f["lru_conv_b"],
           "lru_b_gates": f["lru_b_gates"][0], "lru_lambda": f["lru_lambda"]}
    cols = []
    for name, w in PARAMS:
        v = src[name] if name in src else f[name] if name in f else f[name + "_2"]
        v = columns(v)
        assert v.shape == (P, w), (name, v.shape)
        cols.append(v)
    a["params"] = np.concatenate(cols, axis=1)
    w = chunks(f["lru_w_in"][0])
    a["lru_y"], a["lru_x"] = w[:LT], w[LT:]
    g = f["lru_w_gates"][0].reshape(5, 2, P, 2, 2, P)
    a["lru_gates"] = g.transpose(0, 4, 2, 3, 1, 5).reshape(LT, P, 4 * P)
    a["lru_out"] = chunks(f["lru_w_out"][0], 10)
    kv = chunks(f["w_kv"])
    a["kv_k"], a["kv_v"] = kv[:4], kv[4:]
    a["q"], a["attn_out"] = chunks(f["attn_w_q"][0]), chunks(f["attn_w_o"][0])
    for l in range(2):
        a[f"ffn_up{l}"] = pairs(chunks(f["ffn_w_gate"][l]), chunks(f["ffn_w_up"][l]))
        a[f"ffn_down{l}"] = chunks(f["ffn_w_down"][l], 11)
    for l in range(2):
        w, at = f["w_in_2"][l], [0]

        def take(n):
            at[0] += n
            return w[:, at[0] - n:at[0]]

        b, c, x, z, xs, bc, dt = (take(n) for n in (D, D, D, D, D, D, 16))
        rq, rk, rv, rg, bq, bk, bv, gates = (take(n) for n in (D,) * 7 + (4 * D,))
        a[f"a_cx{l}"], a[f"a_b{l}"] = pairs(chunks(c), chunks(x)), chunks(b)
        a[f"dt{l}"] = chunks(np.concatenate([dt, np.zeros((D, P - 16), dt.dtype)], axis=1))
        for n, v in (("s_x", xs), ("s_bc", bc), ("s_z", z), ("r_v", rv), ("r_q", rq), ("r_k", rk), ("r_g", rg),
                     ("b_v", bv), ("b_k", bk), ("b_q", bq)):
            a[n + str(l)] = chunks(v)
        for j, n in enumerate("abcd"):
            a[f"up_{n}{l}"] = pairs(chunks(gates[:, j * D:(j + 1) * D]), chunks(f["w_branch_2"][l, j]))
        a[f"mix_out{l}"] = chunks(f["w_out_2"][l])
        up = f["w_ffn_in_2"][l]
        a[f"ffn_up{2 + l}"] = pairs(chunks(up[:, :FF]), chunks(up[:, FF:]))
        a[f"ffn_down{2 + l}"] = chunks(f["w_ffn_out_2"][l], 11)
    return {n: np.ascontiguousarray(v) for n, v in a.items()}


def kernel(**inputs):
    import concourse.bacc as bacc
    from concourse.bass_utils import run_bass_kernel_spmd

    nc = bacc.Bacc("TRN2", target_bir_lowering=False, num_devices=1)
    arrays, aps = {}, {}
    for name, v in layout(inputs).items():
        arrays["in_" + name] = v
        aps[name] = nc.dram_tensor("in_" + name, v.shape, mybir.dt.from_np(v.dtype), kind="ExternalInput").ap()
    out = nc.dram_tensor("out", (P, DT8, SEQ), F32, kind="ExternalOutput").ap()
    two_layer_pair(nc, aps, out)
    r = run_bass_kernel_spmd(nc, [arrays], core_ids=[0])
    return r.results[0]["out"].transpose(2, 1, 0).reshape(1, SEQ, D)
```

```python
from contextlib import ExitStack

import numpy as np
import concourse.bass as bass
from concourse import mybir

F32 = mybir.dt.float32
F32R = mybir.dt.float32r
ALU = mybir.AluOpType
ACT = mybir.ActivationFunctionType
AX = mybir.AxisListType

P = 128
D = 1024
SEQ = 256
META = 16
TOK = META + SEQ
DT8 = D // P
LRU = 1280
LT = LRU // P
FF = 2816
FT = FF // P
EPS = 1e-6
SLOTS = 4
KEYS = ((0, 128), (128, 128), (256, 16))
SEG = ((0, 0, 272), (272, 128, 144), (416, 256, 16))
PACK = 432

MU = 256
MOD_SECTIONS = 14
MOD_UNITS = MOD_SECTIONS * D // MU
FIRST = 2 * D // MU

PARAMS = [("c", 8), ("mod_b", 112), ("norm_mix", 16), ("norm_ffn", 16), ("kv_norm", 8), ("final_norm", 8),
          ("lru_conv_w", 40), ("lru_conv_b", 10), ("lru_b_gates", 20), ("lru_lambda", 10),
          ("norm_mix_pre", 16), ("norm_mix_post", 16), ("norm_ffn_pre", 16), ("norm_ffn_post", 16),
          ("conv_a", 48), ("ssd_conv_w", 128), ("ssd_conv_b", 32), ("ssd_norm", 16), ("ssd_d", 16)]
PCOL, _n = {}, 0
for _name, _w in PARAMS:
    PCOL[_name] = _n
    _n += _w
PCOLS = _n

CONSTS = [("ident", 128), ("suffix", 128), ("incl", PACK), ("strict", PACK), ("decay", 4 * PACK),
          ("cos", TOK), ("sin", TOK)]
CCOL, _n = {}, 0
for _name, _w in CONSTS:
    CCOL[_name] = _n
    _n += _w
CCOLS = _n
BIASW = 384


class Phase:

    def __init__(self, name, kind, n, rhs="H", kb=8, off=0, T=TOK, per=1, l=0, mods=None, t0=0, norm=None):
        self.name, self.kind, self.n, self.kb, self.rhs = name, kind, n, kb, rhs
        self.off, self.T, self.per, self.l, self.mods, self.t0, self.norm = off, T, per, l, mods, t0, norm
        self.rounds = -(-n // SLOTS)
        pair = kind in ("glu", "cx", "merge", "merge_split", "rotate")
        self.units = n // 2 if pair else n // per
        self.count = {s: self.units for s in SIGNALS.get(kind, ())}

    def has_mods(self, r):
        return self.mods is not None and (not isinstance(r, int) or self.mods + 2 * r < MOD_UNITS)

    def slots(self, r):
        return min(SLOTS, self.n - SLOTS * r)


SIGNALS = {"conv_split": ("mixed", "high", "low"), "conv_silu": ("mixed", "high"), "vtok": ("turned", "copied"),
           "glu": ("high", "low"), "conv_gate": ("high", "low"), "merge_split": ("mixed", "high", "low"),
           "rotate": ("mixed",)}
OWN_WAITS = {"conv_split": 3, "conv_silu": 3, "conv_gate": 3}


def plan():
    seq = dict(off=META, T=SEQ)
    ph = [Phase("lru_x", "conv_split", 10, mods=8, **seq), Phase("lru_gates", "gates", 10, "XC", kb=4, **seq),
          Phase("lru_y", "act", 10, mods=14, **seq),
          Phase("lru_out", "resid", 8, "XC", kb=10, norm="ffn0", **seq),
          Phase("ffn_up0", "glu", 44, mods=20, **seq),
          Phase("ffn_down0", "resid", 16, "F", kb=11, per=2, mods=42, norm="kv", **seq),
          Phase("kv_k", "act", 4, "Y", **seq), Phase("kv_v", "vtok", 4, "Y", **seq),
          Phase("q", "act", 8, mods=50, **seq),
          Phase("attn_out", "resid", 8, "Y", mods=54, norm="ffn1", **seq), Phase("ffn_up1", "glu", 44, **seq),
          Phase("ffn_down1", "resid", 16, "F", kb=11, per=2, norm="final", **seq)]
    for l in range(2):
        tail = seq if l else {}
        ph += [Phase(f"a_cx{l}", "cx", 16, l=l), Phase(f"a_b{l}", "conv_gate", 8, l=l),
               Phase(f"up_a{l}", "merge", 16, "HY", l=l, **tail),
               Phase(f"dt{l}", "dt", 1, l=l), Phase(f"s_x{l}", "conv_silu", 8, l=l),
               Phase(f"s_bc{l}", "conv_silu", 8, l=l, t0=8), Phase(f"s_z{l}", "act", 8, l=l),
               Phase(f"up_b{l}", "merge", 16, "HY", l=l, **tail),
               Phase(f"r_v{l}", "vtok", 8, l=l), Phase(f"r_q{l}", "rotate", 8, l=l),
               Phase(f"r_k{l}", "rotate", 8, l=l), Phase(f"r_g{l}", "act", 8, l=l),
               Phase(f"up_c{l}", "merge", 16, "HY", l=l, **tail),
               Phase(f"b_v{l}", "vtok", 8, l=l), Phase(f"b_k{l}", "act", 8, l=l), Phase(f"b_q{l}", "act", 8, l=l),
               Phase(f"up_d{l}", "merge_split", 16, "HY", l=l, **tail),
               Phase(f"mix_out{l}", "act", 8, "M", l=l, norm=f"post{l}", **tail),
               Phase(f"ffn_up{2 + l}", "glu", 44, l=l, **tail),
               Phase(f"ffn_down{2 + l}", "act", 16, "F", kb=11, per=2, l=l, norm=f"fpost{l}", **tail)]
    count = {s: 0 for s in ("mixed", "high", "low", "turned", "copied")}
    slot, bank = [0] * SLOTS, [0] * SLOTS
    for p in ph:
        p.base = dict(count)
        for s, c in p.count.items():
            count[s] += c
        p.end = dict(count)
        p.slot, p.bank = list(slot), list(bank)
        for c in range(p.n):
            slot[c % SLOTS] += 1
            if p.per == 1 or c % 2:
                bank[c % SLOTS] += 1
        p.bank_end = list(bank)
    later = [[] for _ in range(SLOTS)]
    for p in reversed(ph):
        p.next_kb = {}
        for c in reversed(range(p.n)):
            s = c % SLOTS
            p.next_kb[c // SLOTS, s] = later[s][-1] if later[s] else None
            later[s].append(p.kb)
        p.looped = p.rounds
        if p.n % SLOTS:
            p.looped = 0
        elif any(p.next_kb[p.rounds - 1, s] != p.kb for s in range(SLOTS)):
            p.looped = p.rounds - 1
        if p.looped < 2 or p.norm:
            p.looped = 0
    return ph


class Own:

    def __init__(self, eng, sem):
        self.eng, self.sem, self.n, self.start, self.in_loop = eng, sem, 0, 0, None

    def wait(self, ins):
        self.n += 1
        ins.then_inc(self.sem, 1)
        at = self.n if self.in_loop is None else self.start + self.in_loop + self.n
        self.eng.wait_ge(self.sem, at)


def rounds(eng, p, step, own=None, per_round=0):
    if p.looped:
        if own is not None:
            own.start, own.n = own.n, 0
        with eng.Fori(0, p.looped) as r:
            if own is not None:
                own.in_loop = r * per_round
            step(r, True)
        if own is not None:
            assert own.n == per_round, (p.name, own.n, per_round)
            own.in_loop, own.n = None, own.start + p.looped * per_round
    for r in range(p.looped, p.rounds):
        step(r, False)


def flat(buf, t, off, n):
    if isinstance(t, int):
        return buf[:, t, off:off + n]
    return buf[:, bass.ds(t, 1), off:off + n].rearrange("p a n -> p (a n)")


def col(buf, c):
    return buf[:, c:c + 1] if isinstance(c, int) else buf[:, bass.ds(c, 1)]


def two_layer_pair(nc, a, out):
    ph = plan()
    by = {p.name: p for p in ph}
    ctx = ExitStack()
    with ctx:
        base = nc.sbuf_base + 31 & ~31
        top = [base]

        def place(name, shape, dt=F32, at=None):
            size = int(np.prod(shape[1:])) * 4
            if at is None:
                at = top[0]
                top[0] = at + (size + 31 & ~31)
            assert at + size <= nc.sbuf_usable_end, (name, at + size - nc.sbuf_usable_end)
            return nc.alloc_sbuf_tensor_at(name, shape, dt, offset=at)

        raw = place("raw", [P, SLOTS, 11 * P])
        w_hi = place("w_hi", [P, SLOTS, 11 * P], F32R)
        w_lo = place("w_lo", [P, SLOTS, 11 * P], F32R)
        X = place("x_res", [P, DT8, TOK])
        Hh = place("h_hi", [P, DT8, TOK], F32R)
        Hl = place("h_lo", [P, DT8, TOK], F32R)
        S8 = place("scratch8", [P, DT8, TOK])
        m_at = top[0]
        M = place("merged", [P, DT8, TOK])
        BT = place("bias_t", [P, 8, SEQ], at=m_at)
        M2 = place("lru_m2", [P, LT - 2, SEQ], at=m_at)
        OH = place("onehot", [32, BIASW], at=m_at)
        RB = place("rel_bias", [32, 8], at=m_at + 4 * BIASW)
        BR = place("bias_row", [8, BIASW], at=m_at + 8 * BIASW)
        CI = place("conv_in", [P, SLOTS, TOK + 4])
        CO = place("conv_out", [P, SLOTS, TOK])
        ACS = place("acs", [16, TOK])
        RSTD = place("rstd", [P, TOK])
        PV = place("params", [P, PCOLS])
        CS = place("consts", [P, CCOLS])
        ONES = place("ones", [P, P])
        MOD = place("mod", [P, MOD_SECTIONS * 8])
        SM = place("small", [P, 224])
        region = top[0]

        def tiles(name, shape, tile, dt=F32):
            return place(name, shape, dt, at=region + (int(tile * TOK) * 4 + 31 & ~31))

        Fh, Fl = tiles("f_hi", [P, FT, TOK], 0, F32R), tiles("f_lo", [P, FT, TOK], FT, F32R)
        MW = tiles("mod_raw", [P, 2, 8, MU], 52)
        ACC = tiles("mod_acc", [P, 2, MU], 50)
        MW8 = tiles("mod_raw_first", [P, FIRST, 8, MU], 0)
        ACC8 = place("mod_acc_first", [P, 2, MU], at=m_at + 12 * BIASW)
        XCh, XCl = tiles("xc_hi", [P, LT, TOK], 0, F32R), tiles("xc_lo", [P, LT, TOK], LT, F32R)
        YB, XC = tiles("y_branch", [P, LT, SEQ], 20), tiles("xc", [P, LT, SEQ], 30)
        LA = tiles("lru_a", [P, LT, SEQ], 40)
        Yh, Yl = tiles("y_hi", [P, DT8, TOK], 0, F32R), tiles("y_lo", [P, DT8, TOK], 8, F32R)
        AK, AQ = tiles("a_k", [P, 4, SEQ], 16), tiles("a_q", [P, 8, SEQ], 20)
        AV = tiles("a_v", [P, 2, 512], 28)
        AL, APT = tiles("a_logits", [P, 2, 384], 32), tiles("a_probs_t", [P, 2, 384], 35)
        U = tiles("u", [P, DT8, TOK + 2], 16)
        XS, BC, Z = tiles("s_xs", [P, 8, TOK], 16), tiles("s_bc", [P, 8, 384], 24), tiles("s_z", [P, 8, TOK], 36)
        XT = tiles("s_xdt", [P, 3, D], 44)
        SE, SX = tiles("s_decay", [P, 2, PACK], 55.5), tiles("s_mix", [P, 2, PACK], 59)
        SD = tiles("s_dt", [16, 7, TOK], 55.5)
        CB = tiles("s_cb", [P, 4, PACK], 0)
        YQ = tiles("y_squares", [P, 8, TOK], 24)
        YR = tiles("y_rstd_rows", [P, 4, TOK], 55.5)
        RQ, RK, RV = tiles("r_q", [P, 8, TOK], 16), tiles("r_k", [P, 8, 384], 24), tiles("r_v", [P, 3, D], 36)
        RG, RP = tiles("r_g", [P, 8, TOK], 47.4), tiles("r_p", [P, 2, PACK], 56)
        BK, BV, BQ = tiles("b_k", [P, 8, 384], 16), tiles("b_v", [P, 3, D], 28), tiles("b_q", [P, 8, TOK], 40)
        ZS, SA, SS, SW = (tiles(n, [P, 2, PACK], 48 + 4 * i) for i, n in enumerate(("b_z", "b_a", "b_s", "b_w")))
        Mh, Ml = tiles("m_hi", [P, DT8, TOK], 16, F32R), tiles("m_lo", [P, DT8, TOK], 24, F32R)

        bank = [ctx.enter_context(nc.psum_tensor(f"stream{i}", [P, 512], F32)) for i in range(SLOTS)]
        B = [ctx.enter_context(nc.psum_tensor(f"side{i}", [P, 512], F32)) for i in range(4)]

        def sem(name):
            return ctx.enter_context(nc.semaphore(name))

        raw_ready = [sem(f"raw_ready{i}") for i in range(SLOTS)]
        hi_ready = [sem(f"hi_ready{i}") for i in range(SLOTS)]
        lo_ready = [sem(f"lo_ready{i}") for i in range(SLOTS)]
        chunk_done = [sem(f"chunk_done{i}") for i in range(SLOTS)]
        bank_free = [sem(f"bank_free{i}") for i in range(SLOTS)]
        sig = {s: sem(s) for s in ("mixed", "high", "low", "turned", "copied")}
        vec_own, act_own = sem("vec_own"), sem("act_own")
        loaded = {n: sem(f"loaded_{n}") for n in ("params", "consts", "x", "meta", "heads", "onehot", "bias")}
        const_ready = sem("const_ready")
        mod_ready = [sem(f"mod_ready{i}") for i in range(2)]
        mod_first = [sem(f"mod_first{i}") for i in range(FIRST)]
        mod_acc = [sem(f"mod_acc{i}") for i in range(2)]
        mod_sum, mod_taken = sem("mod_sum"), sem("mod_taken")
        squares, sum_done, rstd_ready = sem("squares"), sem("sum_done"), sem("rstd_ready")
        scaled, h_hi, h_lo, x_new = sem("scaled"), sem("h_hi_ready"), sem("h_lo_ready"), sem("x_new")
        silu_c = sem("silu_c")
        sp_u, sp_w, sp_ln = sem("sp_u"), sem("sp_w"), sem("sp_ln")
        side = {n: sem(n) for n in (
            "gate_tanh", "gate_in", "gate_a", "gate_m2", "gate_sqrt", "lru_gelu", "lru_y32", "lru_hi", "lru_lo",
            "bias_sum", "bias_row", "bias_out", "att_s", "att_max", "att_exp", "att_p", "att_t", "att_pt",
            "att_o", "side_hi", "side_lo",
            "dt_in", "dt_neg", "dt_acs", "dt_turned", "dt_cols", "x_turned", "x_scaled", "cb_done", "cb_masked",
            "acs_rows", "decay_log", "decay_exp", "decay_mix", "head_y", "y_taken", "y_sq", "y_sum", "y_rstd", "y32",
            "ret_s", "ret_p", "ret_y", "ret_copy", "ret_mean", "sb_s", "sb_z", "sb_soft", "sb_sp", "sb_r",
            "sb_logw", "sb_w", "sb_we", "sb_o")}
        stored = sem("stored")

        norms = ["mix0", "ffn0", "kv", "mix1", "ffn1", "final"] + [n + str(l) for l in range(2)
                                                                   for n in ("pre", "post", "fpre", "fpost")]
        to_x = ["final", "post0", "fpost0", "post1", "fpost1"]
        stat_no = {n: i for i, n in enumerate(n for n in norms if n != "mix1")}
        split_no = {n: i for i, n in enumerate(n for n in norms if n not in to_x)}
        scaled_no = {n: i for i, n in enumerate(n for n in norms if n != "final")}
        x_no = {n: i for i, n in enumerate(to_x)}

        rhs_of = {"H": (Hh, Hl), "XC": (XCh, XCl), "F": (Fh, Fl), "Y": (Yh, Yl), "M": (Mh, Ml)}
        ident = CS[:, CCOL["ident"]:CCOL["ident"] + P]
        suffix = CS[:, CCOL["suffix"]:CCOL["suffix"] + P]
        incl = CS[:, CCOL["incl"]:CCOL["incl"] + PACK]
        strict = CS[:, CCOL["strict"]:CCOL["strict"] + PACK]
        cos, sin = (CS[:, CCOL[n]:CCOL[n] + TOK] for n in ("cos", "sin"))
        CSC, GS, SPL, SPT, SPW, DTT, NAT, AMX, ASM, EAL, EPSC, EA = 0, 8, 36, 46, 56, 96, 144, 192, 196, 200, 210, 212
        bias_rows = nc.dram_tensor("bias_rows", (8, P, BIASW), F32, kind="Internal").ap()

        def pcol(name, k=0):
            return PV[:, PCOL[name] + k:PCOL[name] + k + 1]

        def gen(p, r, s):
            return p.slot[s] + r

        block = ctx.enter_context(nc.Block())

        @block.sync
        def _(sp):
            sp.dma_start(PV[:, :], a["params"]).then_inc(loaded["params"], 16)
            sp.dma_start(X[:, :, META:], a["x"]).then_inc(loaded["x"], 16)
            for u in range(FIRST):
                sp.dma_start(MW8[:, u, :, :], a["mod_w"][u]).then_inc(mod_first[u], 16)
            sp.dma_start(OH[:, :], a["onehot"]).then_inc(loaded["onehot"], 16)
            sp.dma_start(RB[:, :], a["rel_bias"]).then_inc(loaded["onehot"], 16)

            def load(p, r, looped):
                for s in range(p.slots(r) if not looped else SLOTS):
                    if p.name != ph[0].name or r:
                        sp.wait_ge(lo_ready[s], gen(p, r, s))
                    w = a[p.name]
                    src = w[r * SLOTS + s] if isinstance(r, int) else \
                        w[bass.ds(r * SLOTS + s, 1)].rearrange("c p n -> (c p) n")
                    sp.dma_start(raw[:, s, 0:p.kb * P], src).then_inc(raw_ready[s], 16)

            for p in ph:
                rounds(sp, p, lambda r, looped: load(p, r, looped))
                if p.name == "lru_x":
                    sp.dma_start(CS[:, :], a["consts"]).then_inc(loaded["consts"], 16)
                    sp.dma_start(X[:, :, 0:META], a["meta"]).then_inc(loaded["meta"], 16)
                    sp.dma_start(SM[0:16, EAL:EAL + 4], a["heads"]).then_inc(loaded["heads"], 16)
                    sp.wait_ge(side["bias_row"], 1)
                    sp.dma_start(bias_rows, BR[:, :].unsqueeze(1).to_broadcast([8, P, BIASW])).then_inc(side["bias_out"], 16)
                    sp.wait_ge(side["bias_out"], 16)
                if p.name == "lru_out":
                    sp.wait_ge(side["lru_lo"], LT)
                    sp.dma_start(BT[:, :, :], bass.AP(tensor=bias_rows.tensor, offset=P - 1,
                                                      ap=[[BIASW - 1, P], [P * BIASW, 8], [1, SEQ]])).then_inc(loaded["bias"], 16)
            for k in range(DT8):
                sp.wait_ge(x_new, 8 * x_no["fpost1"] + k + 1)
                sp.dma_start(out[:, k, :], X[:, k, META:]).then_inc(stored, 16)
            sp.wait_ge(stored, 16 * DT8)

        @block.gpsimd
        def _(pool):
            def load_mod(m):
                for i in range(2):
                    if not isinstance(m, int) or m > FIRST // 2:
                        pool.wait_ge(mod_acc[i], m)
                    src = a["mod_w"][2 * m + i] if isinstance(m, int) else \
                        a["mod_w"][bass.ds(2 * m + i, 1)].rearrange("u p k n -> (u p) k n")
                    pool.dma_start(MW[:, i, :, :], src).then_inc(mod_ready[i], 16)

            def step(p, r, looped):
                if p.has_mods(r) and (not isinstance(r, int) or p.mods // 2 + r + 1 < MOD_UNITS // 2):
                    load_mod(p.mods // 2 + r + 1)
                for s in (1, 3):
                    kb = p.kb if looped else p.next_kb.get((r, s))
                    if kb is not None:
                        pool.wait_ge(hi_ready[s], gen(p, r, s) + 2)
                        low_w(s, kb)

            def low_w(s, kb):
                pool.tensor_tensor(w_lo[:, s, 0:kb * P], raw[:, s, 0:kb * P], w_hi[:, s, 0:kb * P].bitcast(F32),
                                   ALU.subtract).then_inc(lo_ready[s], 1)

            def run(name):
                p = by[name]
                rounds(pool, p, lambda r, looped: step(p, r, looped))

            def low_h(name, off, n):
                for k in range(DT8):
                    pool.wait_ge(h_hi, 8 * split_no[name] + k + 1)
                    pool.tensor_tensor(Hl[:, k, off:off + n], S8[:, k, off:off + n], Hh[:, k, off:off + n].bitcast(F32),
                                       ALU.subtract).then_inc(h_lo, 1)

            def add_x(name, off, n):
                for k in range(DT8):
                    pool.wait_ge(scaled, 8 * scaled_no[name] + k + 1)
                    x = X[:, k, off:off + n]
                    pool.tensor_tensor(x, x, S8[:, k, off:off + n], ALU.add).then_inc(x_new, 1)

            for u in range(FIRST - 2, FIRST):
                pool.wait_ge(mod_acc[u % 2], u // 2 + 1)
            load_mod(FIRST // 2)
            for s in (1, 3):
                pool.wait_ge(hi_ready[s], 1)
                low_w(s, DT8)
            for p in ph:
                if p.name.startswith("a_cx"):
                    low_h(f"pre{p.l}", 0, TOK)
                run(p.name)
                off, n = p.off, p.T
                if p.name.startswith("mix_out"):
                    add_x(f"post{p.l}", off, n)
                    low_h(f"fpre{p.l}", off, n)
                if p.name in ("ffn_down2", "ffn_down3"):
                    add_x(f"fpost{p.l}", off, n)

        @block.tensor
        def _(pe):
            def three(ps, w, wcols, x, k, off, n, first, last):
                W = slice(wcols * P, (wcols + 1) * P)
                pe.matmul(ps, w_hi[:, w, W], x[0][:, k, off:off + n], start=first, stop=False)
                pe.matmul(ps, w_hi[:, w, W], x[1][:, k, off:off + n], start=False, stop=False)
                return pe.matmul(ps, w_lo[:, w, W], x[0][:, k, off:off + n], start=False, stop=last)

            def chunk(p, r, s, ready):
                pe.wait_ge(lo_ready[s], gen(p, r, s) + 1)
                b = s if p.per == 1 else s | 1
                if p.per == 1 or s % 2 == 0:
                    pe.wait_ge(bank_free[b], p.bank[b] + r)
                if p.kind == "gates":
                    j = 4 * r + s
                    if s % 2 == 0:
                        pe.wait_ge(sig["low"], by["lru_x"].base["low"] + j + 2)
                    for g in range(2):
                        for k in range(2):
                            last = three(bank[s][:, g * SEQ:(g + 1) * SEQ], s, 2 * g + k, rhs_of["XC"],
                                         2 * (j // 2) + k, 0, SEQ, k == 0, k == 1)
                else:
                    x = rhs_of[p.rhs] if p.rhs != "HY" else rhs_of["HY"[s % 2]]
                    kx = 11 * (s % 2) if p.per == 2 else 0
                    off = 0 if p.rhs in ("XC",) else p.off
                    for k in range(p.kb):
                        if ready is not None and s == (1 if p.rhs == "HY" or kx else 0):
                            pe.wait_ge(ready[0], ready[1] + kx + k + 1)
                        last = three(bank[b][:, 0:p.T], s, k, x, kx + k, off, p.T,
                                     k == 0 and (p.per == 1 or s % 2 == 0), k == p.kb - 1 and (p.per == 1 or s % 2 == 1))
                last.then_inc(chunk_done[s], 1)

            def turn(p, r, s):
                t = SLOTS * r + s
                b = B[s % 2]
                pe.wait_ge(bank_free[s], p.bank[s] + r + 1)
                pe.wait_ge(sig["copied"], p.base["copied"] + t + 1)
                keys = KEYS if p.T == TOK else KEYS[:2]
                for i, (q, n) in enumerate(keys):
                    last = pe.transpose(b[0:n, i * P:(i + 1) * P], CO[:, s, q:q + n], ident)
                last.then_inc(sig["turned"], 1)

            def mod_sums(p, r):
                for i in range(2):
                    m = p.mods // 2 + r
                    mod_columns(m, i)

            def mod_columns(m, i):
                acc = ACC8 if isinstance(m, int) and m < FIRST // 2 else ACC
                pe.wait_ge(mod_acc[i], m + 1)
                if not isinstance(m, int) or m:
                    pe.wait_ge(mod_taken, 2 * m + i - 1)
                for j in range(2):
                    last = pe.matmul(B[2 + i][:, j:j + 1], acc[:, i, j * P:(j + 1) * P], ONES[:, 0:1],
                                     start=True, stop=True)
                last.then_inc(mod_sum, 1)

            def step(p, r, looped, ready=None):
                n = SLOTS if looped else p.slots(r)
                for s in range(n):
                    chunk(p, r, s, ready)
                    if p.kind == "vtok" and s:
                        turn(p, r, s - 1)
                    if p.norm:
                        t = (SLOTS * r + s) // p.per - 1
                        if t >= 0 and (p.per == 1 or s % 2 == 0):
                            sum_tile(p.norm, t, p.off, p.T)
                if p.kind == "vtok":
                    turn(p, r, n - 1)
                if p.has_mods(r):
                    mod_sums(p, r)

            def sum_tile(name, k, off, n):
                pe.wait_ge(squares, 8 * stat_no[name] + k + 1)
                last = pe.matmul(B[0][:, 0:n], ONES[:, :], S8[:, k, off:off + n], start=k == 0, stop=k == DT8 - 1)
                if k == DT8 - 1:
                    last.then_inc(sum_done, 1)

            def sum_squares(name, off, n):
                for k in range(DT8):
                    sum_tile(name, k, off, n)

            def attention():
                def scores(h):
                    if h >= 2:
                        pe.wait_ge(side["att_p"], h - 1)
                    pe.matmul(B[h % 2][:, 0:P], AQ[:, h, 0:P], AK[:, h // 2, 0:P], start=True, stop=True)
                    pe.matmul(B[h % 2][:, P:384], AQ[:, h, P:SEQ], AK[:, h // 2, :], start=True, stop=True)\
                        .then_inc(side["att_s"], 1)

                def turn_probs(h):
                    pe.wait_ge(side["att_p"], h + 1)
                    if h:
                        pe.wait_ge(side["att_pt"], h)
                    for i in range(3):
                        last = pe.transpose(B[2][:, i * P:(i + 1) * P], AL[:, h % 2, i * P:(i + 1) * P], ident)
                    last.then_inc(side["att_t"], 1)

                def values(h):
                    pe.wait_ge(side["att_pt"], h + 1)
                    if h:
                        pe.wait_ge(side["side_lo"], h)
                    v = slice(h // 2 * P, (h // 2 + 1) * P)
                    pe.matmul(B[3][:, 0:SEQ], AV[:, 0, v], APT[:, h % 2, 0:SEQ], start=True, stop=False)
                    pe.matmul(B[3][:, P:SEQ], AV[:, 1, v], APT[:, h % 2, SEQ:], start=False, stop=True)\
                        .then_inc(side["att_o"], 1)

                for i in range(8 + 2):
                    if i < 8:
                        scores(i)
                    if i >= 2:
                        values(i - 2)
                    if 1 <= i <= 8:
                        turn_probs(i - 1)

            def packed_scores(b, key, ktiles, q, qt):
                for n, (c, q0, w) in enumerate(SEG):
                    for i, (kt, qq) in enumerate(zip(ktiles, qt)):
                        last = pe.matmul(b[:, c:c + w], key[:, kt, n * P:(n + 1) * P], q[:, qq, q0:q0 + w],
                                         start=i == 0, stop=i == len(qt) - 1)
                return last

            def weighted(b, rows, v, vcols, w):
                for n, (c, q0, m) in enumerate(SEG):
                    k = KEYS[n][1]
                    last = pe.matmul(b[rows, q0:q0 + m], v[0:k, n, vcols], w[0:k, c:c + m], start=n == 0, stop=n == 2)
                return last

            def state_space(l):
                pe.wait_ge(side["dt_acs"], l + 1)
                for i in range(2):
                    for n, (q, w) in enumerate(KEYS):
                        src = SD[0:16, 6, q:q + w] if i == 0 else ACS[0:16, q:q + w]
                        last = pe.transpose(B[0][0:w, 48 * i + 16 * n:48 * i + 16 * n + 16], src, CS[0:16, 0:16])
                last.then_inc(side["dt_turned"], 1)
                p = by[f"s_z{l}"]
                pe.wait_ge(side["dt_cols"], l + 1)
                pe.wait_ge(sig["high"], by[f"s_x{l}"].end["high"])
                for m in range(6):
                    if m >= 3:
                        pe.wait_ge(side["x_scaled"], 6 * l + m - 2)
                    n, half = m // 2, m % 2
                    q, w = KEYS[n]
                    for j in range(4):
                        last = pe.transpose(B[1 + m % 3][0:w, j * P:(j + 1) * P], XS[:, 4 * half + j, q:q + w], ident)
                    last.then_inc(side["x_turned"], 1)
                pe.wait_ge(side["x_scaled"], 6 * (l + 1))
                pe.wait_ge(sig["high"], by[f"s_bc{l}"].end["high"])
                for g in range(4):
                    packed_scores(B[g], BC, [g], BC, [4 + g]).then_inc(side["cb_done"], 1)

                def rows(h):
                    if h < 2:
                        pe.wait_ge(side["cb_masked"], 4 * l + 4)
                    else:
                        pe.wait_ge(side["decay_log"], 16 * l + h - 1)
                    sel = CS[0:16, h:h + 1].to_broadcast([16, P])
                    pe.matmul(B[h % 2][:, 0:TOK], sel, ACS[0:16, :], start=True, stop=True).then_inc(side["acs_rows"], 1)

                def outputs(h):
                    pe.wait_ge(side["decay_mix"], 16 * l + h + 1)
                    if h >= 4 and h % 2 == 0:
                        pe.wait_ge(side["y_taken"], 8 * l + h // 2 - 1)
                    lo = h % 2 * 64
                    weighted(B[2 + h // 2 % 2], slice(lo, lo + 64), XT, slice(h * 64, h * 64 + 64), SX[:, h % 2])\
                        .then_inc(side["head_y"], 1)

                for i in range(17):
                    if i < 16:
                        rows(i)
                    if i >= 1:
                        outputs(i - 1)
                for g in range(4):
                    pe.wait_ge(side["y_sq"], 8 * l + g + 1)
                    for k in range(2):
                        last = pe.matmul(B[g][:, 0:TOK], ONES[:, :], YQ[:, 2 * g + k, :], start=k == 0, stop=k == 1)
                    last.then_inc(side["y_sum"], 1)

            def retention(l):
                pe.wait_ge(sig["mixed"], by[f"r_k{l}"].end["mixed"])
                pe.wait_ge(sig["copied"], by[f"r_v{l}"].end["copied"] + 2)

                def scores(h):
                    if h >= 2:
                        pe.wait_ge(side["ret_p"], 4 * l + h - 1)
                    packed_scores(B[h % 2], RK, [2 * h, 2 * h + 1], RQ, [2 * h, 2 * h + 1]).then_inc(side["ret_s"], 1)

                def outputs(h):
                    pe.wait_ge(side["ret_p"], 4 * l + h + 1)
                    for e in range(2):
                        t = 2 * h + e
                        if t >= 2:
                            pe.wait_ge(side["ret_copy"], 8 * l + t - 1)
                        weighted(B[2 + e], slice(0, P), RV, slice(t * P, (t + 1) * P), RP[:, h % 2])\
                            .then_inc(side["ret_y"], 1)

                for i in range(5):
                    if i < 4:
                        scores(i)
                    if i >= 1:
                        outputs(i - 1)
                for h in range(4):
                    pe.wait_ge(side["ret_copy"], 8 * (l + 1))
                    for k in range(2):
                        last = pe.matmul(B[h][:, 0:TOK], ONES[:, :], S8[:, 2 * h + k, :], start=k == 0, stop=k == 1)
                    last.then_inc(side["ret_mean"], 1)
                for h in range(4):
                    pe.wait_ge(side["y_sq"], 8 * l + 4 + h + 1)
                    for k in range(2):
                        last = pe.matmul(B[h][:, 0:TOK], ONES[:, :], YQ[:, 2 * h + k, :], start=k == 0, stop=k == 1)
                    last.then_inc(side["y_sum"], 1)

            def stick_breaking(l):
                pe.wait_ge(sig["copied"], by[f"b_v{l}"].end["copied"] + 2)
                for s in range(SLOTS):
                    pe.wait_ge(bank_free[s], by[f"b_q{l}"].bank_end[s])

                def scores(h):
                    if h >= 2:
                        pe.wait_ge(side["sb_z"], 8 * l + h - 1)
                    packed_scores(B[h % 2], BK, [h], BQ, [h]).then_inc(side["sb_s"], 1)

                def suffix_sums(h):
                    pe.wait_ge(side["sb_sp"], 8 * l + h + 1)
                    if h:
                        pe.wait_ge(side["sb_logw"], 8 * l + h)
                    S = SS[:, h % 2]
                    b = B[2]
                    pe.matmul(b[:, 0:272], suffix, S[:, 0:272], start=True, stop=False)
                    pe.matmul(b[:, P:272], ONES[:, :], S[:, 272:416], start=False, stop=False)
                    pe.matmul(b[:, 256:272], ONES[0:16, :], S[0:16, 416:432], start=False, stop=True)
                    pe.matmul(b[:, 272:416], suffix, S[:, 272:416], start=True, stop=False)
                    pe.matmul(b[:, 400:416], ONES[0:16, :], S[0:16, 416:432], start=False, stop=True)
                    pe.matmul(b[:, 416:432], suffix[0:16, :], S[0:16, 416:432], start=True, stop=True)\
                        .then_inc(side["sb_r"], 1)

                def outputs(h):
                    pe.wait_ge(side["sb_w"], 8 * l + h + 1)
                    if h:
                        pe.wait_ge(side["side_lo"], 24 + 24 * l + h)
                    weighted(B[3], slice(0, P), BV, slice(h * P, (h + 1) * P), SW[:, h % 2]).then_inc(side["sb_o"], 1)

                for i in range(10):
                    if i < 8:
                        scores(i)
                    if 1 <= i <= 8:
                        suffix_sums(i - 1)
                    if i >= 2:
                        outputs(i - 2)

            def run(name, ready=None):
                p = by[name]
                rounds(pe, p, lambda r, looped: step(p, r, looped, ready))
                if p.norm:
                    sum_tile(p.norm, DT8 - 1, p.off, p.T)

            def split(name):
                return h_lo, 8 * split_no[name]

            def lows(name):
                return sig["low"], by[name].base["low"]

            pe.wait_ge(const_ready, 1)
            sum_squares("mix0", META, SEQ)
            for u in range(FIRST):
                mod_columns(u // 2, u % 2)
            pe.wait_ge(loaded["onehot"], 32)
            pe.matmul(B[1][0:8, 0:BIASW], RB[:, :], OH[:, :], start=True, stop=True).then_inc(side["bias_sum"], 1)
            run("lru_x", split("mix0"))
            run("lru_gates")
            run("lru_y")
            run("lru_out", (side["lru_lo"], 0))
            run("ffn_up0", split("ffn0"))
            run("ffn_down0", lows("ffn_up0"))
            run("kv_k", split("kv"))
            pe.wait_ge(loaded["consts"], 16)
            run("kv_v")
            run("q", split("mix1"))
            for s in range(SLOTS):
                pe.wait_ge(bank_free[s], by["q"].bank_end[s])
            pe.wait_ge(sig["copied"], by["kv_v"].end["copied"] + 2)
            attention()
            run("attn_out", (side["side_lo"], 0))
            run("ffn_up1", split("ffn1"))
            run("ffn_down1", lows("ffn_up1"))
            for l in range(2):
                off, n = (META, SEQ) if l else (0, TOK)
                sum_squares(f"pre{l}", 0, TOK)
                run(f"a_cx{l}", split(f"pre{l}"))
                run(f"a_b{l}")
                run(f"up_a{l}", lows(f"a_b{l}"))
                run(f"dt{l}")
                run(f"s_x{l}")
                run(f"s_bc{l}")
                run(f"s_z{l}")
                state_space(l)
                run(f"up_b{l}", (side["side_lo"], 8 + 24 * l))
                run(f"r_v{l}")
                run(f"r_q{l}")
                run(f"r_k{l}")
                run(f"r_g{l}")
                retention(l)
                run(f"up_c{l}", (side["side_lo"], 16 + 24 * l))
                run(f"b_v{l}")
                run(f"b_k{l}")
                run(f"b_q{l}")
                stick_breaking(l)
                run(f"up_d{l}", (side["side_lo"], 24 + 24 * l))
                run(f"mix_out{l}", lows(f"up_d{l}"))
                sum_squares(f"fpre{l}", off, n)
                run(f"ffn_up{2 + l}", split(f"fpre{l}"))
                run(f"ffn_down{2 + l}", lows(f"ffn_up{2 + l}"))

        @block.scalar
        def _(act):
            own = Own(act, act_own)

            def cut(p, r, s, looped):
                kb = p.kb if looped else p.next_kb[r, s]
                if kb is None:
                    return
                g = gen(p, r, s) + 1
                act.wait_ge(raw_ready[s], 16 * (g + 1))
                act.wait_ge(chunk_done[s], g)
                act.copy(w_hi[:, s, 0:kb * P], raw[:, s, 0:kb * P]).then_inc(hi_ready[s], 1)

            acts = {"lru_y": (YB, ACT.Copy, 1.0), "kv_k": (AK, ACT.Copy, 1.0), "q": (AQ, ACT.Copy, 1.0)}
            for l in range(2):
                acts |= {f"s_z{l}": (Z, ACT.Silu, 1.0), f"r_g{l}": (RG, ACT.Silu, 1.0), f"b_k{l}": (BK, ACT.Copy, 1.0),
                         f"b_q{l}": (BQ, ACT.Copy, P ** -0.5), f"mix_out{l}": (M, ACT.Copy, 1.0),
                         f"ffn_down{2 + l}": (M, ACT.Copy, 1.0)}

            def step(p, r, looped):
                n = SLOTS if looped else p.slots(r)
                for s in range(n):
                    done = gen(p, r, s) + 1
                    free = p.bank[s] + r + 1
                    t = r * SLOTS + s
                    if p.kind in ("conv_split", "conv_silu"):
                        act.wait_ge(chunk_done[s], done)
                        act.copy(CI[:, s, 3:3 + p.T], bank[s][:, 0:p.T]).then_inc(bank_free[s], 1)
                        cut(p, r, s, looped)
                        act.wait_ge(sig["mixed"], p.base["mixed"] + t + 1)
                        if p.kind == "conv_split":
                            act.copy(flat(XCh, t, 0, p.T), flat(XC, t, 0, p.T)).then_inc(sig["high"], 1)
                        else:
                            dst = XS if p.t0 == 0 else BC
                            act.activation(flat(dst, t, 0, p.T), CO[:, s, 0:p.T], ACT.Silu).then_inc(sig["high"], 1)
                        continue
                    if p.kind == "vtok":
                        act.wait_ge(chunk_done[s], done)
                        act.wait_ge(sig["copied"], p.base["copied"] + t + 1)
                        act.copy(CO[:, s, 0:p.T], bank[s][:, 0:p.T]).then_inc(bank_free[s], 1)
                    if p.kind == "act":
                        b = s
                        if p.per == 2:
                            t = r * 2 + s // 2
                        if p.per == 1 or s % 2:
                            act.wait_ge(chunk_done[s], done)
                            dst, func, scale = acts[p.name]
                            off = p.off if dst is M else 0
                            act.activation(flat(dst, t, off, p.T), bank[b][:, 0:p.T], func, scale=scale)\
                                .then_inc(bank_free[b], 1)
                    if p.kind in ("glu", "cx", "merge", "merge_split") and s % 2 == 0:
                        func = {"glu": ACT.Silu, "cx": ACT.Copy}.get(p.kind, ACT.Sigmoid)
                        act.wait_ge(chunk_done[s], done)
                        act.activation(CI[:, s, 3:3 + p.T], bank[s][:, 0:p.T], func).then_inc(bank_free[s], 1)
                    if p.kind in ("glu", "cx", "merge", "merge_split") and s % 2:
                        q = r * 2 + s // 2
                        act.wait_ge(bank_free[s], free)
                        if p.kind == "glu":
                            act.copy(flat(Fh, q, p.off, p.T), CO[:, s - 1, 0:p.T]).then_inc(sig["high"], 1)
                        if p.kind == "merge_split":
                            act.wait_ge(sig["mixed"], p.base["mixed"] + q + 1)
                            act.copy(flat(Mh, q, p.off, p.T), CO[:, s - 1, 0:p.T]).then_inc(sig["high"], 1)
                    if p.kind == "conv_gate":
                        cut(p, r, s, looped)
                        act.wait_ge(bank_free[s], free)
                        act.copy(flat(Yh, t, 0, p.T), CI[:, s, 3:3 + p.T]).then_inc(sig["high"], 1)
                        continue
                    if p.kind == "dt":
                        act.wait_ge(chunk_done[s], done)
                        act.activation(SD[:, 0, :], bank[0][0:16, 0:TOK], ACT.Identity,
                                       bias=SM[0:16, EAL + 2 * p.l:EAL + 2 * p.l + 1]).then_inc(bank_free[0], 1)
                        cut(p, r, s, looped)
                        act.activation(SM[0:16, EA + p.l:EA + p.l + 1], SM[0:16, EAL + 2 * p.l + 1:EAL + 2 * p.l + 2], ACT.Exp)
                        act.wait_ge(bank_free[0], free)
                        softplus(SD[:, 0, :], SD[:, 1, :], SD[:, 2, :], SD[:, 3, :], 2 + p.l)
                        continue
                    if p.kind == "gates":
                        act.wait_ge(chunk_done[s], done)
                        if t >= 8:
                            act.wait_ge(side["gate_in"], t - 7)
                        c = PCOL["lru_b_gates"] + t
                        act.activation(LA[:, t, :], bank[s][:, 0:SEQ], ACT.Sigmoid, bias=PV[:, c:c + 1])
                        act.activation(S8[:, t % 8, 0:SEQ], bank[s][:, SEQ:], ACT.Sigmoid, bias=PV[:, c + LT:c + LT + 1])\
                            .then_inc(bank_free[s], 1)
                        cut(p, r, s, looped)
                        act.wait_ge(bank_free[s], free)
                        dst = M2[:, t, :] if t < 8 else CO[:, t - 8, 0:SEQ]
                        act.activation(dst, LA[:, t, :], ACT.Tanh, scale=SM[:, SPT + t:SPT + t + 1]).then_inc(side["gate_tanh"], 1)
                        continue
                    if p.kind == "resid" and (p.per == 1 or s % 2):
                        t = t if p.per == 1 else r * 2 + s // 2
                        act.wait_ge(bank_free[s], free)
                        act.activation(S8[:, t, META:], X[:, t, META:], ACT.Square).then_inc(squares, 1)
                    cut(p, r, s, looped)

            tables = {"glu": "silu_and_others", "conv_silu": "silu_and_others", "merge": "sigmoid_and_others",
                      "merge_split": "sigmoid_and_others", "gates": "sigmoid_and_others"}

            def log_exp():
                act.preload_act_table_set("natural_log_exp_and_others")

            def run(name):
                p = by[name]
                if p.kind in tables:
                    act.preload_act_table_set(tables[p.kind])
                rounds(act, p, lambda r, looped: step(p, r, looped))

            def inverse_root(src, dst, scale, ready, no, done):
                act.wait_ge(ready, no)
                own.wait(act.activation(dst, src, ACT.Ln, bias=SM[:, EPSC:EPSC + 1], scale=scale))
                act.activation(dst, dst, ACT.Exp, scale=-0.5).then_inc(done, 1)

            def root(name, off, n):
                log_exp()
                inverse_root(B[0][:, 0:n], RSTD[:, 0:n], 1.0 / D, sum_done, stat_no[name] + 1, rstd_ready)

            def high_h(name, off, n, dst, shift=None):
                for k in range(DT8):
                    act.wait_ge(scaled, 8 * scaled_no[name] + k + 1)
                    if shift is None:
                        act.copy(dst[:, k, off:off + n], S8[:, k, off:off + n]).then_inc(h_hi, 1)
                    else:
                        act.activation(dst[:, k, off:off + n], S8[:, k, off:off + n], ACT.Identity,
                                       bias=MOD[:, shift + k:shift + k + 1]).then_inc(h_hi, 1)

            def norm(name, off, n, shift=None):
                root(name, off, n)
                high_h(name, off, n, Hh, shift)

            def square_x(name, off, n):
                for k in range(DT8):
                    act.wait_ge(x_new, 8 * x_no[name] + k + 1)
                    act.activation(S8[:, k, off:off + n], X[:, k, off:off + n], ACT.Square).then_inc(squares, 1)

            def softplus(z, u, ln, w, no):
                log_exp()
                own.wait(act.activation(u, z, ACT.Abs))
                act.activation(u, u, ACT.Exp, scale=-1.0).then_inc(sp_u, 1)
                act.wait_ge(sp_w, no)
                act.activation(ln, w, ACT.Ln).then_inc(sp_ln, 1)

            def recurrence_beside(name):
                p = by[name]
                for r in range(p.rounds):
                    step(p, r, False)
                    for t in range(SLOTS * r, min(SLOTS * (r + 1), LT)):
                        act.wait_ge(side["gate_tanh"], t + 1)
                        act.activation(LA[:, t, :], LA[:, t, :], ACT.Exp, scale=SM[:, SPL + t:SPL + t + 1])\
                            .then_inc(side["gate_a"], 1)
                        if t:
                            input_factor(t - 1)
                input_factor(LT - 1)

            def input_factor(t):
                act.wait_ge(side["gate_m2"], t + 1)
                m = M2[:, t, :] if t < 8 else CO[:, t - 8, 0:SEQ]
                own.wait(act.activation(m, m, ACT.Ln, bias=SM[:, EPSC + 1:EPSC + 2]))
                act.activation(m, m, ACT.Exp, scale=0.5).then_inc(side["gate_sqrt"], 1)

            def attention():
                log_exp()

                def exps(h):
                    b = h % 2
                    act.wait_ge(side["att_max"], h + 1)
                    for i, (c, w) in enumerate(((0, P), (P, SEQ))):
                        ins = act.activation(AL[:, b, c:c + w], AL[:, b, c:c + w], ACT.Exp,
                                             bias=SM[:, AMX + 2 * b + i:AMX + 2 * b + i + 1],
                                             accum_out=SM[:, ASM + 2 * b + i:ASM + 2 * b + i + 1])
                    ins.then_inc(side["att_exp"], 1)

                def take_probs(h):
                    act.wait_ge(side["att_t"], h + 1)
                    if h >= 2:
                        act.wait_ge(side["att_o"], h - 1)
                    act.copy(APT[:, h % 2, :], B[2][:, 0:384]).then_inc(side["att_pt"], 1)

                for i in range(10):
                    if i < 8:
                        exps(i)
                    if 1 <= i <= 8:
                        take_probs(i - 1)
                    if i >= 2:
                        act.wait_ge(side["att_o"], i - 1)
                        act.copy(Yh[:, i - 2, META:], B[3][:, 0:SEQ]).then_inc(side["side_hi"], 1)

            def state_space(l):
                log_exp()
                for h in range(16):
                    n16 = 16 * l + h
                    b = h % 2
                    act.wait_ge(side["decay_log"], n16 + 1)
                    act.activation(SE[:, b, 0:416], SE[:, b, 0:416], ACT.Exp)
                    act.activation(SE[0:16, b, 416:], SE[0:16, b, 416:], ACT.Exp).then_inc(side["decay_exp"], 1)
                for g in range(4):
                    inverse_root(B[g][:, 0:TOK], YR[:, g, :], 1.0 / 256, side["y_sum"], 8 * l + g + 1, side["y_rstd"])
                halves(16 * l)

            def halves(before):
                for k in range(8):
                    act.wait_ge(side["y32"], before + k + 1)
                    act.copy(Yh[:, k, :], S8[:, k, :]).then_inc(side["side_hi"], 1)

            def retention(l):
                log_exp()
                for t in range(8):
                    act.wait_ge(side["ret_y"], 8 * l + t + 1)
                    act.copy(S8[:, t, :], B[2 + t % 2][:, 0:TOK]).then_inc(side["ret_copy"], 1)
                for h in range(4):
                    inverse_root(B[h][:, 0:TOK], YR[:, h, :], 1.0 / 256, side["y_sum"], 8 * l + 4 + h + 1, side["y_rstd"])
                halves(16 * l + 8)

            def stick_breaking(l):
                log_exp()

                def soft(h):
                    b, n8 = h % 2, 8 * l + h
                    act.wait_ge(side["sb_s"], n8 + 1)
                    if h >= 2:
                        act.wait_ge(side["sb_logw"], n8 - 1)
                    act.copy(ZS[:, b, :], B[b][:, 0:PACK])
                    act.activation(SA[:, b, :], B[b][:, 0:PACK], ACT.Abs).then_inc(side["sb_z"], 1)
                    act.wait_ge(side["sb_z"], n8 + 1)
                    own.wait(act.activation(SA[:, b, :], SA[:, b, :], ACT.Exp, scale=-1.0))
                    act.activation(SA[:, b, :], SA[:, b, :], ACT.Ln, bias=ONES[:, 0:1]).then_inc(side["sb_soft"], 1)

                for i in range(10):
                    if i < 8:
                        soft(i)
                    if 1 <= i <= 8:
                        act.wait_ge(side["sb_logw"], 8 * l + i)
                        act.activation(SW[:, (i - 1) % 2, :], SW[:, (i - 1) % 2, :], ACT.Exp).then_inc(side["sb_we"], 1)
                    if i >= 2:
                        act.wait_ge(side["sb_o"], 8 * l + i - 1)
                        act.copy(Yh[:, i - 2, :], B[3][:, 0:TOK]).then_inc(side["side_hi"], 1)

            act.wait_ge(loaded["params"], 16)
            act.activation(SM[:, CSC:CSC + 8], PV[:, PCOL["c"]:PCOL["c"] + 8], ACT.Silu).then_inc(silu_c, 1)
            act.wait_ge(loaded["x"], 16)
            for k in range(DT8):
                act.activation(S8[:, k, META:], X[:, k, META:], ACT.Square).then_inc(squares, 1)
            root("mix0", META, SEQ)
            for s in range(SLOTS):
                act.wait_ge(raw_ready[s], 16)
                act.copy(w_hi[:, s, 0:DT8 * P], raw[:, s, 0:DT8 * P]).then_inc(hi_ready[s], 1)
            high_h("mix0", META, SEQ, Hh, 0)
            softplus(SM[:, SPT:SPT + LT], SM[:, SPW:SPW + 10], SM[:, SPW + 20:SPW + 30], SM[:, SPW + 10:SPW + 20], 1)
            run("lru_x")
            run("lru_gates")
            log_exp()
            recurrence_beside("lru_y")
            act.preload_act_table_set("gelu_apprx_tanh_and_others")
            for t in range(LT + 1):
                if t < LT:
                    act.activation(YB[:, t, :], YB[:, t, :], ACT.Gelu_apprx_tanh).then_inc(side["lru_gelu"], 1)
                if t:
                    act.wait_ge(side["lru_y32"], t)
                    act.copy(XCh[:, t - 1, 0:SEQ], XC[:, t - 1, :]).then_inc(side["lru_hi"], 1)
            run("lru_out")
            norm("ffn0", META, SEQ, shift=24)
            run("ffn_up0")
            run("ffn_down0")
            root("kv", META, SEQ)
            high_h("kv", META, SEQ, Yh, 48)
            high_h("mix1", META, SEQ, Hh, 64)
            run("kv_k")
            run("kv_v")
            run("q")
            attention()
            run("attn_out")
            norm("ffn1", META, SEQ, shift=88)
            run("ffn_up1")
            run("ffn_down1")
            root("final", META, SEQ)
            square_x("final", 0, TOK)
            for l in range(2):
                off, n = (META, SEQ) if l else (0, TOK)
                norm(f"pre{l}", 0, TOK)
                run(f"a_cx{l}")
                run(f"a_b{l}")
                run(f"up_a{l}")
                run(f"dt{l}")
                run(f"s_x{l}")
                run(f"s_bc{l}")
                run(f"s_z{l}")
                state_space(l)
                run(f"up_b{l}")
                run(f"r_v{l}")
                run(f"r_q{l}")
                run(f"r_k{l}")
                run(f"r_g{l}")
                retention(l)
                run(f"up_c{l}")
                run(f"b_v{l}")
                run(f"b_k{l}")
                run(f"b_q{l}")
                stick_breaking(l)
                run(f"up_d{l}")
                run(f"mix_out{l}")
                root(f"post{l}", off, n)
                square_x(f"post{l}", off, n)
                norm(f"fpre{l}", off, n)
                run(f"ffn_up{2 + l}")
                run(f"ffn_down{2 + l}")
                root(f"fpost{l}", off, n)
                if l == 0:
                    square_x(f"fpost{l}", 0, TOK)

        @block.vector
        def _(dve):
            own = Own(dve, vec_own)
            tt, ts, stt = dve.tensor_tensor, dve.tensor_scalar, dve.scalar_tensor_tensor

            def cut(p, r, s, looped):
                kb = p.kb if looped else p.next_kb[r, s]
                if kb is None or s % 2:
                    return
                dve.wait_ge(hi_ready[s], gen(p, r, s) + 2)
                low_w(s, kb)

            def low_w(s, kb):
                tt(w_lo[:, s, 0:kb * P], raw[:, s, 0:kb * P], w_hi[:, s, 0:kb * P].bitcast(F32), ALU.subtract)\
                    .then_inc(lo_ready[s], 1)

            def low(dst, src, high):
                return tt(dst, src, high.bitcast(F32), ALU.subtract)

            def mod_unit(m, i):
                if isinstance(m, int) and m < FIRST // 2:
                    w, acc = MW8[:, 2 * m + i], ACC8
                    dve.wait_ge(mod_first[2 * m + i], 16)
                else:
                    w, acc = MW[:, i], ACC
                    dve.wait_ge(mod_ready[i], 16 * (m + 1 - FIRST // 2))
                for k in range(8):
                    c = SM[:, CSC + k:CSC + k + 1]
                    if k == 0:
                        ins = ts(acc[:, i, :], w[:, 0, :], c, None, ALU.mult)
                    else:
                        ins = stt(acc[:, i, :], w[:, k, :], c, acc[:, i, :], ALU.mult, ALU.add)
                    if k < 7:
                        own.wait(ins)
                ins.then_inc(mod_acc[i], 1)

            def mod_take(m, i):
                dve.wait_ge(mod_sum, 2 * m + i + 1)
                c = (2 * m + i) * 2
                if isinstance(c, int):
                    dst, b = MOD[:, c:c + 2], PV[:, PCOL["mod_b"] + c:PCOL["mod_b"] + c + 2]
                else:
                    dst, b = MOD[:, bass.ds(c, 2)], PV[:, bass.ds(PCOL["mod_b"] + c, 2)]
                return tt(dst, B[2 + i][:, 0:2], b, ALU.add).then_inc(mod_taken, 1)

            resid_gate = {"lru_out": 16, "ffn_down0": 40, "attn_out": 80, "ffn_down1": 104}

            def step(p, r, looped):
                n = SLOTS if looped else p.slots(r)
                for s in range(n):
                    if p.has_mods(r) and s < 2:
                        mod_unit(p.mods // 2 + r, s)
                    done = gen(p, r, s) + 1
                    t = r * SLOTS + s
                    T = p.T
                    if p.kind in ("conv_split", "conv_silu"):
                        tt_ = t + p.t0
                        names = ("lru_conv_w", "lru_conv_b", LT) if p.kind == "conv_split" else ("ssd_conv_w", "ssd_conv_b", 16)
                        w0, b0 = PCOL[names[0]] + 4 * names[2] * p.l, PCOL[names[1]] + names[2] * p.l
                        dve.wait_ge(bank_free[s], p.bank[s] + r + 1)
                        own.wait(ts(CO[:, s, 0:T], CI[:, s, 0:T], col(PV, w0 + tt_), col(PV, b0 + tt_), ALU.mult, ALU.add))
                        for j in range(1, 4):
                            dst = flat(XC, t, 0, T) if p.kind == "conv_split" and j == 3 else CO[:, s, 0:T]
                            ins = stt(dst, CI[:, s, j:j + T], col(PV, w0 + names[2] * j + tt_), CO[:, s, 0:T],
                                      ALU.mult, ALU.add)
                            if j < 3:
                                own.wait(ins)
                        ins.then_inc(sig["mixed"], 1)
                        cut(p, r, s, looped)
                        dve.wait_ge(sig["high"], p.base["high"] + t + 1)
                        if p.kind == "conv_split":
                            low(flat(XCl, t, 0, T), flat(XC, t, 0, T), flat(XCh, t, 0, T)).then_inc(sig["low"], 1)
                        continue
                    if p.kind == "vtok":
                        cut(p, r, s, looped)
                        if s:
                            take_values(p, t - 1, s - 1)
                        if s == n - 1:
                            take_values(p, t, s)
                        continue
                    if p.kind == "resid":
                        if p.per == 2:
                            t = r * 2 + s // 2
                        if p.per == 1 or s % 2:
                            dve.wait_ge(chunk_done[s], done)
                            x = flat(X, t, META, SEQ)
                            stt(x, bank[s][:, 0:SEQ], col(MOD, resid_gate[p.name] + t), x, ALU.mult, ALU.add)\
                                .then_inc(bank_free[s], 1)
                    q = r * 2 + s // 2
                    if p.kind in ("glu", "cx", "merge", "merge_split") and s % 2:
                        dve.wait_ge(chunk_done[s], done)
                        dve.wait_ge(bank_free[s - 1], p.bank[s - 1] + r + 1)
                        f = CI[:, s - 1, 3:3 + T]
                        if p.kind == "cx":
                            dst = U[:, q, 2:2 + T] if isinstance(q, int) else flat(U, q, 2, T)
                        elif p.name in ("up_a0", "up_a1"):
                            dst = flat(M, q, p.off, T)
                        else:
                            dst = CO[:, s - 1, 0:T]
                        tt(dst, f, bank[s][:, 0:T], ALU.mult).then_inc(bank_free[s], 1)
                        if p.kind in ("merge", "merge_split") and not p.name.startswith("up_a"):
                            dve.wait_ge(bank_free[s], p.bank[s] + r + 1)
                            m = flat(M, q, p.off, T)
                            if p.kind == "merge":
                                tt(m, m, dst, ALU.add)
                            else:
                                tt(dst, m, dst, ALU.add).then_inc(sig["mixed"], 1)
                    if p.kind == "conv_gate":
                        w0 = PCOL["conv_a"] + 24 * p.l
                        own.wait(ts(CO[:, s, 0:T], flat(U, t, 0, T), col(PV, w0 + t), None, ALU.mult))
                        for j in (1, 2):
                            own.wait(stt(CO[:, s, 0:T], flat(U, t, j, T), col(PV, w0 + 8 * j + t), CO[:, s, 0:T],
                                         ALU.mult, ALU.add))
                        dve.wait_ge(chunk_done[s], done)
                        tt(CI[:, s, 3:3 + T], CO[:, s, 0:T], bank[s][:, 0:T], ALU.mult).then_inc(bank_free[s], 1)
                        cut(p, r, s, looped)
                        dve.wait_ge(sig["high"], p.base["high"] + t + 1)
                        low(flat(Yl, t, 0, T), CI[:, s, 3:3 + T], flat(Yh, t, 0, T)).then_inc(sig["low"], 1)
                        continue
                    if p.kind == "rotate" and s % 2:
                        e = s - 1
                        dve.wait_ge(chunk_done[e], done)
                        dve.wait_ge(chunk_done[s], done)
                        p1, p2 = bank[e][:, 0:T], bank[s][:, 0:T]
                        t1, t2, t3, t4 = CO[:, e, 0:T], CO[:, s, 0:T], CI[:, e, 3:3 + T], CI[:, s, 3:3 + T]
                        tt(t1, p1, cos, ALU.mult)
                        tt(t3, p1, sin, ALU.mult).then_inc(bank_free[e], 1)
                        tt(t2, p2, sin, ALU.mult)
                        tt(t4, p2, cos, ALU.mult).then_inc(bank_free[s], 1)
                        dve.wait_ge(bank_free[s], p.bank[s] + r + 1)
                        dst = RQ if p.name.startswith("r_q") else RK
                        tt(flat(dst, 2 * q, 0, T), t1, t2, ALU.subtract)
                        tt(flat(dst, 2 * q + 1, 0, T), t3, t4, ALU.add).then_inc(sig["mixed"], 1)
                    if p.kind == "gates":
                        dve.wait_ge(bank_free[s], p.bank[s] + r + 1)
                        tt(XC[:, t, :], XC[:, t, :], S8[:, t % 8, 0:SEQ], ALU.mult).then_inc(side["gate_in"], 1)
                        cut(p, r, s, looped)
                        continue
                    if p.norm and p.kind == "act" and (p.per == 1 or s % 2):
                        t = t if p.per == 1 else r * 2 + s // 2
                        dve.wait_ge(bank_free[s], p.bank[s] + r + 1)
                        m = M[:, t, p.off:p.off + T]
                        tt(S8[:, t, p.off:p.off + T], m, m, ALU.mult).then_inc(squares, 1)
                    if p.kind == "dt":
                        cut(p, r, s, looped)
                        continue
                    cut(p, r, s, looped)
                    if p.kind in ("glu", "merge_split") and s % 2:
                        dve.wait_ge(sig["high"], p.base["high"] + q + 1)
                        h, l_ = (Fh, Fl) if p.kind == "glu" else (Mh, Ml)
                        low(flat(l_, q, p.off, T), CO[:, s - 1, 0:T], flat(h, q, p.off, T)).then_inc(sig["low"], 1)
                if p.has_mods(r):
                    for i in range(2):
                        mod_take(p.mods // 2 + r, i)

            def take_values(p, t, s):
                dve.wait_ge(sig["turned"], p.base["turned"] + t + 1)
                V = AV if p.name == "kv_v" else RV if p.name.startswith("r_v") else BV
                b = B[s % 2]
                if isinstance(t, int):
                    cols = slice(t * P, (t + 1) * P)
                else:
                    cols = bass.ds(t * P, P)
                if p.T == TOK:
                    dve.tensor_copy(V[0:16, 2, cols], b[0:16, 2 * P:3 * P])
                dve.tensor_copy(V[:, 0:2, cols], b[:, 0:2 * P].rearrange("p (a n) -> p a n", a=2)).then_inc(sig["copied"], 1)

            def run(name):
                p = by[name]
                per = OWN_WAITS.get(p.kind, 0) * SLOTS
                rounds(dve, p, lambda r, looped: step(p, r, looped), own, per + (14 if p.mods is not None else 0))

            def norm(name, off, n, src, g, shift=None, hi=Hh, lo=Hl):
                if name == "mix1":
                    dve.wait_ge(scaled, 8 * scaled_no[name])
                if shift is not None:
                    scale = shift + 8
                    own.wait(stt(SM[:, GS:GS + 8], MOD[:, scale:scale + 8], 1.0, PV[:, g:g + 8], ALU.add, ALU.mult))
                if name in stat_no:
                    dve.wait_ge(rstd_ready, stat_no[name] + 1)
                for k in range(DT8):
                    w = PV[:, g + k:g + k + 1] if shift is None else SM[:, GS + k:GS + k + 1]
                    if name == "mix1":
                        dve.wait_ge(h_lo, 8 * split_no["kv"] + k + 1)
                    dst = X if name == "final" else S8
                    stt(dst[:, k, off:off + n], src[:, k, off:off + n], w, RSTD[:, 0:n], ALU.mult, ALU.mult)\
                        .then_inc(x_new if name == "final" else scaled, 1)
                    if shift is not None and k:
                        low_h(name, k - 1, off, n, shift, hi, lo)
                if shift is not None:
                    low_h(name, DT8 - 1, off, n, shift, hi, lo)

            def low_h(name, k, off, n, shift, hi, lo):
                dve.wait_ge(h_hi, 8 * split_no[name] + k + 1)
                stt(lo[:, k, off:off + n], S8[:, k, off:off + n], MOD[:, shift + k:shift + k + 1],
                    hi[:, k, off:off + n].bitcast(F32), ALU.add, ALU.subtract).then_inc(h_lo, 1)

            def taken(name):
                for s in range(SLOTS):
                    dve.wait_ge(bank_free[s], by[name].bank_end[s])

            def softplus(z, u, ln, w, d, tmp, dst, no):
                dve.wait_ge(sp_u, no)
                ts(w, u, 1.0, None, ALU.add).then_inc(sp_w, 1)
                dve.wait_ge(sp_w, no)
                own.wait(ts(d, w, -1.0, None, ALU.add))
                own.wait(ts(tmp, d, 1e-30, None, ALU.max))
                own.wait(dve.reciprocal(tmp, tmp))
                own.wait(tt(tmp, tmp, u, ALU.mult))
                dve.wait_ge(sp_ln, no)
                own.wait(tt(tmp, tmp, ln, ALU.mult))
                own.wait(stt(d, d, 0.0, u, ALU.is_equal, ALU.mult))
                own.wait(tt(tmp, tmp, d, ALU.add))
                own.wait(stt(dst, z, 0.0, tmp, ALU.max, ALU.add))

            def recurrence_beside(name):
                p = by[name]
                for r in range(p.rounds):
                    step(p, r, False)
                    for t in range(SLOTS * r, min(SLOTS * (r + 1), LT)):
                        m = M2[:, t, :] if t < 8 else CO[:, t - 8, 0:SEQ]
                        a2 = S8[:, t % 8, 0:SEQ]
                        dve.wait_ge(side["gate_a"], t + 1)
                        own.wait(tt(a2, LA[:, t, :], LA[:, t, :], ALU.mult))
                        stt(m, a2, 1.0, m, ALU.add, ALU.mult).then_inc(side["gate_m2"], 1)
                        if t:
                            scan(t - 1)
                scan(LT - 1)
                for t in range(LT + 1):
                    if t < LT:
                        dve.wait_ge(side["lru_gelu"], t + 1)
                        tt(XC[:, t, :], XC[:, t, :], YB[:, t, :], ALU.mult).then_inc(side["lru_y32"], 1)
                    if t:
                        low_y(t - 1)

            def scan(t):
                dve.wait_ge(side["gate_sqrt"], t + 1)
                m = M2[:, t, :] if t < 8 else CO[:, t - 8, 0:SEQ]
                own.wait(tt(XC[:, t, :], XC[:, t, :], m, ALU.mult))
                own.wait(dve.tensor_tensor_scan(XC[:, t, :], LA[:, t, :], XC[:, t, :], 0.0, ALU.mult, ALU.add))

            def low_y(t):
                dve.wait_ge(side["lru_hi"], t + 1)
                low(XCl[:, t, 0:SEQ], XC[:, t, :], XCh[:, t, 0:SEQ]).then_inc(side["lru_lo"], 1)

            def attention():
                dve.wait_ge(loaded["bias"], 16)

                def logits(h):
                    b = h % 2
                    dve.wait_ge(side["att_s"], h + 1)
                    if h >= 2:
                        dve.wait_ge(side["att_t"], h - 1)
                    stt(AL[:, b, 0:P], B[b][:, 0:P], P ** -0.5, BT[:, h, P:SEQ], ALU.mult, ALU.add)
                    own.wait(stt(AL[:, b, P:], B[b][:, P:384], P ** -0.5, BT[:, h, :], ALU.mult, ALU.add))
                    m = SM[:, AMX + 2 * b:AMX + 2 * b + 2]
                    dve.tensor_reduce(m[:, 0:1], AL[:, b, 0:P], AX.X, ALU.max)
                    own.wait(dve.tensor_reduce(m[:, 1:2], AL[:, b, P:], AX.X, ALU.max))
                    ts(m, m, -1.0, None, ALU.mult).then_inc(side["att_max"], 1)

                def probs(h):
                    b = h % 2
                    dve.wait_ge(side["att_exp"], h + 1)
                    sm = SM[:, ASM + 2 * b:ASM + 2 * b + 2]
                    own.wait(dve.reciprocal(sm, sm))
                    ts(AL[:, b, 0:P], AL[:, b, 0:P], sm[:, 0:1], None, ALU.mult)
                    ts(AL[:, b, P:], AL[:, b, P:], sm[:, 1:2], None, ALU.mult).then_inc(side["att_p"], 1)

                for i in range(10):
                    if i < 8:
                        logits(i)
                    if 1 <= i <= 8:
                        probs(i - 1)
                    if i >= 2:
                        h = i - 2
                        dve.wait_ge(side["side_hi"], h + 1)
                        low(Yl[:, h, META:], B[3][:, 0:SEQ], Yh[:, h, META:]).then_inc(side["side_lo"], 1)

            def step_sizes(l):
                softplus(SD[:, 0, :], SD[:, 1, :], SD[:, 2, :], SD[:, 3, :], SD[:, 4, :], SD[:, 5, :], SD[:, 6, :], 2 + l)
                own.wait(ts(SD[:, 5, :], SD[:, 6, :], SM[0:16, EA + l:EA + l + 1], -1.0, ALU.mult, ALU.mult))
                dve.tensor_tensor_scan(ACS[:, :], ONES[0:16, 0:1].to_broadcast([16, TOK]), SD[:, 5, :], 0.0,
                                       ALU.mult, ALU.add).then_inc(side["dt_acs"], 1)

            def state_space(l):
                dve.wait_ge(side["dt_turned"], l + 1)
                dve.tensor_copy(SM[:, DTT:DTT + 32], B[0][:, 0:32])
                dve.tensor_copy(SM[0:16, DTT + 32:DTT + 48], B[0][0:16, 32:48])
                ts(SM[:, NAT:NAT + 32], B[0][:, 48:80], -1.0, None, ALU.mult)
                ts(SM[0:16, NAT + 32:NAT + 48], B[0][0:16, 80:96], -1.0, None, ALU.mult).then_inc(side["dt_cols"], 1)
                dve.wait_ge(side["dt_cols"], l + 1)
                for m in range(6):
                    n, half = m // 2, m % 2
                    w = KEYS[n][1]
                    dve.wait_ge(side["x_turned"], 6 * l + m + 1)
                    step_size = SM[0:w, DTT + 16 * n + 8 * half:DTT + 16 * n + 8 * half + 8]
                    tt(XT[0:w, n, 512 * half:512 * half + 512].rearrange("p (h d) -> p h d", d=64),
                       B[1 + m % 3][0:w, :].rearrange("p (h d) -> p h d", d=64),
                       step_size.unsqueeze(2).to_broadcast([w, 8, 64]), ALU.mult).then_inc(side["x_scaled"], 1)
                for g in range(4):
                    dve.wait_ge(side["cb_done"], 4 * l + g + 1)
                    tt(CB[:, g, :], B[g][:, 0:PACK], incl, ALU.mult).then_inc(side["cb_masked"], 1)
                dve.wait_ge(side["cb_masked"], 4 * l + 4)

                def take(j):
                    dve.wait_ge(side["head_y"], 16 * l + 2 * j + 2)
                    c = PCOL["ssd_d"] + 8 * l + j
                    stt(S8[:, j, :], XS[:, j, :], PV[:, c:c + 1], B[2 + j % 2][:, 0:TOK], ALU.mult, ALU.add)\
                        .then_inc(side["y_taken"], 1)

                def log_decay(h):
                    b, n16 = h % 2, 16 * l + h
                    dve.wait_ge(side["acs_rows"], n16 + 1)
                    for n, (c, q0, w) in enumerate(SEG):
                        k, c0 = KEYS[n][1], NAT + 16 * n + h
                        ins = ts(SE[0:k, b, c:c + w], B[b][0:k, q0:q0 + w], SM[0:k, c0:c0 + 1], 0.0, ALU.add, ALU.min)
                    ins.then_inc(side["decay_log"], 1)

                def mix(h):
                    b, n16 = h % 2, 16 * l + h
                    dve.wait_ge(side["decay_exp"], n16 + 1)
                    if h >= 2:
                        dve.wait_ge(side["head_y"], n16 - 1)
                    tt(SX[:, b, 0:416], SE[:, b, 0:416], CB[:, h // 4, 0:416], ALU.mult)
                    tt(SX[0:16, b, 416:], SE[0:16, b, 416:], CB[0:16, h // 4, 416:], ALU.mult).then_inc(side["decay_mix"], 1)

                for i in range(17):
                    if i < 16:
                        log_decay(i)
                    if i:
                        mix(i - 1)
                    if i >= 3 and i % 2:
                        take((i - 3) // 2)
                take(7)
                taken(f"s_z{l}")
                dve.wait_ge(side["y_taken"], 8 * l + 8)
                for g in range(4):
                    y = S8[:, 2 * g:2 * g + 2, :]
                    own.wait(tt(y, y, Z[:, 2 * g:2 * g + 2, :], ALU.mult))
                    tt(YQ[:, 2 * g:2 * g + 2, :], y, y, ALU.mult).then_inc(side["y_sq"], 1)
                for g in range(4):
                    dve.wait_ge(side["y_rstd"], 8 * l + g + 1)
                    for t in (2 * g, 2 * g + 1):
                        c = PCOL["ssd_norm"] + 8 * l + t
                        stt(S8[:, t, :], S8[:, t, :], PV[:, c:c + 1], YR[:, g, :], ALU.mult, ALU.mult)\
                            .then_inc(side["y32"], 1)
                        if t:
                            low_side(8 + 24 * l, t - 1)
                low_side(8 + 24 * l, 7)

            def low_side(before, t):
                dve.wait_ge(side["side_hi"], before + t + 1)
                low(Yl[:, t, :], S8[:, t, :], Yh[:, t, :]).then_inc(side["side_lo"], 1)

            def retention(l):
                for h in range(4):
                    dve.wait_ge(side["ret_s"], 4 * l + h + 1)
                    if h >= 2:
                        dve.wait_ge(side["ret_y"], 8 * l + 2 * (h - 1))
                    c = CCOL["decay"] + h * PACK
                    tt(RP[:, h % 2, :], B[h % 2][:, 0:PACK], CS[:, c:c + PACK], ALU.mult).then_inc(side["ret_p"], 1)
                for h in range(4):
                    dve.wait_ge(side["ret_mean"], 4 * l + h + 1)
                    for t in (2 * h, 2 * h + 1):
                        ins = stt(S8[:, t, :], B[h][:, 0:TOK], -1.0 / 256, S8[:, t, :], ALU.mult, ALU.add)
                    own.wait(ins)
                    y = S8[:, 2 * h:2 * h + 2, :]
                    tt(YQ[:, 2 * h:2 * h + 2, :], y, y, ALU.mult).then_inc(side["y_sq"], 1)
                taken(f"r_g{l}")
                dve.wait_ge(side["y_sq"], 8 * l + 8)
                own.wait(tt(S8[:, :, :], S8[:, :, :], RG[:, :, :], ALU.mult))
                for h in range(4):
                    dve.wait_ge(side["y_rstd"], 8 * l + 4 + h + 1)
                    for t in (2 * h, 2 * h + 1):
                        tt(S8[:, t, :], S8[:, t, :], YR[:, h, :], ALU.mult).then_inc(side["y32"], 1)
                        if t:
                            low_side(16 + 24 * l, t - 1)
                low_side(16 + 24 * l, 7)

            def stick_breaking(l):
                for i in range(10):
                    n8 = 8 * l + i
                    if i < 8:
                        b = i % 2
                        dve.wait_ge(side["sb_soft"], n8 + 1)
                        if i >= 2:
                            dve.wait_ge(side["sb_r"], n8 - 1)
                        own.wait(stt(SS[:, b, :], ZS[:, b, :], 0.0, SA[:, b, :], ALU.max, ALU.add))
                        tt(SS[:, b, :], SS[:, b, :], strict, ALU.mult).then_inc(side["sb_sp"], 1)
                    if 1 <= i <= 8:
                        b = (i - 1) % 2
                        dve.wait_ge(side["sb_r"], n8)
                        if i >= 3:
                            dve.wait_ge(side["sb_o"], n8 - 2)
                        own.wait(tt(SW[:, b, :], ZS[:, b, :], B[2][:, 0:PACK], ALU.subtract))
                        ts(SW[:, b, :], SW[:, b, :], 0.0, None, ALU.min).then_inc(side["sb_logw"], 1)
                        dve.wait_ge(side["sb_we"], n8)
                        tt(SW[:, b, :], SW[:, b, :], strict, ALU.mult).then_inc(side["sb_w"], 1)
                    if i >= 2:
                        h = i - 2
                        dve.wait_ge(side["side_hi"], 24 + 24 * l + h + 1)
                        low(Yl[:, h, :], B[3][:, 0:TOK], Yh[:, h, :]).then_inc(side["side_lo"], 1)

            dve.memset(ONES[:, :], 1.0)
            dve.memset(CI[:, :, 0:3], 0.0)
            dve.memset(SM[:, EPSC:EPSC + 1], EPS).then_inc(sig["copied"], 2)
            dve.wait_ge(sig["copied"], 2)
            dve.memset(SM[:, EPSC + 1:EPSC + 2], 1e-37).then_inc(const_ready, 1)
            dve.wait_ge(loaded["params"], 16)
            c = PCOL["lru_lambda"]
            ts(SM[:, SPT:SPT + LT], PV[:, c:c + LT], -1.0, None, ALU.mult).then_inc(const_ready, 1)
            dve.wait_ge(silu_c, 1)
            for u in range(FIRST + 1):
                if u < FIRST:
                    mod_unit(u // 2, u % 2)
                if u:
                    mod_take((u - 1) // 2, (u - 1) % 2)
            dve.wait_ge(mod_taken, FIRST)
            norm("mix0", META, SEQ, X, PCOL["norm_mix"], 0)
            for s in (0, 2):
                dve.wait_ge(hi_ready[s], 1)
                low_w(s, DT8)
            sp = SM[:, SPW + 30:SPW + 40]
            softplus(SM[:, SPT:SPT + LT], SM[:, SPW:SPW + 10], SM[:, SPW + 20:SPW + 30], SM[:, SPW + 10:SPW + 20],
                     sp, SM[:, DTT:DTT + LT], SM[:, DTT + 16:DTT + 16 + LT], 1)
            ts(SM[:, SPL:SPL + LT], SM[:, DTT + 16:DTT + 16 + LT], -8.0, None, ALU.mult)
            own.wait(ts(SM[:, SPT:SPT + LT], SM[:, DTT + 16:DTT + 16 + LT], 8.0, None, ALU.mult))
            dve.wait_ge(side["bias_sum"], 1)
            own.wait(dve.tensor_copy(BR[:, :], B[1][0:8, 0:BIASW]))
            dve.memset(BR[:, SEQ:], -1e30).then_inc(side["bias_row"], 1)
            run("lru_x")
            run("lru_gates")
            recurrence_beside("lru_y")
            run("lru_out")
            norm("ffn0", META, SEQ, X, PCOL["norm_ffn"], 24)
            run("ffn_up0")
            run("ffn_down0")
            norm("kv", META, SEQ, X, PCOL["kv_norm"], 48, Yh, Yl)
            norm("mix1", META, SEQ, X, PCOL["norm_mix"] + 8, 64)
            run("kv_k")
            run("kv_v")
            run("q")
            attention()
            run("attn_out")
            norm("ffn1", META, SEQ, X, PCOL["norm_ffn"] + 8, 88)
            run("ffn_up1")
            run("ffn_down1")
            dve.wait_ge(loaded["meta"], 16)
            dve.wait_ge(loaded["heads"], 16)
            norm("final", META, SEQ, X, PCOL["final_norm"])
            for l in range(2):
                off, n = (META, SEQ) if l else (0, TOK)
                norm(f"pre{l}", 0, TOK, X, PCOL["norm_mix_pre"] + 8 * l)
                dve.memset(U[:, :, 0:2], 0.0)
                run(f"a_cx{l}")
                for s in range(SLOTS):
                    dve.wait_ge(bank_free[s], by[f"a_cx{l}"].bank_end[s])
                run(f"a_b{l}")
                run(f"up_a{l}")
                run(f"dt{l}")
                step_sizes(l)
                dve.memset(BC[:, 0:4, TOK:], 0.0)
                run(f"s_x{l}")
                run(f"s_bc{l}")
                run(f"s_z{l}")
                state_space(l)
                run(f"up_b{l}")
                dve.memset(RK[:, :, TOK:], 0.0)
                run(f"r_v{l}")
                run(f"r_q{l}")
                run(f"r_k{l}")
                run(f"r_g{l}")
                retention(l)
                run(f"up_c{l}")
                dve.memset(BK[:, :, TOK:], 0.0)
                run(f"b_v{l}")
                run(f"b_k{l}")
                run(f"b_q{l}")
                stick_breaking(l)
                run(f"up_d{l}")
                run(f"mix_out{l}")
                norm(f"post{l}", off, n, M, PCOL["norm_mix_post"] + 8 * l)
                norm(f"fpre{l}", off, n, X, PCOL["norm_ffn_pre"] + 8 * l)
                run(f"ffn_up{2 + l}")
                run(f"ffn_down{2 + l}")
                norm(f"fpost{l}", off, n, M, PCOL["norm_ffn_post"] + 8 * l)


def chunks(w, kb=8):
    k, m = w.shape
    w = w.reshape(k // (kb * P), kb, P, m // P, P)
    return w.transpose(3, 0, 2, 1, 4).reshape(-1, P, kb * P)


def pairs(u, v):
    return np.stack([u, v], axis=1).reshape(-1, *u.shape[1:])


def constants():
    cs = np.zeros((P, CCOLS), np.float32)
    cs[:, CCOL["ident"]:CCOL["ident"] + P] = np.eye(P)
    cs[:, CCOL["suffix"]:CCOL["suffix"] + P] = np.tril(np.ones((P, P)))
    gamma = np.log(1.0 - 2.0 ** (-5.0 - np.arange(4, dtype=np.float64)))
    for (c, q0, w), (k0, kn) in zip(SEG, KEYS):
        key, query = k0 + np.arange(kn)[:, None], q0 + np.arange(w)[None, :]
        cs[:kn, CCOL["incl"] + c:CCOL["incl"] + c + w] = key <= query
        cs[:kn, CCOL["strict"] + c:CCOL["strict"] + c + w] = key < query
        for h in range(4):
            at = CCOL["decay"] + h * PACK + c
            cs[:kn, at:at + w] = np.where(key <= query, np.exp(gamma[h] * np.maximum(query - key, 0)), 0) / 16
    pos = np.arange(P - META, P + SEQ).astype(np.float32)
    inv = np.float32(10000.0) ** (-np.arange(P, dtype=np.float32) / np.float32(P))
    ang = (pos[None, :] * inv[:, None]).astype(np.float32)
    cs[:, CCOL["cos"]:CCOL["cos"] + TOK] = np.cos(ang)
    cs[:, CCOL["sin"]:CCOL["sin"] + TOK] = np.sin(ang)
    dist = SEQ - 1 - np.arange(BIASW)
    d = np.maximum(dist, 1).astype(np.float32)
    large = 16 + (np.log(d / np.float32(16)) / np.float32(np.log(128 / 16)) * np.float32(16)).astype(np.int32)
    bucket = np.where(dist < 16, dist, np.minimum(large, 31))
    onehot = (np.arange(32)[:, None] == bucket[None, :]) & (dist >= 0)[None, :]
    return cs, onehot.astype(np.float32)


def columns(v):
    return v.reshape(-1, P).T


def layout(i):
    f = {n: np.asarray(v) for n, v in i.items()}
    a = {}
    a["x"] = f["x"][0].reshape(SEQ, DT8, P).transpose(2, 1, 0)
    a["meta"] = f["meta_2"].reshape(META, DT8, P).transpose(2, 1, 0)
    a["consts"], a["onehot"] = constants()
    a["rel_bias"] = f["rel_bias"].T
    a["heads"] = np.stack([f["ssd_dt_bias_2"][0], f["ssd_a_log_2"][0], f["ssd_dt_bias_2"][1], f["ssd_a_log_2"][1]], axis=1)
    mod = np.concatenate([f["mod_w"][0], f["kv_mod_w"], f["mod_w"][1]], axis=1)
    a["mod_w"] = mod.reshape(8, P, MOD_UNITS, MU).transpose(2, 1, 0, 3)
    src = {"c": f["c"], "mod_b": np.concatenate([f["mod_b"][0], f["kv_mod_b"], f["mod_b"][1]]),
           "ssd_d": np.repeat(f["ssd_d_2"], 64, axis=1), "lru_conv_w": f["lru_conv_w"][0], "lru_conv_b": f["lru_conv_b"],
           "lru_b_gates": f["lru_b_gates"][0], "lru_lambda": f["lru_lambda"]}
    cols = []
    for name, w in PARAMS:
        v = src[name] if name in src else f[name] if name in f else f[name + "_2"]
        v = columns(v)
        assert v.shape == (P, w), (name, v.shape)
        cols.append(v)
    a["params"] = np.concatenate(cols, axis=1)
    w = chunks(f["lru_w_in"][0])
    a["lru_y"], a["lru_x"] = w[:LT], w[LT:]
    g = f["lru_w_gates"][0].reshape(5, 2, P, 2, 2, P)
    a["lru_gates"] = g.transpose(0, 4, 2, 3, 1, 5).reshape(LT, P, 4 * P)
    a["lru_out"] = chunks(f["lru_w_out"][0], 10)
    kv = chunks(f["w_kv"])
    a["kv_k"], a["kv_v"] = kv[:4], kv[4:]
    a["q"], a["attn_out"] = chunks(f["attn_w_q"][0]), chunks(f["attn_w_o"][0])
    for l in range(2):
        a[f"ffn_up{l}"] = pairs(chunks(f["ffn_w_gate"][l]), chunks(f["ffn_w_up"][l]))
        a[f"ffn_down{l}"] = chunks(f["ffn_w_down"][l], 11)
    for l in range(2):
        w, at = f["w_in_2"][l], [0]

        def take(n):
            at[0] += n
            return w[:, at[0] - n:at[0]]

        b, c, x, z, xs, bc, dt = (take(n) for n in (D, D, D, D, D, D, 16))
        rq, rk, rv, rg, bq, bk, bv, gates = (take(n) for n in (D,) * 7 + (4 * D,))
        a[f"a_cx{l}"], a[f"a_b{l}"] = pairs(chunks(c), chunks(x)), chunks(b)
        a[f"dt{l}"] = chunks(np.concatenate([dt, np.zeros((D, P - 16), dt.dtype)], axis=1))
        for n, v in (("s_x", xs), ("s_bc", bc), ("s_z", z), ("r_v", rv), ("r_q", rq), ("r_k", rk), ("r_g", rg),
                     ("b_v", bv), ("b_k", bk), ("b_q", bq)):
            a[n + str(l)] = chunks(v)
        for j, n in enumerate("abcd"):
            a[f"up_{n}{l}"] = pairs(chunks(gates[:, j * D:(j + 1) * D]), chunks(f["w_branch_2"][l, j]))
        a[f"mix_out{l}"] = chunks(f["w_out_2"][l])
        up = f["w_ffn_in_2"][l]
        a[f"ffn_up{2 + l}"] = pairs(chunks(up[:, :FF]), chunks(up[:, FF:]))
        a[f"ffn_down{2 + l}"] = chunks(f["w_ffn_out_2"][l], 11)
    return {n: np.ascontiguousarray(v) for n, v in a.items()}


def kernel(**inputs):
    import concourse.bacc as bacc
    from concourse.bass_utils import run_bass_kernel_spmd

    nc = bacc.Bacc("TRN2", target_bir_lowering=False, num_devices=1)
    arrays, aps = {}, {}
    for name, v in layout(inputs).items():
        arrays["in_" + name] = v
        aps[name] = nc.dram_tensor("in_" + name, v.shape, mybir.dt.from_np(v.dtype), kind="ExternalInput").ap()
    out = nc.dram_tensor("out", (P, DT8, SEQ), F32, kind="ExternalOutput").ap()
    two_layer_pair(nc, aps, out)
    r = run_bass_kernel_spmd(nc, [arrays], core_ids=[0])
    return r.results[0]["out"].transpose(2, 1, 0).reshape(1, SEQ, D)
```

```python
from contextlib import ExitStack

import numpy as np
import concourse.bass as bass
from concourse import mybir

F32 = mybir.dt.float32
F32R = mybir.dt.float32r
ALU = mybir.AluOpType
ACT = mybir.ActivationFunctionType
AX = mybir.AxisListType

P = 128
D = 1024
SEQ = 256
META = 16
TOK = META + SEQ
DT8 = D // P
LRU = 1280
LT = LRU // P
FF = 2816
FT = FF // P
EPS = 1e-6
SLOTS = 4
KEYS = ((0, 128), (128, 128), (256, 16))
SEG = ((0, 0, 272), (272, 128, 144), (416, 256, 16))
PACK = 432

MU = 256
MOD_SECTIONS = 14
MOD_UNITS = MOD_SECTIONS * D // MU
FIRST = 2 * D // MU

PARAMS = [("c", 8), ("norm_mix", 16), ("norm_ffn", 16), ("kv_norm", 8), ("final_norm", 8),
          ("lru_conv_w", 40), ("lru_conv_b", 10), ("lru_b_gates", 20), ("lru_lambda", 10),
          ("norm_mix_pre", 16), ("norm_mix_post", 16), ("norm_ffn_pre", 16), ("norm_ffn_post", 16),
          ("conv_a", 48), ("ssd_conv_w", 128), ("ssd_conv_b", 32), ("ssd_norm", 16), ("ssd_d", 16)]
PCOL, _n = {}, 0
for _name, _w in PARAMS:
    PCOL[_name] = _n
    _n += _w
PCOLS = _n

CONSTS = [("ident", 128), ("suffix", 128), ("incl", PACK), ("strict", PACK), ("decay", 4 * PACK),
          ("cos", TOK), ("sin", TOK)]
CCOL, _n = {}, 0
for _name, _w in CONSTS:
    CCOL[_name] = _n
    _n += _w
CCOLS = _n
BIASW = 384


class Phase:

    def __init__(self, name, kind, n, rhs="H", kb=8, off=0, T=TOK, per=1, l=0, mods=None, t0=0, norm=None):
        self.name, self.kind, self.n, self.kb, self.rhs = name, kind, n, kb, rhs
        self.off, self.T, self.per, self.l, self.mods, self.t0, self.norm = off, T, per, l, mods, t0, norm
        self.rounds, self.s0 = -(-n // SLOTS), 0
        pair = kind in ("glu", "cx", "merge", "merge_split", "rotate")
        self.units = n // 2 if pair else n // per
        self.count = {s: self.units for s in SIGNALS.get(kind, ())}

    def has_mods(self, r):
        return self.mods is not None and (not isinstance(r, int) or self.mods + 2 * r < MOD_UNITS)

    def slots(self, r, looped):
        n = SLOTS if looped else min(SLOTS, self.n - SLOTS * r)
        return [(i + self.s0) % SLOTS for i in range(n)]


SIGNALS = {"conv_split": ("mixed", "high", "low"), "conv_silu": ("mixed", "high"), "vtok": ("turned", "copied"),
           "glu": ("high", "low"), "conv_gate": ("high", "low"), "merge_split": ("mixed", "high", "low"),
           "rotate": ("mixed",)}
OWN_WAITS = {"conv_split": 3, "conv_silu": 2, "conv_gate": 3}


def plan():
    seq = dict(off=META, T=SEQ)
    ph = [Phase("lru_x", "conv_split", 10, mods=8, **seq), Phase("lru_gates", "gates", 10, "XC", kb=4, **seq),
          Phase("lru_y", "act", 10, mods=14, **seq),
          Phase("lru_out", "resid", 8, "XC", kb=10, norm="ffn0", **seq),
          Phase("ffn_up0", "glu", 44, mods=20, **seq),
          Phase("ffn_down0", "resid", 16, "F", kb=11, per=2, mods=42, norm="kv", **seq),
          Phase("kv_k", "act", 4, "Y", mods=50, **seq), Phase("kv_v", "vtok", 4, "Y", mods=52, **seq),
          Phase("q", "act", 8, **seq),
          Phase("attn_out", "resid", 8, "Y", mods=54, norm="ffn1", **seq), Phase("ffn_up1", "glu", 44, **seq),
          Phase("ffn_down1", "resid", 16, "F", kb=11, per=2, norm="final", **seq)]
    for l in range(2):
        tail = seq if l else {}
        ph += [Phase(f"a_cx{l}", "cx", 16, l=l), Phase(f"a_b{l}", "conv_gate", 8, l=l),
               Phase(f"up_a{l}", "merge", 16, "HY", l=l, **tail),
               Phase(f"dt{l}", "dt", 1, l=l), Phase(f"s_x{l}", "conv_silu", 8, l=l),
               Phase(f"s_bc{l}", "conv_silu", 8, l=l, t0=8), Phase(f"s_z{l}", "act", 8, l=l),
               Phase(f"r_q{l}", "rotate", 8, l=l), Phase(f"r_k{l}", "rotate", 8, l=l),
               Phase(f"up_b{l}", "merge", 16, "HY", l=l, **tail),
               Phase(f"r_v{l}", "vtok", 8, l=l), Phase(f"r_g{l}", "act", 8, l=l),
               Phase(f"up_c{l}", "merge", 16, "HY", l=l, **tail),
               Phase(f"b_v{l}", "vtok", 8, l=l), Phase(f"b_kq{l}", "act", 16, l=l),
               Phase(f"up_d{l}", "merge_split", 16, "HY", l=l, **tail),
               Phase(f"mix_out{l}", "act", 8, "M", l=l, norm=f"post{l}", **tail),
               Phase(f"ffn_up{2 + l}", "glu", 44, l=l, **tail),
               Phase(f"ffn_down{2 + l}", "act", 16, "F", kb=11, per=2, l=l, norm=f"fpost{l}", **tail)]
    count = {s: 0 for s in ("mixed", "high", "low", "turned", "copied")}
    slot, bank = [0] * SLOTS, [0] * SLOTS
    for prev, p in zip([ph[0]] + ph, ph):
        p.s0 = (prev.s0 + prev.n) % SLOTS if p is not prev and (p.n % SLOTS or p.norm) and p.per == 1 else 0
        p.base = dict(count)
        for s, c in p.count.items():
            count[s] += c
        p.end = dict(count)
        p.slot, p.bank = list(slot), list(bank)
        for c in range(p.n):
            slot[(c + p.s0) % SLOTS] += 1
            if p.per == 1 or c % 2:
                bank[(c + p.s0) % SLOTS] += 1
        p.bank_end = list(bank)
    later = [[] for _ in range(SLOTS)]
    for p in reversed(ph):
        p.next_kb = {}
        for c in reversed(range(p.n)):
            s = (c + p.s0) % SLOTS
            p.next_kb[c // SLOTS, s] = later[s][-1] if later[s] else None
            later[s].append(p.kb)
        p.looped = p.rounds
        if p.n % SLOTS or p.s0:
            p.looped = 0
        elif any(p.next_kb[p.rounds - 1, s] != p.kb for s in range(SLOTS)):
            p.looped = p.rounds - 1
        if p.looped < 2 or p.norm:
            p.looped = 0
    return ph


class Own:

    def __init__(self, eng, sem):
        self.eng, self.sem, self.n, self.start, self.in_loop = eng, sem, 0, 0, None

    def mark(self, ins):
        self.n += 1
        ins.then_inc(self.sem, 1)

    def wait(self, ins=None, back=0):
        if ins is not None:
            self.mark(ins)
        at = self.n if self.in_loop is None else self.start + self.in_loop + self.n
        self.eng.wait_ge(self.sem, at - back)


def rounds(eng, p, step, own=None, per_round=0):
    if p.looped:
        if own is not None:
            own.start, own.n = own.n, 0
        with eng.Fori(0, p.looped) as r:
            if own is not None:
                own.in_loop = r * per_round
            step(r, True)
        if own is not None:
            assert own.n == per_round, (p.name, own.n, per_round)
            own.in_loop, own.n = None, own.start + p.looped * per_round
    for r in range(p.looped, p.rounds):
        step(r, False)


def flat(buf, t, off, n):
    if len(buf.shape) == 2:
        pitch = 384 if buf.shape[1] == 8 * 384 else TOK
        at = t * pitch + off
        return buf[:, at:at + n] if isinstance(t, int) else buf[:, bass.ds(at, n)]
    if isinstance(t, int):
        return buf[:, t, off:off + n]
    return buf[:, bass.ds(t, 1), off:off + n].rearrange("p a n -> p (a n)")


def col(buf, c):
    return buf[:, c:c + 1] if isinstance(c, int) else buf[:, bass.ds(c, 1)]


def two_layer_pair(nc, a, out):
    ph = plan()
    by = {p.name: p for p in ph}
    ctx = ExitStack()
    with ctx:
        base = nc.sbuf_base + 31 & ~31
        top = [base]

        def place(name, shape, dt=F32, at=None):
            size = int(np.prod(shape[1:])) * 4
            if at is None:
                at = top[0]
                top[0] = at + (size + 31 & ~31)
            assert at + size <= nc.sbuf_usable_end, (name, at + size - nc.sbuf_usable_end)
            return nc.alloc_sbuf_tensor_at(name, shape, dt, offset=at)

        raw = place("raw", [P, SLOTS, 11 * P])
        w_hi = place("w_hi", [P, SLOTS, 11 * P], F32R)
        w_lo = place("w_lo", [P, SLOTS, 11 * P], F32R)
        X = place("x_res", [P, DT8, TOK])
        Hh = place("h_hi", [P, DT8, TOK], F32R)
        Hl = place("h_lo", [P, DT8, TOK], F32R)
        S8 = place("scratch8", [P, DT8, TOK])
        m_at = top[0]
        M = place("merged", [P, DT8, TOK])
        BT = place("bias_t", [P, 8, SEQ], at=m_at)
        M2 = place("lru_m2", [P, LT - 2, SEQ], at=m_at)
        OH = place("onehot", [32, BIASW], at=m_at)
        RB = place("rel_bias", [32, 8], at=m_at + 4 * BIASW)
        BR = place("bias_row", [8, BIASW], at=m_at + 8 * BIASW)
        CI = place("conv_in", [P, SLOTS, TOK + 4])
        CO = place("conv_out", [P, SLOTS, TOK])
        ACS = place("acs", [16, TOK])
        RSTD = place("rstd", [P, TOK])
        PV = place("params", [P, PCOLS])
        CS = place("consts", [P, CCOLS])
        ONES = place("ones", [P, P])
        MOD = place("mod", [P, MOD_SECTIONS * 8])
        SM = place("small", [P, 188])
        region = top[0]

        def tiles(name, shape, tile, dt=F32):
            return place(name, shape, dt, at=region + (int(tile * TOK) * 4 + 31 & ~31))

        Fh, Fl = tiles("f_hi", [P, FT, TOK], 0, F32R), tiles("f_lo", [P, FT, TOK], FT, F32R)
        MW = tiles("mod_raw", [P, 2, 8, MU], 52)
        ACC = tiles("mod_acc", [P, 2, MU], 50)
        MW8 = tiles("mod_raw_first", [P, FIRST, 8, MU], 0)
        ACC8 = place("mod_acc_first", [P, 2, MU], at=m_at + 12 * BIASW)
        XCh, XCl = tiles("xc_hi", [P, LT, TOK], 0, F32R), tiles("xc_lo", [P, LT, TOK], LT, F32R)
        YB, XC = tiles("y_branch", [P, LT, SEQ], 20), tiles("xc", [P, LT, SEQ], 30)
        LA = tiles("lru_a", [P, LT, SEQ], 40)
        Yh, Yl = tiles("y_hi", [P, DT8, TOK], 0, F32R), tiles("y_lo", [P, DT8, TOK], 8, F32R)
        AK, AQ = tiles("a_k", [P, 4, SEQ], 16), tiles("a_q", [P, 8, SEQ], 20)
        AV = tiles("a_v", [P, 2, 512], 28)
        AL, APT = tiles("a_logits", [P, 2, 384], 32), tiles("a_probs_t", [P, 2, 384], 35)
        U = tiles("u", [P, DT8, TOK + 2], 16)
        XS, BC, Z = tiles("s_xs", [P, 8, TOK], 16), tiles("s_bc", [P, 8 * TOK], 24), tiles("s_z", [P, 8, TOK], 32)
        XT = tiles("s_xdt", [P, 3, D], 40)
        CB = tiles("s_cb", [P, 4, PACK], 0)
        SE, SX = tiles("s_decay", [P, 2, PACK], 6.4), tiles("s_mix", [P, 2, PACK], 9.6)
        SD = tiles("s_dt", [16, 7, TOK], 6.4)
        YQ = {"ssd": tiles("y_squares", [P, 8, TOK], 24), "ret": tiles("r_squares", [P, 8, TOK], 43.2)}
        YR = {"ssd": tiles("y_roots", [P, 4, TOK], 40), "ret": tiles("r_roots", [P, 4, TOK], 39.2)}
        RQ, RK = tiles("r_q", [P, 8 * TOK], 51.3), tiles("r_k", [P, 8 * TOK + P - 16], 59.3)
        RV, RG, RP = tiles("r_v", [P, 3, D], 16), tiles("r_g", [P, 8, TOK], 28), tiles("r_p", [P, 2, PACK], 36)
        BK, BV, BQ = tiles("b_k", [P, 8 * 384], 16), tiles("b_v", [P, 3, D], 28), tiles("b_q", [P, 8 * TOK], 40)
        ZS, SA, SS, SW = (tiles(n, [P, 2, PACK], 48 + 4 * i) for i, n in enumerate(("b_z", "b_a", "b_s", "b_w")))
        Mh, Ml = tiles("m_hi", [P, DT8, TOK], 16, F32R), tiles("m_lo", [P, DT8, TOK], 24, F32R)

        bank = [ctx.enter_context(nc.psum_tensor(f"stream{i}", [P, 512], F32)) for i in range(SLOTS)]
        B = [ctx.enter_context(nc.psum_tensor(f"side{i}", [P, 512], F32)) for i in range(4)]

        def sem(name):
            return ctx.enter_context(nc.semaphore(name))

        raw_ready = [sem(f"raw_ready{i}") for i in range(SLOTS)]
        hi_ready = [sem(f"hi_ready{i}") for i in range(SLOTS)]
        lo_ready = [sem(f"lo_ready{i}") for i in range(SLOTS)]
        chunk_done = [sem(f"chunk_done{i}") for i in range(SLOTS)]
        bank_free = [sem(f"bank_free{i}") for i in range(SLOTS)]
        sig = {s: sem(s) for s in ("mixed", "high", "low", "turned", "copied")}
        vec_own, act_own = sem("vec_own"), sem("act_own")
        loaded = {n: sem(f"loaded_{n}") for n in ("params", "mod_b", "consts", "x", "meta", "heads", "onehot", "bias")}
        pool_own = sem("pool_own")
        const_ready, silu_c = sem("const_ready"), sem("silu_c")
        mod_ready = [sem(f"mod_ready{i}") for i in range(2)]
        mod_first = [sem(f"mod_first{i}") for i in range(FIRST)]
        mod_acc = [sem(f"mod_acc{i}") for i in range(2)]
        mod_sum, mod_taken = sem("mod_sum"), sem("mod_taken")
        squares_added = sem("squares_added")
        squares, sum_done, rstd_ready = sem("squares"), sem("sum_done"), sem("rstd_ready")
        scaled, h_hi, h_lo, x_new = sem("scaled"), sem("h_hi_ready"), sem("h_lo_ready"), sem("x_new")
        sp_u, sp_w, sp_ln = sem("sp_u"), sem("sp_w"), sem("sp_ln")
        side = {n: sem(n) for n in (
            "gate_tanh", "gate_in", "gate_a", "gate_m2", "gate_sqrt", "lru_gelu", "lru_y32", "lru_hi", "lru_lo",
            "bias_sum", "bias_row", "bias_out", "att_s", "att_max", "att_exp", "att_p", "att_t", "att_pt",
            "att_o", "side_hi", "side_lo",
            "dt_acs", "dt_turned", "dt_cols", "x_turned", "x_scaled", "cb_done", "cb_masked",
            "acs_rows", "decay_log", "decay_exp", "decay_mix", "head_y", "y_taken", "y_sq", "y_sum", "y_rstd", "y32",
            "ret_s", "ret_p", "ret_y", "ret_copy", "ret_mean", "sb_s", "sb_z", "sb_soft", "sb_sp", "sb_r",
            "sb_logw", "sb_w", "sb_we", "sb_o")}
        stored, tapped = sem("stored"), sem("tapped")

        norms = ["mix0", "ffn0", "kv", "mix1", "ffn1", "final"] + [n + str(l) for l in range(2)
                                                                   for n in ("pre", "post", "fpre", "fpost")]
        to_x = ["final", "post0", "fpost0", "post1", "fpost1"]
        stat_no = {n: i for i, n in enumerate(n for n in norms if n != "mix1")}
        split_no = {n: i for i, n in enumerate(n for n in norms if n not in to_x)}
        scaled_no = {n: i for i, n in enumerate(n for n in norms if n != "final")}
        x_no = {n: i for i, n in enumerate(to_x)}
        added_no = {p.norm: i for i, p in enumerate(p for p in ph if p.norm)}

        rhs_of = {"H": (Hh, Hl), "XC": (XCh, XCl), "F": (Fh, Fl), "Y": (Yh, Yl), "M": (Mh, Ml)}
        ident = CS[:, CCOL["ident"]:CCOL["ident"] + P]
        suffix = CS[:, CCOL["suffix"]:CCOL["suffix"] + P]
        incl = CS[:, CCOL["incl"]:CCOL["incl"] + PACK]
        strict = CS[:, CCOL["strict"]:CCOL["strict"] + PACK]
        cos, sin = (CS[:, CCOL[n]:CCOL[n] + TOK] for n in ("cos", "sin"))
        CSC, GS, SPL, SPT, SPW, DTT, NAT, AMX, ASM, EAL, EPSC, EA = 0, 8, 16, 26, 36, 76, 124, 172, 176, 180, 184, 186
        bias_rows = nc.dram_tensor("bias_rows", (8, P, BIASW), F32, kind="Internal").ap()

        def gen(p, r, s):
            return p.slot[s] + r

        block = ctx.enter_context(nc.Block())

        @block.sync
        def _(sp):
            sp.dma_start(PV[:, :], a["params"]).then_inc(loaded["params"], 16)
            sp.dma_start(MOD[:, :], a["mod_b"]).then_inc(loaded["mod_b"], 16)
            sp.dma_start(X[:, :, META:], a["x"]).then_inc(loaded["x"], 16)
            for u in range(FIRST):
                sp.dma_start(MW8[:, u, :, :], a["mod_w"][u]).then_inc(mod_first[u], 16)
            sp.dma_start(OH[:, :], a["onehot"]).then_inc(loaded["onehot"], 16)
            sp.dma_start(RB[:, :], a["rel_bias"]).then_inc(loaded["onehot"], 16)

            def load(p, r, looped):
                for i, s in enumerate(p.slots(r, looped)):
                    if p.name != ph[0].name or r:
                        sp.wait_ge(lo_ready[s], gen(p, r, s))
                    w = a[p.name]
                    src = w[r * SLOTS + i] if isinstance(r, int) else \
                        w[bass.ds(r * SLOTS + i, 1)].rearrange("c p n -> (c p) n")
                    sp.dma_start(raw[:, s, 0:p.kb * P], src).then_inc(raw_ready[s], 16)

            for p in ph:
                rounds(sp, p, lambda r, looped: load(p, r, looped))
                if p.name == "lru_x":
                    sp.wait_ge(side["bias_row"], 1)
                    sp.dma_start(bias_rows, BR[:, :].unsqueeze(1).to_broadcast([8, P, BIASW])).then_inc(side["bias_out"], 16)
                if p.name == "lru_out":
                    sp.dma_start(CS[:, :], a["consts"]).then_inc(loaded["consts"], 16)
                    sp.dma_start(X[:, :, 0:META], a["meta"]).then_inc(loaded["meta"], 16)
                    sp.dma_start(SM[0:16, EAL:EAL + 4], a["heads"]).then_inc(loaded["heads"], 16)
                    sp.wait_ge(side["bias_out"], 16)
                    sp.wait_ge(side["lru_lo"], LT)
                    sp.dma_start(BT[:, :, :], bass.AP(tensor=bias_rows.tensor, offset=P - 1,
                                                      ap=[[BIASW - 1, P], [P * BIASW, 8], [1, SEQ]])).then_inc(loaded["bias"], 16)
            for k in range(DT8):
                sp.wait_ge(x_new, 8 * x_no["fpost1"] + k + 1)
                sp.dma_start(out[:, k, :], X[:, k, META:]).then_inc(stored, 16)
            sp.wait_ge(stored, 16 * DT8)

        @block.gpsimd
        def _(pool):
            def load_mod(m):
                for i in range(2):
                    if not isinstance(m, int) or m > FIRST // 2:
                        pool.wait_ge(mod_acc[i], m)
                    src = a["mod_w"][2 * m + i] if isinstance(m, int) else \
                        a["mod_w"][bass.ds(2 * m + i, 1)].rearrange("u p k n -> (u p) k n")
                    pool.dma_start(MW[:, i, :, :], src).then_inc(mod_ready[i], 16)

            def step(p, r, looped):
                if p.has_mods(r) and (not isinstance(r, int) or p.mods // 2 + r + 1 < MOD_UNITS // 2):
                    load_mod(p.mods // 2 + r + 1)
                for s in (s for s in p.slots(r, looped) if s % 2):
                    kb = p.kb if looped else p.next_kb[r, s]
                    if kb is not None:
                        pool.wait_ge(hi_ready[s], gen(p, r, s) + 2)
                        low_w(s, kb)

            def low_w(s, kb):
                pool.tensor_tensor(w_lo[:, s, 0:kb * P], raw[:, s, 0:kb * P], w_hi[:, s, 0:kb * P].bitcast(F32),
                                   ALU.subtract).then_inc(lo_ready[s], 1)

            def run(name):
                p = by[name]
                rounds(pool, p, lambda r, looped: step(p, r, looped))

            def low_h(name, off, n):
                for k in range(DT8):
                    pool.wait_ge(h_hi, 8 * split_no[name] + k + 1)
                    pool.tensor_tensor(Hl[:, k, off:off + n], S8[:, k, off:off + n], Hh[:, k, off:off + n].bitcast(F32),
                                       ALU.subtract).then_inc(h_lo, 1)

            def add_x(name, off, n):
                for k in range(DT8):
                    pool.wait_ge(scaled, 8 * scaled_no[name] + k + 1)
                    x = X[:, k, off:off + n]
                    pool.tensor_tensor(x, x, S8[:, k, off:off + n], ALU.add).then_inc(x_new, 1)

            own = Own(pool, pool_own)
            pool.wait_ge(silu_c, 1)
            for m in (1, 3):
                w = MW8[:, 2 * m + 1, :, :]
                c = SM[:, CSC:CSC + 8].unsqueeze(2).to_broadcast([P, 8, MU])
                pool.wait_ge(mod_first[2 * m + 1], 16)
                own.wait(pool.tensor_tensor(w, w, c, ALU.mult))
                own.wait(pool.tensor_tensor(w[:, 0:4], w[:, 0:4], w[:, 4:8], ALU.add))
                own.wait(pool.tensor_tensor(w[:, 0:2], w[:, 0:2], w[:, 2:4], ALU.add))
                pool.wait_ge(mod_sum, 2 * m)
                pool.tensor_tensor(ACC8[:, 1, :], w[:, 0], w[:, 1], ALU.add).then_inc(mod_acc[1], 1)
            for u in range(FIRST - 2, FIRST):
                pool.wait_ge(mod_acc[u % 2], u // 2 + 1)
            load_mod(FIRST // 2)
            for s in (1, 3):
                pool.wait_ge(hi_ready[s], 1)
                low_w(s, DT8)
            for p in ph:
                if p.name.startswith("a_cx"):
                    low_h(f"pre{p.l}", 0, TOK)
                run(p.name)
                off, n = p.off, p.T
                if p.name.startswith("mix_out"):
                    add_x(f"post{p.l}", off, n)
                    low_h(f"fpre{p.l}", off, n)
                if p.name in ("ffn_down2", "ffn_down3"):
                    add_x(f"fpost{p.l}", off, n)

        @block.tensor
        def _(pe):
            def three(ps, w, wcols, x, k, off, n, first, last):
                W = slice(wcols * P, (wcols + 1) * P)
                pe.matmul(ps, w_hi[:, w, W], x[0][:, k, off:off + n], start=first, stop=False)
                pe.matmul(ps, w_hi[:, w, W], x[1][:, k, off:off + n], start=False, stop=False)
                return pe.matmul(ps, w_lo[:, w, W], x[0][:, k, off:off + n], start=False, stop=last)

            def chunk(p, r, s, ready):
                pe.wait_ge(lo_ready[s], gen(p, r, s) + 1)
                b = s if p.per == 1 else s | 1
                if p.per == 1 or s % 2 == 0:
                    pe.wait_ge(bank_free[b], p.bank[b] + r)
                if p.kind == "gates":
                    j = SLOTS * r + (s - p.s0) % SLOTS
                    if s % 2 == 0:
                        pe.wait_ge(sig["low"], by["lru_x"].base["low"] + j + 2)
                    for g in range(2):
                        for k in range(2):
                            last = three(bank[s][:, g * SEQ:(g + 1) * SEQ], s, 2 * g + k, rhs_of["XC"],
                                         2 * (j // 2) + k, 0, SEQ, k == 0, k == 1)
                else:
                    x = rhs_of[p.rhs] if p.rhs != "HY" else rhs_of["HY"[s % 2]]
                    kx = 11 * (s % 2) if p.per == 2 else 0
                    off = 0 if p.rhs in ("XC",) else p.off
                    for k in range(p.kb):
                        if ready is not None and (s - p.s0) % SLOTS == (1 if p.rhs == "HY" or kx else 0):
                            pe.wait_ge(ready[0], ready[1] + kx + k + 1)
                        last = three(bank[b][:, 0:p.T], s, k, x, kx + k, off, p.T,
                                     k == 0 and (p.per == 1 or s % 2 == 0), k == p.kb - 1 and (p.per == 1 or s % 2 == 1))
                last.then_inc(chunk_done[s], 1)

            def turn(p, r, s):
                t = SLOTS * r + s
                b = B[s % 2]
                pe.wait_ge(bank_free[s], p.bank[s] + r + 1)
                pe.wait_ge(sig["copied"], p.base["copied"] + t + 1)
                keys = KEYS if p.T == TOK else KEYS[:2]
                for i, (q, n) in enumerate(keys):
                    last = pe.transpose(b[0:n, i * P:(i + 1) * P], CO[:, s, q:q + n], ident)
                last.then_inc(sig["turned"], 1)

            def mod_sums(p, r):
                for i in range(2):
                    m = p.mods // 2 + r
                    mod_columns(m, i)

            def mod_columns(m, i):
                acc = ACC8 if isinstance(m, int) and m < FIRST // 2 else ACC
                pe.wait_ge(mod_acc[i], m + 1)
                if not isinstance(m, int) or m:
                    pe.wait_ge(mod_taken, 2 * m + i - 1)
                for j in range(2):
                    last = pe.matmul(B[2 + i][:, j:j + 1], acc[:, i, j * P:(j + 1) * P], ONES[:, 0:1],
                                     start=True, stop=True)
                last.then_inc(mod_sum, 1)

            def step(p, r, looped, ready=None, beside=None):
                slots = p.slots(r, looped)
                for i, s in enumerate(slots):
                    chunk(p, r, s, ready)
                    if beside is not None:
                        beside(SLOTS * r + i)
                    if p.kind == "vtok" and i:
                        turn(p, r, slots[i - 1])
                if p.kind == "vtok":
                    turn(p, r, slots[-1])
                if p.has_mods(r):
                    mod_sums(p, r)

            def sum_tile(name, k, off, n):
                pe.wait_ge(squares, 8 * stat_no[name] + k + 1)
                last = pe.matmul(B[0][:, 0:n], ONES[:, :], S8[:, k, off:off + n], start=k == 0, stop=k == DT8 - 1)
                if k == DT8 - 1:
                    last.then_inc(sum_done, 1)

            def sum_squares(name, off, n):
                for k in range(DT8):
                    sum_tile(name, k, off, n)

            def attention():
                def scores(h):
                    if h >= 2:
                        pe.wait_ge(side["att_p"], h - 1)
                    pe.matmul(B[h % 2][:, 0:P], AQ[:, h, 0:P], AK[:, h // 2, 0:P], start=True, stop=True)
                    pe.matmul(B[h % 2][:, P:384], AQ[:, h, P:SEQ], AK[:, h // 2, :], start=True, stop=True)\
                        .then_inc(side["att_s"], 1)

                def turn_probs(h):
                    pe.wait_ge(side["att_p"], h + 1)
                    if h:
                        pe.wait_ge(side["att_pt"], h)
                    for i in range(3):
                        last = pe.transpose(B[2][:, i * P:(i + 1) * P], AL[:, h % 2, i * P:(i + 1) * P], ident)
                    last.then_inc(side["att_t"], 1)

                def values(h):
                    pe.wait_ge(side["att_pt"], h + 1)
                    if h:
                        pe.wait_ge(side["side_lo"], h)
                    v = slice(h // 2 * P, (h // 2 + 1) * P)
                    pe.matmul(B[3][:, 0:SEQ], AV[:, 0, v], APT[:, h % 2, 0:SEQ], start=True, stop=False)
                    pe.matmul(B[3][:, P:SEQ], AV[:, 1, v], APT[:, h % 2, SEQ:], start=False, stop=True)\
                        .then_inc(side["att_o"], 1)

                def head(i):
                    if 2 <= i <= 9:
                        turn_probs(i - 2)
                    if i < 8:
                        pe.wait_ge(bank_free[i % SLOTS], by["q"].bank[i % SLOTS] + i // SLOTS + 1)
                        scores(i)
                    if i >= 3:
                        values(i - 3)

                run("q", split("mix1"), beside=lambda c: head(c - 1) if c else None)
                for i in range(7, 11):
                    head(i)

            def packed_scores(b, key, kt, q, qt, tiles=1, pitch=TOK):
                for n, (c, q0, w) in enumerate(SEG):
                    for i in range(tiles):
                        at = pitch * (kt + i) + n * P
                        last = pe.matmul(b[:, c:c + w], key[:, at:at + P], q[:, TOK * (qt + i) + q0:TOK * (qt + i) + q0 + w],
                                         start=i == 0, stop=i == tiles - 1)
                return last

            def weighted(b, rows, v, vcols, w):
                for n, (c, q0, m) in enumerate(SEG):
                    k = KEYS[n][1]
                    last = pe.matmul(b[rows, q0:q0 + m], v[0:k, n, vcols], w[0:k, c:c + m], start=n == 0, stop=n == 2)
                return last

            def state_space(l):
                def turn_steps():
                    pe.wait_ge(side["dt_acs"], l + 1)
                    for i in range(2):
                        for n, (q, w) in enumerate(KEYS):
                            src = SD[0:16, 6, q:q + w] if i == 0 else ACS[0:16, q:q + w]
                            last = pe.transpose(B[0][0:w, 48 * i + 16 * n:48 * i + 16 * n + 16], src, CS[0:16, 0:16])
                    last.then_inc(side["dt_turned"], 1)

                def turn_x(m):
                    if m == 0:
                        pe.wait_ge(side["dt_cols"], l + 1)
                        pe.wait_ge(sig["high"], by[f"s_x{l}"].end["high"])
                    if m >= 3:
                        pe.wait_ge(side["x_scaled"], 6 * l + m - 2)
                    n, half = m // 2, m % 2
                    q, w = KEYS[n]
                    for j in range(4):
                        last = pe.transpose(B[1 + m % 3][0:w, j * P:(j + 1) * P], XS[:, 4 * half + j, q:q + w], ident)
                    last.then_inc(side["x_turned"], 1)

                def group_scores(g):
                    if g == 0:
                        pe.wait_ge(sig["high"], by[f"s_bc{l}"].end["high"])
                    pe.wait_ge(side["x_scaled"], 6 * l + (4, 4, 5, 6)[g])
                    packed_scores(B[g], BC, g, BC, 4 + g).then_inc(side["cb_done"], 1)

                def front(i):
                    if i == 0:
                        turn_steps()
                    elif i < 4:
                        turn_x(2 * i - 2)
                        turn_x(2 * i - 1)
                    elif i == 4:
                        for g in range(4):
                            group_scores(g)

                def rows(h):
                    if h < 2:
                        pe.wait_ge(side["cb_masked"], 4 * l + 4)
                    else:
                        pe.wait_ge(side["decay_log"], 16 * l + h - 1)
                    sel = CS[0:16, h:h + 1].to_broadcast([16, P])
                    pe.matmul(B[h % 2][:, 0:TOK], sel, ACS[0:16, :], start=True, stop=True).then_inc(side["acs_rows"], 1)

                def outputs(h):
                    pe.wait_ge(side["decay_mix"], 16 * l + h + 1)
                    if h >= 4 and h % 2 == 0:
                        pe.wait_ge(side["y_taken"], 8 * l + h // 2 - 1)
                    lo = h % 2 * 64
                    weighted(B[2 + h // 2 % 2], slice(lo, lo + 64), XT, slice(h * 64, h * 64 + 64), SX[:, h % 2])\
                        .then_inc(side["head_y"], 1)

                def head(i):
                    if i < 16:
                        rows(i)
                    if i >= 2:
                        outputs(i - 2)

                run(f"s_z{l}", beside=lambda c: front(c - 4) if c >= 4 else None)
                run(f"r_q{l}", beside=lambda c: head(c - 1) if c else front(4))
                run(f"r_k{l}", beside=lambda c: head(7 + c))
                for i in (15, 16, 17):
                    head(i)
                for g in range(4):
                    pe.wait_ge(side["y_sq"], 8 * l + g + 1)
                    for k in range(2):
                        last = pe.matmul(B[g][:, 0:TOK], ONES[:, :], YQ["ssd"][:, 2 * g + k, :], start=k == 0, stop=k == 1)
                    last.then_inc(side["y_sum"], 1)

            def retention(l):
                pe.wait_ge(sig["mixed"], by[f"r_k{l}"].end["mixed"])
                pe.wait_ge(sig["copied"], by[f"r_v{l}"].end["copied"] + 2)

                def scores(h):
                    if h >= 2:
                        pe.wait_ge(side["ret_p"], 4 * l + h - 1)
                    packed_scores(B[h % 2], RK, 2 * h, RQ, 2 * h, 2).then_inc(side["ret_s"], 1)

                def outputs(h):
                    pe.wait_ge(side["ret_p"], 4 * l + h + 1)
                    for e in range(2):
                        t = 2 * h + e
                        if t >= 2:
                            pe.wait_ge(side["ret_copy"], 8 * l + t - 1)
                        weighted(B[2 + e], slice(0, P), RV, slice(t * P, (t + 1) * P), RP[:, h % 2])\
                            .then_inc(side["ret_y"], 1)

                for i in range(5):
                    if i < 4:
                        scores(i)
                    if i >= 1:
                        outputs(i - 1)
                for h in range(4):
                    pe.wait_ge(side["ret_copy"], 8 * (l + 1))
                    for k in range(2):
                        last = pe.matmul(B[h][:, 0:TOK], ONES[:, :], S8[:, 2 * h + k, :], start=k == 0, stop=k == 1)
                    last.then_inc(side["ret_mean"], 1)
                for h in range(4):
                    pe.wait_ge(side["y_sq"], 8 * l + 4 + h + 1)
                    for k in range(2):
                        last = pe.matmul(B[h][:, 0:TOK], ONES[:, :], YQ["ret"][:, 2 * h + k, :], start=k == 0, stop=k == 1)
                    last.then_inc(side["y_sum"], 1)

            def stick_breaking(l):
                p = by[f"b_kq{l}"]
                pe.wait_ge(sig["copied"], by[f"b_v{l}"].end["copied"] + 2)

                def scores(h):
                    for s in (2 * h % SLOTS, 2 * h % SLOTS + 1):
                        pe.wait_ge(bank_free[s], p.bank[s] + h // 2 + 1)
                    if h >= 2:
                        pe.wait_ge(side["sb_z"], 8 * l + h - 1)
                    packed_scores(B[h % 2], BK, h, BQ, h, pitch=384).then_inc(side["sb_s"], 1)

                def suffix_sums(h):
                    pe.wait_ge(side["sb_sp"], 8 * l + h + 1)
                    if h:
                        pe.wait_ge(side["sb_logw"], 8 * l + h)
                    S = SS[:, h % 2]
                    b = B[2]
                    pe.matmul(b[:, 0:272], suffix, S[:, 0:272], start=True, stop=False)
                    pe.matmul(b[:, P:272], ONES[:, :], S[:, 272:416], start=False, stop=False)
                    pe.matmul(b[:, 256:272], ONES[0:16, :], S[0:16, 416:432], start=False, stop=True)
                    pe.matmul(b[:, 272:416], suffix, S[:, 272:416], start=True, stop=False)
                    pe.matmul(b[:, 400:416], ONES[0:16, :], S[0:16, 416:432], start=False, stop=True)
                    pe.matmul(b[:, 416:432], suffix[0:16, :], S[0:16, 416:432], start=True, stop=True)\
                        .then_inc(side["sb_r"], 1)

                def outputs(h):
                    pe.wait_ge(side["sb_w"], 8 * l + h + 1)
                    if h:
                        pe.wait_ge(side["side_lo"], 24 + 24 * l + h)
                    weighted(B[3], slice(0, P), BV, slice(h * P, (h + 1) * P), SW[:, h % 2]).then_inc(side["sb_o"], 1)

                def head(i):
                    if i < 8:
                        scores(i)
                    if 1 <= i <= 8:
                        suffix_sums(i - 1)
                    if i >= 2:
                        outputs(i - 2)

                run(p.name, beside=lambda c: head(c // 2 - 1) if c >= 2 and c % 2 == 0 else None)
                for i in range(7, 10):
                    head(i)

            def run(name, ready=None, beside=None):
                p = by[name]
                if beside is None:
                    rounds(pe, p, lambda r, looped: step(p, r, looped, ready))
                else:
                    for r in range(p.rounds):
                        step(p, r, False, ready, beside)
                if p.norm:
                    pe.wait_ge(squares_added, added_no[p.norm] + 1)
                    pe.matmul(B[0][:, 0:p.T], ONES[:, :], RSTD[:, 0:p.T], start=True, stop=True).then_inc(sum_done, 1)

            def split(name):
                return h_lo, 8 * split_no[name]

            def lows(name):
                return sig["low"], by[name].base["low"]

            pe.wait_ge(const_ready, 1)
            sum_squares("mix0", META, SEQ)
            for u in range(FIRST):
                mod_columns(u // 2, u % 2)
            pe.wait_ge(loaded["onehot"], 32)
            pe.matmul(B[1][0:8, 0:BIASW], RB[:, :], OH[:, :], start=True, stop=True).then_inc(side["bias_sum"], 1)
            run("lru_x", split("mix0"))
            run("lru_gates")
            run("lru_y")
            run("lru_out", (side["lru_lo"], 0))
            run("ffn_up0", split("ffn0"))
            run("ffn_down0", lows("ffn_up0"))
            run("kv_k", split("kv"))
            pe.wait_ge(loaded["consts"], 16)
            run("kv_v")
            pe.wait_ge(sig["copied"], by["kv_v"].end["copied"] + 2)
            attention()
            run("attn_out", (side["side_lo"], 0))
            run("ffn_up1", split("ffn1"))
            run("ffn_down1", lows("ffn_up1"))
            for l in range(2):
                off, n = (META, SEQ) if l else (0, TOK)
                sum_squares(f"pre{l}", 0, TOK)
                run(f"a_cx{l}", split(f"pre{l}"))
                run(f"a_b{l}")
                run(f"up_a{l}", lows(f"a_b{l}"))
                run(f"dt{l}")
                run(f"s_x{l}")
                run(f"s_bc{l}")
                state_space(l)
                run(f"up_b{l}", (side["side_lo"], 8 + 24 * l))
                run(f"r_v{l}")
                run(f"r_g{l}")
                retention(l)
                run(f"up_c{l}", (side["side_lo"], 16 + 24 * l))
                run(f"b_v{l}")
                stick_breaking(l)
                run(f"up_d{l}", (side["side_lo"], 24 + 24 * l))
                run(f"mix_out{l}", lows(f"up_d{l}"))
                sum_squares(f"fpre{l}", off, n)
                run(f"ffn_up{2 + l}", split(f"fpre{l}"))
                run(f"ffn_down{2 + l}", lows(f"ffn_up{2 + l}"))

        @block.scalar
        def _(act):
            own = Own(act, act_own)
            table_set = [None]

            def cut(p, r, s, looped):
                kb = p.kb if looped else p.next_kb[r, s]
                if kb is None:
                    return
                g = gen(p, r, s) + 1
                act.wait_ge(raw_ready[s], 16 * (g + 1))
                act.wait_ge(chunk_done[s], g)
                act.copy(w_hi[:, s, 0:kb * P], raw[:, s, 0:kb * P]).then_inc(hi_ready[s], 1)

            acts = {"lru_y": (YB, ACT.Copy, 1.0), "kv_k": (AK, ACT.Copy, 1.0), "q": (AQ, ACT.Copy, 1.0)}
            for l in range(2):
                acts |= {f"s_z{l}": (Z, ACT.Silu, 1.0), f"r_g{l}": (RG, ACT.Silu, 1.0), f"mix_out{l}": (M, ACT.Copy, 1.0),
                         f"ffn_down{2 + l}": (M, ACT.Copy, 1.0)}

            def convolved(p, t, s):
                act.wait_ge(sig["mixed"], p.base["mixed"] + t + 1)
                if p.kind == "conv_split":
                    act.copy(flat(XCh, t, 0, p.T), flat(XC, t, 0, p.T)).then_inc(sig["high"], 1)
                else:
                    dst = XS if p.t0 == 0 else BC
                    act.activation(flat(dst, t, 0, p.T), CO[:, s, 0:p.T], ACT.Silu).then_inc(sig["high"], 1)

            def tile(p, r, s, looped):
                done = gen(p, r, s) + 1
                free = p.bank[s] + r + 1
                t = r * SLOTS + (s - p.s0) % SLOTS
                if p.kind in ("conv_split", "conv_silu"):
                    act.wait_ge(chunk_done[s], done)
                    act.copy(CI[:, s, 3:3 + p.T], bank[s][:, 0:p.T]).then_inc(bank_free[s], 1)
                    if p.kind == "conv_silu":
                        act.wait_ge(bank_free[s], free)
                        act.wait_ge(sig["high"], p.base["high"] + t - 3)
                        act.activation(CO[:, s, 0:p.T], CI[:, s, 0:p.T], ACT.Identity,
                                       bias=col(PV, PCOL["ssd_conv_b"] + 16 * p.l + p.t0 + t),
                                       scale=col(PV, PCOL["ssd_conv_w"] + 64 * p.l + p.t0 + t)).then_inc(tapped, 1)
                    cut(p, r, s, looped)
                    if s != p.slots(r, looped)[0]:
                        convolved(p, t - 1, s - 1)
                    if s == p.slots(r, looped)[-1]:
                        convolved(p, t, s)
                    return
                if p.kind == "vtok":
                    act.wait_ge(chunk_done[s], done)
                    act.wait_ge(sig["copied"], p.base["copied"] + t + 1)
                    act.copy(CO[:, s, 0:p.T], bank[s][:, 0:p.T]).then_inc(bank_free[s], 1)
                if p.kind == "act":
                    b = s
                    if p.per == 2:
                        t = r * 2 + s // 2
                    if p.per == 1 or s % 2:
                        act.wait_ge(chunk_done[s], done)
                        if p.name.startswith("b_kq"):
                            dst, func, scale, t = (BQ if s % 2 else BK), ACT.Copy, (P ** -0.5 if s % 2 else 1.0), t // 2
                        else:
                            dst, func, scale = acts[p.name]
                        off = p.off if dst is M else 0
                        if p.norm:
                            act.activation(flat(S8, t, off, p.T), bank[b][:, 0:p.T], ACT.Square).then_inc(squares, 1)
                        act.activation(flat(dst, t, off, p.T), bank[b][:, 0:p.T], func, scale=scale)\
                            .then_inc(bank_free[b], 1)
                if p.kind in ("glu", "cx", "merge", "merge_split") and s % 2 == 0:
                    func = {"glu": ACT.Silu, "cx": ACT.Copy}.get(p.kind, ACT.Sigmoid)
                    act.wait_ge(chunk_done[s], done)
                    act.activation(CI[:, s, 3:3 + p.T], bank[s][:, 0:p.T], func).then_inc(bank_free[s], 1)
                if p.kind in ("glu", "cx", "merge", "merge_split") and s % 2:
                    q = r * 2 + s // 2
                    act.wait_ge(bank_free[s], free)
                    if p.kind == "glu":
                        act.copy(flat(Fh, q, p.off, p.T), CO[:, s - 1, 0:p.T]).then_inc(sig["high"], 1)
                    if p.kind == "merge_split":
                        act.wait_ge(sig["mixed"], p.base["mixed"] + q + 1)
                        act.copy(flat(Mh, q, p.off, p.T), CO[:, s - 1, 0:p.T]).then_inc(sig["high"], 1)
                if p.kind == "conv_gate":
                    cut(p, r, s, looped)
                    act.wait_ge(bank_free[s], free)
                    act.copy(flat(Yh, t, 0, p.T), CI[:, s, 3:3 + p.T]).then_inc(sig["high"], 1)
                    return
                if p.kind == "dt":
                    act.wait_ge(chunk_done[s], done)
                    act.activation(SD[:, 0, :], bank[0][0:16, 0:TOK], ACT.Identity,
                                   bias=SM[0:16, EAL + 2 * p.l:EAL + 2 * p.l + 1]).then_inc(bank_free[0], 1)
                    cut(p, r, s, looped)
                    act.activation(SM[0:16, EA + p.l:EA + p.l + 1], SM[0:16, EAL + 2 * p.l + 1:EAL + 2 * p.l + 2], ACT.Exp)
                    return
                if p.kind == "gates":
                    act.wait_ge(chunk_done[s], done)
                    if t >= 8:
                        act.wait_ge(side["gate_in"], t - 7)
                    c = PCOL["lru_b_gates"] + t
                    act.activation(LA[:, t, :], bank[s][:, 0:SEQ], ACT.Sigmoid, bias=PV[:, c:c + 1])
                    act.activation(S8[:, t % 8, 0:SEQ], bank[s][:, SEQ:], ACT.Sigmoid, bias=PV[:, c + LT:c + LT + 1])\
                        .then_inc(bank_free[s], 1)
                    cut(p, r, s, looped)
                    act.wait_ge(bank_free[s], free)
                    dst = M2[:, t, :] if t < 8 else CO[:, t - 8, 0:SEQ]
                    act.activation(dst, LA[:, t, :], ACT.Tanh, scale=SM[:, SPT + t:SPT + t + 1]).then_inc(side["gate_tanh"], 1)
                    return
                if p.kind == "resid" and (p.per == 1 or s % 2):
                    t = t if p.per == 1 else r * 2 + s // 2
                    act.wait_ge(bank_free[s], free)
                    act.activation(S8[:, t, META:], X[:, t, META:], ACT.Square).then_inc(squares, 1)
                cut(p, r, s, looped)

            def step(p, r, looped, beside=None):
                for i, s in enumerate(p.slots(r, looped)):
                    tile(p, r, s, looped)
                    if beside is not None:
                        beside(SLOTS * r + i)

            tables = {"glu": "silu_and_others", "conv_silu": "silu_and_others", "merge": "sigmoid_and_others",
                      "merge_split": "sigmoid_and_others", "gates": "sigmoid_and_others"}

            def table(name):
                if name != table_set[0]:
                    act.preload_act_table_set(name)
                    table_set[0] = name

            def log_exp():
                table("natural_log_exp_and_others")

            def run(name, beside=None):
                p = by[name]
                if p.kind in tables:
                    table(tables[p.kind])
                elif p.name in acts and acts[p.name][1] is ACT.Silu:
                    table("silu_and_others")
                if beside is None:
                    rounds(act, p, lambda r, looped: step(p, r, looped))
                else:
                    for r in range(p.rounds):
                        step(p, r, False, beside)

            def inverse_root(src, dst, scale, ready, no, done):
                act.wait_ge(ready, no)
                own.wait(act.activation(dst, src, ACT.Ln, bias=SM[:, EPSC:EPSC + 1], scale=scale))
                act.activation(dst, dst, ACT.Exp, scale=-0.5).then_inc(done, 1)

            def root(name, off, n):
                log_exp()
                inverse_root(B[0][:, 0:n], RSTD[:, 0:n], 1.0 / D, sum_done, stat_no[name] + 1, rstd_ready)

            def high_h(name, off, n, dst, shift=None):
                for k in range(DT8):
                    act.wait_ge(scaled, 8 * scaled_no[name] + k + 1)
                    if shift is None:
                        act.copy(dst[:, k, off:off + n], S8[:, k, off:off + n]).then_inc(h_hi, 1)
                    else:
                        act.activation(dst[:, k, off:off + n], S8[:, k, off:off + n], ACT.Identity,
                                       bias=MOD[:, shift + k:shift + k + 1]).then_inc(h_hi, 1)

            def norm(name, off, n, shift=None):
                root(name, off, n)
                high_h(name, off, n, Hh, shift)

            def square_x(name, off, n):
                for k in range(DT8):
                    act.wait_ge(x_new, 8 * x_no[name] + k + 1)
                    act.activation(S8[:, k, off:off + n], X[:, k, off:off + n], ACT.Square).then_inc(squares, 1)

            def softplus(z, u, ln, w, no):
                log_exp()
                if no > 1:
                    act.wait_ge(bank_free[0], by[f"dt{no - 2}"].bank_end[0])
                own.wait(act.activation(u, z, ACT.Abs))
                act.activation(u, u, ACT.Exp, scale=-1.0).then_inc(sp_u, 1)
                act.wait_ge(sp_w, no)
                act.activation(ln, w, ACT.Ln).then_inc(sp_ln, 1)

            def recurrence_beside(name):
                def decay(t):
                    act.wait_ge(side["gate_tanh"], t + 1)
                    act.activation(LA[:, t, :], LA[:, t, :], ACT.Exp, scale=SM[:, SPL + t:SPL + t + 1])\
                        .then_inc(side["gate_a"], 1)
                    if t:
                        input_factor(t - 1)

                run(name, beside=decay)
                input_factor(LT - 1)

            def input_factor(t):
                act.wait_ge(side["gate_m2"], t + 1)
                m = M2[:, t, :] if t < 8 else CO[:, t - 8, 0:SEQ]
                own.wait(act.activation(m, m, ACT.Ln, bias=SM[:, EPSC + 1:EPSC + 2]))
                act.activation(m, m, ACT.Exp, scale=0.5).then_inc(side["gate_sqrt"], 1)

            def attention():
                log_exp()

                def exps(h):
                    b = h % 2
                    act.wait_ge(side["att_max"], h + 1)
                    for i, (c, w) in enumerate(((0, P), (P, SEQ))):
                        ins = act.activation(AL[:, b, c:c + w], AL[:, b, c:c + w], ACT.Exp,
                                             bias=SM[:, AMX + 2 * b + i:AMX + 2 * b + i + 1],
                                             accum_out=SM[:, ASM + 2 * b + i:ASM + 2 * b + i + 1])
                    ins.then_inc(side["att_exp"], 1)

                def take_probs(h):
                    act.wait_ge(side["att_t"], h + 1)
                    if h >= 2:
                        act.wait_ge(side["att_o"], h - 1)
                    act.copy(APT[:, h % 2, :], B[2][:, 0:384]).then_inc(side["att_pt"], 1)

                def head(i):
                    if i < 8:
                        exps(i)
                    if 2 <= i <= 9:
                        take_probs(i - 2)
                    if i >= 3:
                        act.wait_ge(side["att_o"], i - 2)
                        act.copy(Yh[:, i - 3, META:], B[3][:, 0:SEQ]).then_inc(side["side_hi"], 1)

                run("q", beside=lambda c: head(c - 1) if c else None)
                for i in range(7, 11):
                    head(i)

            def state_space(l):
                softplus(SD[:, 0, :], SD[:, 1, :], SD[:, 2, :], SD[:, 3, :], 2 + l)

                def head(h):
                    n16 = 16 * l + h
                    b = h % 2
                    act.wait_ge(side["decay_log"], n16 + 1)
                    act.activation(SE[:, b, 0:416], SE[:, b, 0:416], ACT.Exp)
                    act.activation(SE[0:16, b, 416:], SE[0:16, b, 416:], ACT.Exp).then_inc(side["decay_exp"], 1)

                run(f"s_z{l}")
                log_exp()
                run(f"r_q{l}", beside=lambda c: head(c - 1) if c else None)
                run(f"r_k{l}", beside=lambda c: head(7 + c))
                head(15)
                for g in range(4):
                    inverse_root(B[g][:, 0:TOK], YR["ssd"][:, g, :], 1.0 / 256, side["y_sum"], 8 * l + g + 1, side["y_rstd"])
                halves(16 * l)

            def halves(before):
                for k in range(8):
                    act.wait_ge(side["y32"], before + k + 1)
                    act.copy(Yh[:, k, :], S8[:, k, :]).then_inc(side["side_hi"], 1)

            def retention(l):
                log_exp()
                for t in range(8):
                    act.wait_ge(side["ret_y"], 8 * l + t + 1)
                    act.copy(S8[:, t, :], B[2 + t % 2][:, 0:TOK]).then_inc(side["ret_copy"], 1)
                for h in range(4):
                    inverse_root(B[h][:, 0:TOK], YR["ret"][:, h, :], 1.0 / 256, side["y_sum"], 8 * l + 4 + h + 1, side["y_rstd"])
                halves(16 * l + 8)

            def stick_breaking(l):
                log_exp()

                def soft(h):
                    b, n8 = h % 2, 8 * l + h
                    act.wait_ge(side["sb_s"], n8 + 1)
                    if h >= 2:
                        act.wait_ge(side["sb_logw"], n8 - 1)
                    act.copy(ZS[:, b, :], B[b][:, 0:PACK])
                    act.activation(SA[:, b, :], B[b][:, 0:PACK], ACT.Abs).then_inc(side["sb_z"], 1)
                    act.wait_ge(side["sb_z"], n8 + 1)
                    own.wait(act.activation(SA[:, b, :], SA[:, b, :], ACT.Exp, scale=-1.0))
                    act.activation(SA[:, b, :], SA[:, b, :], ACT.Ln, bias=ONES[:, 0:1]).then_inc(side["sb_soft"], 1)

                def head(i):
                    if i < 8:
                        soft(i)
                    if 1 <= i <= 8:
                        act.wait_ge(side["sb_logw"], 8 * l + i)
                        act.activation(SW[:, (i - 1) % 2, :], SW[:, (i - 1) % 2, :], ACT.Exp).then_inc(side["sb_we"], 1)
                    if i >= 2:
                        act.wait_ge(side["sb_o"], 8 * l + i - 1)
                        act.copy(Yh[:, i - 2, :], B[3][:, 0:TOK]).then_inc(side["side_hi"], 1)

                run(f"b_kq{l}", beside=lambda c: head(c // 2 - 1) if c >= 2 and c % 2 == 0 else None)
                for i in range(7, 10):
                    head(i)

            table("silu_and_others")
            act.wait_ge(loaded["params"], 16)
            act.activation(SM[:, CSC:CSC + 8], PV[:, PCOL["c"]:PCOL["c"] + 8], ACT.Silu).then_inc(silu_c, 1)
            act.wait_ge(loaded["x"], 16)
            for k in range(DT8):
                act.activation(S8[:, k, META:], X[:, k, META:], ACT.Square).then_inc(squares, 1)
            root("mix0", META, SEQ)
            for s in range(SLOTS):
                act.wait_ge(raw_ready[s], 16)
                act.copy(w_hi[:, s, 0:DT8 * P], raw[:, s, 0:DT8 * P]).then_inc(hi_ready[s], 1)
            high_h("mix0", META, SEQ, Hh, 0)
            softplus(SM[:, SPT:SPT + LT], SM[:, SPW:SPW + 10], SM[:, SPW + 20:SPW + 30], SM[:, SPW + 10:SPW + 20], 1)
            run("lru_x")
            run("lru_gates")
            log_exp()
            recurrence_beside("lru_y")
            table("gelu_apprx_tanh_and_others")
            for t in range(LT + 1):
                if t < LT:
                    act.activation(YB[:, t, :], YB[:, t, :], ACT.Gelu_apprx_tanh).then_inc(side["lru_gelu"], 1)
                if t:
                    act.wait_ge(side["lru_y32"], t)
                    act.copy(XCh[:, t - 1, 0:SEQ], XC[:, t - 1, :]).then_inc(side["lru_hi"], 1)
            run("lru_out")
            norm("ffn0", META, SEQ, shift=24)
            run("ffn_up0")
            run("ffn_down0")
            root("kv", META, SEQ)
            high_h("kv", META, SEQ, Yh, 48)
            high_h("mix1", META, SEQ, Hh, 64)
            run("kv_k")
            run("kv_v")
            attention()
            run("attn_out")
            norm("ffn1", META, SEQ, shift=88)
            run("ffn_up1")
            run("ffn_down1")
            root("final", META, SEQ)
            square_x("final", 0, TOK)
            for l in range(2):
                off, n = (META, SEQ) if l else (0, TOK)
                norm(f"pre{l}", 0, TOK)
                run(f"a_cx{l}")
                run(f"a_b{l}")
                run(f"up_a{l}")
                run(f"dt{l}")
                run(f"s_x{l}")
                run(f"s_bc{l}")
                state_space(l)
                run(f"up_b{l}")
                run(f"r_v{l}")
                run(f"r_g{l}")
                retention(l)
                run(f"up_c{l}")
                run(f"b_v{l}")
                stick_breaking(l)
                run(f"up_d{l}")
                run(f"mix_out{l}")
                root(f"post{l}", off, n)
                square_x(f"post{l}", off, n)
                norm(f"fpre{l}", off, n)
                run(f"ffn_up{2 + l}")
                run(f"ffn_down{2 + l}")
                root(f"fpost{l}", off, n)
                if l == 0:
                    square_x(f"fpost{l}", 0, TOK)

        @block.vector
        def _(dve):
            own = Own(dve, vec_own)
            tt, ts, stt = dve.tensor_tensor, dve.tensor_scalar, dve.scalar_tensor_tensor

            def cut(p, r, s, looped):
                kb = p.kb if looped else p.next_kb[r, s]
                if kb is None or s % 2:
                    return
                dve.wait_ge(hi_ready[s], gen(p, r, s) + 2)
                low_w(s, kb)

            def low_w(s, kb):
                tt(w_lo[:, s, 0:kb * P], raw[:, s, 0:kb * P], w_hi[:, s, 0:kb * P].bitcast(F32), ALU.subtract)\
                    .then_inc(lo_ready[s], 1)

            def low(dst, src, high):
                return tt(dst, src, high.bitcast(F32), ALU.subtract)

            def mod_units(m, units=(0, 1)):
                for k in range(8):
                    for i in units:
                        if isinstance(m, int) and m < FIRST // 2:
                            w, acc, ready, n = MW8[:, 2 * m + i], ACC8, mod_first[2 * m + i], 1
                        else:
                            w, acc, ready, n = MW[:, i], ACC, mod_ready[i], m + 1 - FIRST // 2
                        c = SM[:, CSC + k:CSC + k + 1]
                        if k == 0:
                            dve.wait_ge(ready, 16 * n)
                            ins = ts(acc[:, i, :], w[:, 0, :], c, None, ALU.mult)
                        else:
                            own.wait(back=0 if len(units) == 1 or k == 7 and i else 1)
                            ins = stt(acc[:, i, :], w[:, k, :], c, acc[:, i, :], ALU.mult, ALU.add)
                        if k < 7:
                            own.mark(ins)
                        else:
                            ins.then_inc(mod_acc[i], 1)

            def mod_take(m, i):
                dve.wait_ge(mod_sum, 2 * m + i + 1)
                c = (2 * m + i) * 2
                dst = MOD[:, c:c + 2] if isinstance(c, int) else MOD[:, bass.ds(c, 2)]
                return tt(dst, B[2 + i][:, 0:2], dst, ALU.add).then_inc(mod_taken, 1)

            resid_gate = {"lru_out": 16, "ffn_down0": 40, "attn_out": 80, "ffn_down1": 104}

            def low_conv(p, t):
                dve.wait_ge(sig["high"], p.base["high"] + t + 1)
                low(flat(XCl, t, 0, p.T), flat(XC, t, 0, p.T), flat(XCh, t, 0, p.T)).then_inc(sig["low"], 1)

            def tile(p, r, s, looped):
                if p.has_mods(r) and s == p.s0:
                    mod_units(p.mods // 2 + r)
                done = gen(p, r, s) + 1
                t = r * SLOTS + (s - p.s0) % SLOTS
                T = p.T
                if p.kind in ("conv_split", "conv_silu"):
                    at = t + p.t0
                    names = ("lru_conv_w", "lru_conv_b", LT) if p.kind == "conv_split" else ("ssd_conv_w", "ssd_conv_b", 16)
                    w0, b0 = PCOL[names[0]] + 4 * names[2] * p.l, PCOL[names[1]] + names[2] * p.l
                    dve.wait_ge(bank_free[s], p.bank[s] + r + 1)
                    if p.kind == "conv_split":
                        own.wait(ts(CO[:, s, 0:T], CI[:, s, 0:T], col(PV, w0 + at), col(PV, b0 + at), ALU.mult, ALU.add))
                    else:
                        dve.wait_ge(tapped, 16 * p.l + p.t0 + t + 1)
                    for j in range(1, 4):
                        dst = flat(XC, t, 0, T) if p.kind == "conv_split" and j == 3 else CO[:, s, 0:T]
                        ins = stt(dst, CI[:, s, j:j + T], col(PV, w0 + names[2] * j + at), CO[:, s, 0:T],
                                  ALU.mult, ALU.add)
                        if j < 3:
                            own.wait(ins)
                    ins.then_inc(sig["mixed"], 1)
                    cut(p, r, s, looped)
                    if p.kind == "conv_split":
                        if s != p.slots(r, looped)[0]:
                            low_conv(p, t - 1)
                        if s == p.slots(r, looped)[-1]:
                            low_conv(p, t)
                    return
                if p.kind == "vtok":
                    cut(p, r, s, looped)
                    if s:
                        take_values(p, t - 1, s - 1)
                    if s == p.slots(r, looped)[-1]:
                        take_values(p, t, s)
                    return
                if p.kind == "resid":
                    if p.per == 2:
                        t = r * 2 + s // 2
                    if p.per == 1 or s % 2:
                        dve.wait_ge(chunk_done[s], done)
                        x = flat(X, t, META, SEQ)
                        stt(x, bank[s][:, 0:SEQ], col(MOD, resid_gate[p.name] + t), x, ALU.mult, ALU.add)\
                            .then_inc(bank_free[s], 1)
                q = r * 2 + s // 2
                if p.kind in ("glu", "cx", "merge", "merge_split") and s % 2:
                    dve.wait_ge(chunk_done[s], done)
                    dve.wait_ge(bank_free[s - 1], p.bank[s - 1] + r + 1)
                    f = CI[:, s - 1, 3:3 + T]
                    if p.kind == "cx":
                        dst = U[:, q, 2:2 + T] if isinstance(q, int) else flat(U, q, 2, T)
                    elif p.name in ("up_a0", "up_a1"):
                        dst = flat(M, q, p.off, T)
                    else:
                        dst = CO[:, s - 1, 0:T]
                    tt(dst, f, bank[s][:, 0:T], ALU.mult).then_inc(bank_free[s], 1)
                    if p.kind in ("merge", "merge_split") and not p.name.startswith("up_a"):
                        dve.wait_ge(bank_free[s], p.bank[s] + r + 1)
                        m = flat(M, q, p.off, T)
                        if p.kind == "merge":
                            tt(m, m, dst, ALU.add)
                        else:
                            tt(dst, m, dst, ALU.add).then_inc(sig["mixed"], 1)
                if p.kind == "conv_gate":
                    w0 = PCOL["conv_a"] + 24 * p.l
                    own.wait(ts(CO[:, s, 0:T], flat(U, t, 0, T), col(PV, w0 + t), None, ALU.mult))
                    for j in (1, 2):
                        own.wait(stt(CO[:, s, 0:T], flat(U, t, j, T), col(PV, w0 + 8 * j + t), CO[:, s, 0:T],
                                     ALU.mult, ALU.add))
                    dve.wait_ge(chunk_done[s], done)
                    tt(CI[:, s, 3:3 + T], CO[:, s, 0:T], bank[s][:, 0:T], ALU.mult).then_inc(bank_free[s], 1)
                    cut(p, r, s, looped)
                    dve.wait_ge(sig["high"], p.base["high"] + t + 1)
                    low(flat(Yl, t, 0, T), CI[:, s, 3:3 + T], flat(Yh, t, 0, T)).then_inc(sig["low"], 1)
                    return
                if p.kind == "rotate" and s % 2:
                    e = s - 1
                    dve.wait_ge(chunk_done[e], done)
                    dve.wait_ge(chunk_done[s], done)
                    p1, p2 = bank[e][:, 0:T], bank[s][:, 0:T]
                    t1, t2, t3, t4 = CO[:, e, 0:T], CO[:, s, 0:T], CI[:, e, 3:3 + T], CI[:, s, 3:3 + T]
                    tt(t1, p1, cos, ALU.mult)
                    tt(t3, p1, sin, ALU.mult).then_inc(bank_free[e], 1)
                    tt(t2, p2, sin, ALU.mult)
                    tt(t4, p2, cos, ALU.mult).then_inc(bank_free[s], 1)
                    dve.wait_ge(bank_free[s], p.bank[s] + r + 1)
                    dst = RQ if p.name.startswith("r_q") else RK
                    tt(flat(dst, 2 * q, 0, T), t1, t2, ALU.subtract)
                    tt(flat(dst, 2 * q + 1, 0, T), t3, t4, ALU.add).then_inc(sig["mixed"], 1)
                if p.kind == "gates":
                    dve.wait_ge(bank_free[s], p.bank[s] + r + 1)
                    tt(XC[:, t, :], XC[:, t, :], S8[:, t % 8, 0:SEQ], ALU.mult).then_inc(side["gate_in"], 1)
                    cut(p, r, s, looped)
                    return
                if p.kind == "dt":
                    cut(p, r, s, looped)
                    return
                cut(p, r, s, looped)
                if p.norm and (p.per == 1 or s % 2):
                    t = t if p.per == 1 else r * 2 + s // 2
                    if t > 1:
                        add_squares(p, t - 1)
                if p.kind in ("glu", "merge_split") and s % 2:
                    dve.wait_ge(sig["high"], p.base["high"] + q + 1)
                    h, l_ = (Fh, Fl) if p.kind == "glu" else (Mh, Ml)
                    low(flat(l_, q, p.off, T), CO[:, s - 1, 0:T], flat(h, q, p.off, T)).then_inc(sig["low"], 1)

            def step(p, r, looped, beside=None):
                for i, s in enumerate(p.slots(r, looped)):
                    tile(p, r, s, looped)
                    if beside is not None:
                        beside(SLOTS * r + i)
                if p.has_mods(r):
                    for i in range(2):
                        mod_take(p.mods // 2 + r, i)

            def add_squares(p, t):
                dve.wait_ge(squares, 8 * stat_no[p.norm] + t + 1)
                total = RSTD[:, 0:p.T]
                before = S8[:, 0, p.off:p.off + p.T] if t == 1 else total
                ins = tt(total, before, S8[:, t, p.off:p.off + p.T], ALU.add)
                if t < DT8 - 1:
                    own.wait(ins)
                else:
                    ins.then_inc(squares_added, 1)

            def take_values(p, t, s):
                dve.wait_ge(sig["turned"], p.base["turned"] + t + 1)
                V = AV if p.name == "kv_v" else RV if p.name.startswith("r_v") else BV
                b = B[s % 2]
                if isinstance(t, int):
                    cols = slice(t * P, (t + 1) * P)
                else:
                    cols = bass.ds(t * P, P)
                if p.T == TOK:
                    dve.tensor_copy(V[0:16, 2, cols], b[0:16, 2 * P:3 * P])
                dve.tensor_copy(V[:, 0:2, cols], b[:, 0:2 * P].rearrange("p (a n) -> p a n", a=2)).then_inc(sig["copied"], 1)

            def run(name, beside=None):
                p = by[name]
                per = OWN_WAITS.get(p.kind, 0) * SLOTS
                if beside is None:
                    rounds(dve, p, lambda r, looped: step(p, r, looped), own, per + (14 if p.mods is not None else 0))
                else:
                    for r in range(p.rounds):
                        step(p, r, False, beside)
                if p.norm:
                    add_squares(p, DT8 - 1)

            def norm(name, off, n, src, g, shift=None, hi=Hh, lo=Hl):
                if name == "mix1":
                    dve.wait_ge(scaled, 8 * scaled_no[name])
                if shift is not None:
                    scale = shift + 8
                    own.wait(stt(SM[:, GS:GS + 8], MOD[:, scale:scale + 8], 1.0, PV[:, g:g + 8], ALU.add, ALU.mult))
                if name in stat_no:
                    dve.wait_ge(rstd_ready, stat_no[name] + 1)
                for k in range(DT8):
                    w = PV[:, g + k:g + k + 1] if shift is None else SM[:, GS + k:GS + k + 1]
                    if name == "mix1":
                        dve.wait_ge(h_lo, 8 * split_no["kv"] + k + 1)
                    dst = X if name == "final" else S8
                    stt(dst[:, k, off:off + n], src[:, k, off:off + n], w, RSTD[:, 0:n], ALU.mult, ALU.mult)\
                        .then_inc(x_new if name == "final" else scaled, 1)
                    if shift is not None and k:
                        low_h(name, k - 1, off, n, shift, hi, lo)
                if shift is not None:
                    low_h(name, DT8 - 1, off, n, shift, hi, lo)

            def low_h(name, k, off, n, shift, hi, lo):
                dve.wait_ge(h_hi, 8 * split_no[name] + k + 1)
                stt(lo[:, k, off:off + n], S8[:, k, off:off + n], MOD[:, shift + k:shift + k + 1],
                    hi[:, k, off:off + n].bitcast(F32), ALU.add, ALU.subtract).then_inc(h_lo, 1)

            def taken(name):
                for s in range(SLOTS):
                    dve.wait_ge(bank_free[s], by[name].bank_end[s])

            def softplus(z, u, ln, w, d, tmp, dst, no):
                dve.wait_ge(sp_u, no)
                ts(w, u, 1.0, None, ALU.add).then_inc(sp_w, 1)
                dve.wait_ge(sp_w, no)
                own.wait(ts(d, w, -1.0, None, ALU.add))
                own.wait(ts(tmp, d, 1e-30, None, ALU.max))
                own.wait(dve.reciprocal(tmp, tmp))
                own.wait(tt(tmp, tmp, u, ALU.mult))
                dve.wait_ge(sp_ln, no)
                own.wait(tt(tmp, tmp, ln, ALU.mult))
                own.wait(stt(d, d, 0.0, u, ALU.is_equal, ALU.mult))
                own.wait(tt(tmp, tmp, d, ALU.add))
                own.wait(stt(dst, z, 0.0, tmp, ALU.max, ALU.add))

            def recurrence_beside(name):
                def decay(t):
                    m = M2[:, t, :] if t < 8 else CO[:, t - 8, 0:SEQ]
                    a2 = S8[:, t % 8, 0:SEQ]
                    dve.wait_ge(side["gate_a"], t + 1)
                    own.wait(tt(a2, LA[:, t, :], LA[:, t, :], ALU.mult))
                    stt(m, a2, 1.0, m, ALU.add, ALU.mult).then_inc(side["gate_m2"], 1)
                    if t:
                        scan(t - 1)

                run(name, beside=decay)
                scan(LT - 1)
                for t in range(LT + 1):
                    if t < LT:
                        dve.wait_ge(side["lru_gelu"], t + 1)
                        tt(XC[:, t, :], XC[:, t, :], YB[:, t, :], ALU.mult).then_inc(side["lru_y32"], 1)
                    if t:
                        low_y(t - 1)

            def scan(t):
                dve.wait_ge(side["gate_sqrt"], t + 1)
                m = M2[:, t, :] if t < 8 else CO[:, t - 8, 0:SEQ]
                own.wait(tt(XC[:, t, :], XC[:, t, :], m, ALU.mult))
                own.wait(dve.tensor_tensor_scan(XC[:, t, :], LA[:, t, :], XC[:, t, :], 0.0, ALU.mult, ALU.add))

            def low_y(t):
                dve.wait_ge(side["lru_hi"], t + 1)
                low(XCl[:, t, 0:SEQ], XC[:, t, :], XCh[:, t, 0:SEQ]).then_inc(side["lru_lo"], 1)

            def attention():
                dve.wait_ge(loaded["bias"], 16)

                def logits(h):
                    b = h % 2
                    dve.wait_ge(side["att_s"], h + 1)
                    if h >= 2:
                        dve.wait_ge(side["att_t"], h - 1)
                    stt(AL[:, b, 0:P], B[b][:, 0:P], P ** -0.5, BT[:, h, P:SEQ], ALU.mult, ALU.add)
                    own.wait(stt(AL[:, b, P:], B[b][:, P:384], P ** -0.5, BT[:, h, :], ALU.mult, ALU.add))
                    m = SM[:, AMX + 2 * b:AMX + 2 * b + 2]
                    dve.tensor_reduce(m[:, 0:1], AL[:, b, 0:P], AX.X, ALU.max)
                    own.wait(dve.tensor_reduce(m[:, 1:2], AL[:, b, P:], AX.X, ALU.max))
                    ts(m, m, -1.0, None, ALU.mult).then_inc(side["att_max"], 1)

                def probs(h):
                    b = h % 2
                    dve.wait_ge(side["att_exp"], h + 1)
                    sm = SM[:, ASM + 2 * b:ASM + 2 * b + 2]
                    own.wait(dve.reciprocal(sm, sm))
                    ts(AL[:, b, 0:P], AL[:, b, 0:P], sm[:, 0:1], None, ALU.mult)
                    ts(AL[:, b, P:], AL[:, b, P:], sm[:, 1:2], None, ALU.mult).then_inc(side["att_p"], 1)

                def head(i):
                    if i < 8:
                        logits(i)
                    if 1 <= i <= 8:
                        probs(i - 1)
                    if i >= 3:
                        h = i - 3
                        dve.wait_ge(side["side_hi"], h + 1)
                        low(Yl[:, h, META:], B[3][:, 0:SEQ], Yh[:, h, META:]).then_inc(side["side_lo"], 1)

                run("q", beside=lambda c: head(c - 1) if c else None)
                for i in range(7, 11):
                    head(i)

            def step_sizes(l):
                softplus(SD[:, 0, :], SD[:, 1, :], SD[:, 2, :], SD[:, 3, :], SD[:, 4, :], SD[:, 5, :], SD[:, 6, :], 2 + l)
                own.wait(ts(SD[:, 5, :], SD[:, 6, :], SM[0:16, EA + l:EA + l + 1], -1.0, ALU.mult, ALU.mult))
                dve.tensor_tensor_scan(ACS[:, :], ONES[0:16, 0:1].to_broadcast([16, TOK]), SD[:, 5, :], 0.0,
                                       ALU.mult, ALU.add).then_inc(side["dt_acs"], 1)

            def state_space(l):
                def take_steps():
                    dve.wait_ge(side["dt_turned"], l + 1)
                    dve.tensor_copy(SM[:, DTT:DTT + 32], B[0][:, 0:32])
                    dve.tensor_copy(SM[0:16, DTT + 32:DTT + 48], B[0][0:16, 32:48])
                    ts(SM[:, NAT:NAT + 32], B[0][:, 48:80], -1.0, None, ALU.mult)
                    ts(SM[0:16, NAT + 32:NAT + 48], B[0][0:16, 80:96], -1.0, None, ALU.mult).then_inc(side["dt_cols"], 1)
                    dve.wait_ge(side["dt_cols"], l + 1)

                def scale_x(m):
                    n, half = m // 2, m % 2
                    w = KEYS[n][1]
                    dve.wait_ge(side["x_turned"], 6 * l + m + 1)
                    step_size = SM[0:w, DTT + 16 * n + 8 * half:DTT + 16 * n + 8 * half + 8]
                    tt(XT[0:w, n, 512 * half:512 * half + 512].rearrange("p (h d) -> p h d", d=64),
                       B[1 + m % 3][0:w, :].rearrange("p (h d) -> p h d", d=64),
                       step_size.unsqueeze(2).to_broadcast([w, 8, 64]), ALU.mult).then_inc(side["x_scaled"], 1)
                def mask_scores(g):
                    dve.wait_ge(side["cb_done"], 4 * l + g + 1)
                    tt(CB[:, g, :], B[g][:, 0:PACK], incl, ALU.mult).then_inc(side["cb_masked"], 1)

                def front(i):
                    if i == 0:
                        take_steps()
                    elif i < 4:
                        scale_x(2 * i - 2)
                        scale_x(2 * i - 1)
                    elif i == 4:
                        for g in range(4):
                            mask_scores(g)
                        dve.wait_ge(side["cb_masked"], 4 * l + 4)

                def take(j):
                    dve.wait_ge(side["head_y"], 16 * l + 2 * j + 2)
                    c = PCOL["ssd_d"] + 8 * l + j
                    stt(S8[:, j, :], XS[:, j, :], PV[:, c:c + 1], B[2 + j % 2][:, 0:TOK], ALU.mult, ALU.add)\
                        .then_inc(side["y_taken"], 1)

                def log_decay(h):
                    b, n16 = h % 2, 16 * l + h
                    dve.wait_ge(side["acs_rows"], n16 + 1)
                    if h >= 2:
                        dve.wait_ge(side["decay_mix"], n16 - 1)
                    for n, (c, q0, w) in enumerate(SEG):
                        k, c0 = KEYS[n][1], NAT + 16 * n + h
                        ins = ts(SE[0:k, b, c:c + w], B[b][0:k, q0:q0 + w], SM[0:k, c0:c0 + 1], 0.0, ALU.add, ALU.min)
                    ins.then_inc(side["decay_log"], 1)

                def mix(h):
                    b, n16 = h % 2, 16 * l + h
                    dve.wait_ge(side["decay_exp"], n16 + 1)
                    if h >= 2:
                        dve.wait_ge(side["head_y"], n16 - 1)
                    tt(SX[:, b, 0:416], SE[:, b, 0:416], CB[:, h // 4, 0:416], ALU.mult)
                    tt(SX[0:16, b, 416:], SE[0:16, b, 416:], CB[0:16, h // 4, 416:], ALU.mult).then_inc(side["decay_mix"], 1)

                def head(i):
                    if i < 16:
                        log_decay(i)
                    if i:
                        mix(i - 1)
                    if i >= 4 and i % 2 == 0:
                        take((i - 4) // 2)

                run(f"s_z{l}", beside=lambda c: front(c - 4) if c >= 4 else None)
                run(f"r_q{l}", beside=lambda c: head(c - 1) if c else front(4))
                run(f"r_k{l}", beside=lambda c: head(7 + c))
                head(15)
                head(16)
                take(7)
                taken(f"s_z{l}")
                dve.wait_ge(side["y_taken"], 8 * l + 8)
                for g in range(4):
                    y = S8[:, 2 * g:2 * g + 2, :]
                    own.wait(tt(y, y, Z[:, 2 * g:2 * g + 2, :], ALU.mult))
                    tt(YQ["ssd"][:, 2 * g:2 * g + 2, :], y, y, ALU.mult).then_inc(side["y_sq"], 1)
                for g in range(4):
                    dve.wait_ge(side["y_rstd"], 8 * l + g + 1)
                    for t in (2 * g, 2 * g + 1):
                        c = PCOL["ssd_norm"] + 8 * l + t
                        stt(S8[:, t, :], S8[:, t, :], PV[:, c:c + 1], YR["ssd"][:, g, :], ALU.mult, ALU.mult)\
                            .then_inc(side["y32"], 1)
                        if t:
                            low_side(8 + 24 * l, t - 1)
                low_side(8 + 24 * l, 7)

            def low_side(before, t):
                dve.wait_ge(side["side_hi"], before + t + 1)
                low(Yl[:, t, :], S8[:, t, :], Yh[:, t, :]).then_inc(side["side_lo"], 1)

            def retention(l):
                for h in range(4):
                    dve.wait_ge(side["ret_s"], 4 * l + h + 1)
                    if h >= 2:
                        dve.wait_ge(side["ret_y"], 8 * l + 2 * (h - 1))
                    c = CCOL["decay"] + h * PACK
                    tt(RP[:, h % 2, :], B[h % 2][:, 0:PACK], CS[:, c:c + PACK], ALU.mult).then_inc(side["ret_p"], 1)
                for h in range(4):
                    dve.wait_ge(side["ret_mean"], 4 * l + h + 1)
                    for t in (2 * h, 2 * h + 1):
                        ins = stt(S8[:, t, :], B[h][:, 0:TOK], -1.0 / 256, S8[:, t, :], ALU.mult, ALU.add)
                    own.wait(ins)
                    y = S8[:, 2 * h:2 * h + 2, :]
                    tt(YQ["ret"][:, 2 * h:2 * h + 2, :], y, y, ALU.mult).then_inc(side["y_sq"], 1)
                taken(f"r_g{l}")
                dve.wait_ge(side["y_sq"], 8 * l + 8)
                own.wait(tt(S8[:, :, :], S8[:, :, :], RG[:, :, :], ALU.mult))
                for h in range(4):
                    dve.wait_ge(side["y_rstd"], 8 * l + 4 + h + 1)
                    for t in (2 * h, 2 * h + 1):
                        tt(S8[:, t, :], S8[:, t, :], YR["ret"][:, h, :], ALU.mult).then_inc(side["y32"], 1)
                        if t:
                            low_side(16 + 24 * l, t - 1)
                low_side(16 + 24 * l, 7)

            def stick_breaking(l):
                def head(i):
                    n8 = 8 * l + i
                    if i < 8:
                        b = i % 2
                        dve.wait_ge(side["sb_soft"], n8 + 1)
                        if i >= 2:
                            dve.wait_ge(side["sb_r"], n8 - 1)
                        own.wait(stt(SS[:, b, :], ZS[:, b, :], 0.0, SA[:, b, :], ALU.max, ALU.add))
                        tt(SS[:, b, :], SS[:, b, :], strict, ALU.mult).then_inc(side["sb_sp"], 1)
                    if 1 <= i <= 8:
                        b = (i - 1) % 2
                        dve.wait_ge(side["sb_r"], n8)
                        if i >= 3:
                            dve.wait_ge(side["sb_o"], n8 - 2)
                        own.wait(tt(SW[:, b, :], ZS[:, b, :], B[2][:, 0:PACK], ALU.subtract))
                        ts(SW[:, b, :], SW[:, b, :], 0.0, None, ALU.min).then_inc(side["sb_logw"], 1)
                        dve.wait_ge(side["sb_we"], n8)
                        tt(SW[:, b, :], SW[:, b, :], strict, ALU.mult).then_inc(side["sb_w"], 1)
                    if i >= 2:
                        h = i - 2
                        dve.wait_ge(side["side_hi"], 24 + 24 * l + h + 1)
                        low(Yl[:, h, :], B[3][:, 0:TOK], Yh[:, h, :]).then_inc(side["side_lo"], 1)

                run(f"b_kq{l}", beside=lambda c: head(c // 2 - 1) if c >= 2 and c % 2 == 0 else None)
                for i in range(7, 10):
                    head(i)

            dve.memset(ONES[:, :], 1.0)
            dve.memset(CI[:, :, 0:3], 0.0)
            dve.memset(SM[:, EPSC:EPSC + 1], EPS).then_inc(sig["copied"], 2)
            dve.wait_ge(sig["copied"], 2)
            dve.memset(SM[:, EPSC + 1:EPSC + 2], 1e-37).then_inc(const_ready, 1)
            dve.wait_ge(loaded["params"], 16)
            c = PCOL["lru_lambda"]
            ts(SM[:, SPT:SPT + LT], PV[:, c:c + LT], -1.0, None, ALU.mult).then_inc(const_ready, 1)
            dve.wait_ge(silu_c, 1)
            dve.wait_ge(loaded["mod_b"], 16)
            for m in range(FIRST // 2 + 1):
                if 2 * m < FIRST:
                    if m:
                        dve.wait_ge(mod_sum, 2 * m)
                    mod_units(m, (0, 1) if m % 2 == 0 else (0,))
                if m:
                    mod_take(m - 1, 0)
                    mod_take(m - 1, 1)
            for s in (0, 2):
                dve.wait_ge(hi_ready[s], 1)
                low_w(s, DT8)
            dve.wait_ge(mod_taken, FIRST)
            norm("mix0", META, SEQ, X, PCOL["norm_mix"], 0)
            sp = SM[:, SPW + 30:SPW + 40]
            softplus(SM[:, SPT:SPT + LT], SM[:, SPW:SPW + 10], SM[:, SPW + 20:SPW + 30], SM[:, SPW + 10:SPW + 20],
                     sp, SM[:, DTT:DTT + LT], SM[:, DTT + 16:DTT + 16 + LT], 1)
            ts(SM[:, SPL:SPL + LT], SM[:, DTT + 16:DTT + 16 + LT], -8.0, None, ALU.mult)
            own.wait(ts(SM[:, SPT:SPT + LT], SM[:, DTT + 16:DTT + 16 + LT], 8.0, None, ALU.mult))
            dve.wait_ge(side["bias_sum"], 1)
            own.wait(dve.tensor_copy(BR[:, :], B[1][0:8, 0:BIASW]))
            dve.memset(BR[:, SEQ:], -1e30).then_inc(side["bias_row"], 1)
            run("lru_x")
            run("lru_gates")
            recurrence_beside("lru_y")
            run("lru_out")
            norm("ffn0", META, SEQ, X, PCOL["norm_ffn"], 24)
            run("ffn_up0")
            run("ffn_down0")
            norm("kv", META, SEQ, X, PCOL["kv_norm"], 48, Yh, Yl)
            norm("mix1", META, SEQ, X, PCOL["norm_mix"] + 8, 64)
            run("kv_k")
            run("kv_v")
            attention()
            run("attn_out")
            norm("ffn1", META, SEQ, X, PCOL["norm_ffn"] + 8, 88)
            run("ffn_up1")
            run("ffn_down1")
            dve.wait_ge(loaded["meta"], 16)
            dve.wait_ge(loaded["heads"], 16)
            norm("final", META, SEQ, X, PCOL["final_norm"])
            for l in range(2):
                off, n = (META, SEQ) if l else (0, TOK)
                norm(f"pre{l}", 0, TOK, X, PCOL["norm_mix_pre"] + 8 * l)
                dve.memset(U[:, :, 0:2], 0.0)
                dve.memset(RK[:, 8 * TOK:], 0.0)
                run(f"a_cx{l}")
                for s in range(SLOTS):
                    dve.wait_ge(bank_free[s], by[f"a_cx{l}"].bank_end[s])
                run(f"a_b{l}")
                run(f"up_a{l}")
                run(f"dt{l}")
                run(f"s_x{l}")
                run(f"s_bc{l}")
                step_sizes(l)
                state_space(l)
                run(f"up_b{l}")
                run(f"r_v{l}")
                run(f"r_g{l}")
                retention(l)
                run(f"up_c{l}")
                dve.memset(BK[:, :].rearrange("p (a n) -> p a n", a=8)[:, :, TOK:], 0.0)
                run(f"b_v{l}")
                stick_breaking(l)
                run(f"up_d{l}")
                run(f"mix_out{l}")
                norm(f"post{l}", off, n, M, PCOL["norm_mix_post"] + 8 * l)
                norm(f"fpre{l}", off, n, X, PCOL["norm_ffn_pre"] + 8 * l)
                run(f"ffn_up{2 + l}")
                run(f"ffn_down{2 + l}")
                norm(f"fpost{l}", off, n, M, PCOL["norm_ffn_post"] + 8 * l)


def chunks(w, kb=8):
    k, m = w.shape
    w = w.reshape(k // (kb * P), kb, P, m // P, P)
    return w.transpose(3, 0, 2, 1, 4).reshape(-1, P, kb * P)


def pairs(u, v):
    return np.stack([u, v], axis=1).reshape(-1, *u.shape[1:])


def constants():
    cs = np.zeros((P, CCOLS), np.float32)
    cs[:, CCOL["ident"]:CCOL["ident"] + P] = np.eye(P)
    cs[:, CCOL["suffix"]:CCOL["suffix"] + P] = np.tril(np.ones((P, P)))
    gamma = np.log(1.0 - 2.0 ** (-5.0 - np.arange(4, dtype=np.float64)))
    for (c, q0, w), (k0, kn) in zip(SEG, KEYS):
        key, query = k0 + np.arange(kn)[:, None], q0 + np.arange(w)[None, :]
        cs[:kn, CCOL["incl"] + c:CCOL["incl"] + c + w] = key <= query
        cs[:kn, CCOL["strict"] + c:CCOL["strict"] + c + w] = key < query
        for h in range(4):
            at = CCOL["decay"] + h * PACK + c
            cs[:kn, at:at + w] = np.where(key <= query, np.exp(gamma[h] * np.maximum(query - key, 0)), 0) / 16
    pos = np.arange(P - META, P + SEQ).astype(np.float32)
    inv = np.float32(10000.0) ** (-np.arange(P, dtype=np.float32) / np.float32(P))
    ang = (pos[None, :] * inv[:, None]).astype(np.float32)
    cs[:, CCOL["cos"]:CCOL["cos"] + TOK] = np.cos(ang)
    cs[:, CCOL["sin"]:CCOL["sin"] + TOK] = np.sin(ang)
    dist = SEQ - 1 - np.arange(BIASW)
    d = np.maximum(dist, 1).astype(np.float32)
    large = 16 + (np.log(d / np.float32(16)) / np.float32(np.log(128 / 16)) * np.float32(16)).astype(np.int32)
    bucket = np.where(dist < 16, dist, np.minimum(large, 31))
    onehot = (np.arange(32)[:, None] == bucket[None, :]) & (dist >= 0)[None, :]
    return cs, onehot.astype(np.float32)


def columns(v):
    return v.reshape(-1, P).T


def layout(i):
    f = {n: np.asarray(v) for n, v in i.items()}
    a = {}
    a["x"] = f["x"][0].reshape(SEQ, DT8, P).transpose(2, 1, 0)
    a["meta"] = f["meta_2"].reshape(META, DT8, P).transpose(2, 1, 0)
    a["consts"], a["onehot"] = constants()
    a["rel_bias"] = f["rel_bias"].T
    a["heads"] = np.stack([f["ssd_dt_bias_2"][0], f["ssd_a_log_2"][0], f["ssd_dt_bias_2"][1], f["ssd_a_log_2"][1]], axis=1)
    mod = np.concatenate([f["mod_w"][0], f["kv_mod_w"], f["mod_w"][1]], axis=1)
    a["mod_w"] = mod.reshape(8, P, MOD_UNITS, MU).transpose(2, 1, 0, 3)
    a["mod_b"] = columns(np.concatenate([f["mod_b"][0], f["kv_mod_b"], f["mod_b"][1]]))
    src = {"c": f["c"],
           "ssd_d": np.repeat(f["ssd_d_2"], 64, axis=1), "lru_conv_w": f["lru_conv_w"][0], "lru_conv_b": f["lru_conv_b"],
           "lru_b_gates": f["lru_b_gates"][0], "lru_lambda": f["lru_lambda"]}
    cols = []
    for name, w in PARAMS:
        v = src[name] if name in src else f[name] if name in f else f[name + "_2"]
        v = columns(v)
        assert v.shape == (P, w), (name, v.shape)
        cols.append(v)
    a["params"] = np.concatenate(cols, axis=1)
    w = chunks(f["lru_w_in"][0])
    a["lru_y"], a["lru_x"] = w[:LT], w[LT:]
    g = f["lru_w_gates"][0].reshape(5, 2, P, 2, 2, P)
    a["lru_gates"] = g.transpose(0, 4, 2, 3, 1, 5).reshape(LT, P, 4 * P)
    a["lru_out"] = chunks(f["lru_w_out"][0], 10)
    kv = chunks(f["w_kv"])
    a["kv_k"], a["kv_v"] = kv[:4], kv[4:]
    a["q"], a["attn_out"] = chunks(f["attn_w_q"][0]), chunks(f["attn_w_o"][0])
    for l in range(2):
        a[f"ffn_up{l}"] = pairs(chunks(f["ffn_w_gate"][l]), chunks(f["ffn_w_up"][l]))
        a[f"ffn_down{l}"] = chunks(f["ffn_w_down"][l], 11)
    for l in range(2):
        w, at = f["w_in_2"][l], [0]

        def take(n):
            at[0] += n
            return w[:, at[0] - n:at[0]]

        b, c, x, z, xs, bc, dt = (take(n) for n in (D, D, D, D, D, D, 16))
        rq, rk, rv, rg, bq, bk, bv, gates = (take(n) for n in (D,) * 7 + (4 * D,))
        a[f"a_cx{l}"], a[f"a_b{l}"] = pairs(chunks(c), chunks(x)), chunks(b)
        a[f"dt{l}"] = chunks(np.concatenate([dt, np.zeros((D, P - 16), dt.dtype)], axis=1))
        for n, v in (("s_x", xs), ("s_bc", bc), ("s_z", z), ("r_v", rv), ("r_q", rq), ("r_k", rk), ("r_g", rg),
                     ("b_v", bv)):
            a[n + str(l)] = chunks(v)
        a[f"b_kq{l}"] = pairs(chunks(bk), chunks(bq))
        for j, n in enumerate("abcd"):
            a[f"up_{n}{l}"] = pairs(chunks(gates[:, j * D:(j + 1) * D]), chunks(f["w_branch_2"][l, j]))
        a[f"mix_out{l}"] = chunks(f["w_out_2"][l])
        up = f["w_ffn_in_2"][l]
        a[f"ffn_up{2 + l}"] = pairs(chunks(up[:, :FF]), chunks(up[:, FF:]))
        a[f"ffn_down{2 + l}"] = chunks(f["w_ffn_out_2"][l], 11)
    return {n: np.ascontiguousarray(v) for n, v in a.items()}


def kernel(**inputs):
    import concourse.bacc as bacc
    from concourse.bass_utils import run_bass_kernel_spmd

    nc = bacc.Bacc("TRN2", target_bir_lowering=False, num_devices=1)
    arrays, aps = {}, {}
    for name, v in layout(inputs).items():
        arrays["in_" + name] = v
        aps[name] = nc.dram_tensor("in_" + name, v.shape, mybir.dt.from_np(v.dtype), kind="ExternalInput").ap()
    out = nc.dram_tensor("out", (P, DT8, SEQ), F32, kind="ExternalOutput").ap()
    two_layer_pair(nc, aps, out)
    r = run_bass_kernel_spmd(nc, [arrays], core_ids=[0])
    return r.results[0]["out"].transpose(2, 1, 0).reshape(1, SEQ, D)
```
